# Optimizing a Trainium2 kernel written in Bass

```python
import math
import jax, jax.numpy as jnp
from jax import lax
import numpy as np

D_MODEL = 1024
BATCH = 1
SEQ = 256
DEPTH = 2

CHUNK = 64
Q_BLOCK = 128
N_MIXERS = 3
N_HEADS = 16
HEAD_DIM = D_MODEL // N_HEADS
INNER = N_HEADS * HEAD_DIM
IDX_HEADS = 8
IDX_DIM = 64
TOPK_MAX = 256
DIFF_HEADS = N_HEADS // 2
DIFF_DIM = HEAD_DIM
ROPE_THETA = 10000.0
LN_EPS = 1e-5
RMS_EPS = 1e-5
ALPHA = (2.0 * DEPTH) ** 0.25
BETA = (8.0 * DEPTH) ** -0.25
A_IN = 4 * INNER + IDX_HEADS * IDX_DIM + IDX_HEADS + IDX_DIM
B_IN = 4 * INNER
C_IN = 4 * INNER


def _n_layers_of(m):
    return len(range(m, DEPTH, N_MIXERS))

def rope_tables(seq, dim):
    inv = 1.0 / (ROPE_THETA ** (jnp.arange(0, dim, 2, dtype=jnp.float32) / dim))
    ang = jnp.arange(seq, dtype=jnp.float32)[:, None] * inv[None, :]
    return jnp.cos(ang), jnp.sin(ang)

def apply_rope(t, cos, sin):
    c = cos[None, :, None, :].astype(t.dtype)
    s = sin[None, :, None, :].astype(t.dtype)
    t1, t2 = jnp.split(t, 2, axis=-1)
    return jnp.concatenate([t1 * c - t2 * s, t2 * c + t1 * s], axis=-1)

def to_blocks(a):
    b, s = a.shape[0], a.shape[1]
    return jnp.moveaxis(a.reshape(b, s // Q_BLOCK, Q_BLOCK, *a.shape[2:]), 1, 0)

def from_blocks(o):
    o = jnp.moveaxis(o, 0, 1)
    return o.reshape(o.shape[0], o.shape[1] * o.shape[2], *o.shape[3:])

def layer_norm(x, g, b):
    xf = x.astype(jnp.float32)
    mu = jnp.mean(xf, axis=-1, keepdims=True)
    var = jnp.mean(jnp.square(xf - mu), axis=-1, keepdims=True)
    return ((xf - mu) * lax.rsqrt(var + LN_EPS) * g + b).astype(x.dtype)

def rms_norm(x, g):
    xf = x.astype(jnp.float32)
    return (xf * lax.rsqrt(jnp.mean(xf * xf, axis=-1, keepdims=True) + RMS_EPS) * g).astype(x.dtype)

def dsa_mixer(x, w_in, w_out, cos, sin):
    b, s, _ = x.shape
    k_top = min(TOPK_MAX, s // 4)
    cuts = [INNER, 2 * INNER, 3 * INNER, 4 * INNER,
            4 * INNER + IDX_HEADS * IDX_DIM, 4 * INNER + IDX_HEADS * IDX_DIM + IDX_HEADS]
    q, k, v, g, qi, wi, ki = jnp.split(x @ w_in, cuts, axis=-1)
    q = apply_rope(q.reshape(b, s, N_HEADS, HEAD_DIM), cos, sin)
    k = apply_rope(k.reshape(b, s, N_HEADS, HEAD_DIM), cos, sin)
    v = v.reshape(b, s, N_HEADS, HEAD_DIM)
    qi = apply_rope(qi.reshape(b, s, IDX_HEADS, IDX_DIM), cos, sin)
    ki = apply_rope(ki[:, :, None, :], cos, sin)[:, :, 0, :]
    wi = wi.astype(jnp.float32) * IDX_HEADS ** -0.5
    pos = jnp.arange(s)
    key_chunk = pos // CHUNK

    def block(args):
        qb, qib, wib, pb = args
        q_chunk = pb // CHUNK
        rel = jax.nn.relu(jnp.einsum('bqhd,bsd->bqhs', qib, ki).astype(jnp.float32) * IDX_DIM ** -0.5)
        score = jnp.einsum('bqhs,bqh->bqs', rel, wib)
        adm = key_chunk[None, :] <= q_chunk[:, None]
        score = jnp.where(adm[None], score, -jnp.inf)
        _, idx = lax.top_k(score, k_top)
        ks = jax.vmap(lambda kk, ii: kk[ii])(k, idx)
        vs = jax.vmap(lambda vv, ii: vv[ii])(v, idx)
        logits = jnp.einsum('bqhd,bqkhd->bhqk', qb, ks).astype(jnp.float32) * HEAD_DIM ** -0.5
        sel_ok = (idx // CHUNK) <= q_chunk[None, :, None]
        logits = jnp.where(sel_ok[:, None], logits, -jnp.inf)
        p = jax.nn.softmax(logits, axis=-1).astype(vs.dtype)
        return jnp.einsum('bhqk,bqkhd->bqhd', p, vs)

    o = lax.map(block, (to_blocks(q), to_blocks(qi), to_blocks(wi), pos.reshape(-1, Q_BLOCK)))
    o = from_blocks(o).reshape(b, s, INNER)
    return (o * jax.nn.silu(g)) @ w_out

def stick_breaking_mixer(x, w_in, w_out):
    b, s, _ = x.shape
    q, k, v, g = jnp.split(x @ w_in, 4, axis=-1)
    q = q.reshape(b, s, N_HEADS, HEAD_DIM)
    k = k.reshape(b, s, N_HEADS, HEAD_DIM)
    v = v.reshape(b, s, N_HEADS, HEAD_DIM)
    pos = jnp.arange(s)

    def block(args):
        qb, pb = args
        z = jnp.einsum('bqhd,bshd->bhqs', qb, k).astype(jnp.float32) * HEAD_DIM ** -0.5
        before = pos[None, :] < pb[:, None]
        log_one_minus = jnp.where(before, jax.nn.log_sigmoid(-z), 0.0)
        log_stick = lax.cumsum(log_one_minus, axis=3, reverse=True) - log_one_minus
        a = jnp.where(before, jnp.exp(jax.nn.log_sigmoid(z) + log_stick), 0.0).astype(v.dtype)
        return jnp.einsum('bhqs,bshd->bqhd', a, v)

    o = lax.map(block, (to_blocks(q), pos.reshape(-1, Q_BLOCK)))
    o = from_blocks(o).reshape(b, s, INNER)
    return (o * jax.nn.silu(g)) @ w_out

def diff_mixer(x, w_in, w_out, lq1, lk1, lq2, lk2, sub_g, lambda_init, cos, sin):
    b, s, _ = x.shape
    q, k, v, g = jnp.split(x @ w_in, 4, axis=-1)
    q = apply_rope(q.reshape(b, s, 2 * DIFF_HEADS, DIFF_DIM), cos, sin).reshape(b, s, DIFF_HEADS, 2, DIFF_DIM)
    k = apply_rope(k.reshape(b, s, 2 * DIFF_HEADS, DIFF_DIM), cos, sin).reshape(b, s, DIFF_HEADS, 2, DIFF_DIM)
    v = v.reshape(b, s, DIFF_HEADS, 2 * DIFF_DIM)
    lam = (jnp.exp(jnp.sum(lq1.astype(jnp.float32) * lk1.astype(jnp.float32)))
           - jnp.exp(jnp.sum(lq2.astype(jnp.float32) * lk2.astype(jnp.float32))) + lambda_init)
    pos = jnp.arange(s)
    key_chunk = pos // CHUNK

    def block(args):
        qb, pb = args
        logits = jnp.einsum('bqhmd,bshmd->bhmqs', qb, k).astype(jnp.float32) * DIFF_DIM ** -0.5
        adm = key_chunk[None, :] <= (pb // CHUNK)[:, None]
        p = jax.nn.softmax(jnp.where(adm, logits, -jnp.inf), axis=-1)
        wdiff = (p[:, :, 0] - lam * p[:, :, 1]).astype(v.dtype)
        return jnp.einsum('bhqs,bshe->bqhe', wdiff, v)

    o = from_blocks(lax.map(block, (to_blocks(q), pos.reshape(-1, Q_BLOCK))))
    o = rms_norm(o, sub_g) * (1.0 - lambda_init)
    o = o.reshape(b, s, INNER)
    return (o * jax.nn.silu(g)) @ w_out

def first_inputs(seed: int = 0) -> dict:
    key = jax.random.key(seed)
    ks = jax.random.split(key, 14)
    na, nb_, nc = _n_layers_of(0), _n_layers_of(1), _n_layers_of(2)

    def in_proj(k, n, width):
        col = jnp.ones((width,), jnp.float32).at[2 * INNER:3 * INNER].set(BETA)
        return jax.random.normal(k, (n, D_MODEL, width), jnp.float32) * D_MODEL ** -0.5 * col

    def out_proj(k, n):
        return jax.random.normal(k, (n, INNER, D_MODEL), jnp.float32) * INNER ** -0.5 * BETA

    return {
        "x": jax.random.normal(ks[0], (BATCH, SEQ, D_MODEL), jnp.float32),
        "w_in_a": in_proj(ks[1], na, A_IN),
        "w_out_a": out_proj(ks[2], na),
        "w_in_b": in_proj(ks[3], nb_, B_IN),
        "w_out_b": out_proj(ks[4], nb_),
        "w_in_c": in_proj(ks[5], nc, C_IN),
        "w_out_c": out_proj(ks[6], nc),
        "lambda_q1": 0.1 * jax.random.normal(ks[7], (nc, DIFF_DIM), jnp.float32),
        "lambda_k1": 0.1 * jax.random.normal(ks[8], (nc, DIFF_DIM), jnp.float32),
        "lambda_q2": 0.1 * jax.random.normal(ks[9], (nc, DIFF_DIM), jnp.float32),
        "lambda_k2": 0.1 * jax.random.normal(ks[10], (nc, DIFF_DIM), jnp.float32),
        "subln_g": 1.0 + 0.02 * jax.random.normal(ks[11], (nc, 2 * DIFF_DIM), jnp.float32),
        "ln_g": 1.0 + 0.02 * jax.random.normal(ks[12], (DEPTH, D_MODEL), jnp.float32),
        "ln_b": 0.02 * jax.random.normal(ks[13], (DEPTH, D_MODEL), jnp.float32),
    }

def first_block(x, w_in_a, w_out_a, w_in_b, w_out_b, w_in_c, w_out_c,
              lambda_q1, lambda_k1, lambda_q2, lambda_k2, subln_g, ln_g, ln_b):
    s = x.shape[1]
    cos_a, sin_a = rope_tables(s, HEAD_DIM)
    cos_i, sin_i = rope_tables(s, IDX_DIM)
    cos_c, sin_c = rope_tables(s, DIFF_DIM)
    for i in range(DEPTH):
        m, j = i % N_MIXERS, i // N_MIXERS
        if m == 0:
            y = dsa_mixer(x, w_in_a[j], w_out_a[j], cos_a, sin_a) if HEAD_DIM == IDX_DIM else None
        elif m == 1:
            y = stick_breaking_mixer(x, w_in_b[j], w_out_b[j])
        else:
            lambda_init = 0.8 - 0.6 * math.exp(-0.3 * i)
            y = diff_mixer(x, w_in_c[j], w_out_c[j], lambda_q1[j], lambda_k1[j],
                           lambda_q2[j], lambda_k2[j], subln_g[j], lambda_init, cos_c, sin_c)
        x = layer_norm(ALPHA * x + y, ln_g[i], ln_b[i])
    return x


N_MEM = 256
GRID_W = 64
EPS = 1e-6
FOURIER_GROUPS = 4
FOURIER_GROUP_DIM = D_MODEL // 8
FOURIER_WIDTH = FOURIER_GROUPS * FOURIER_GROUP_DIM
NA_HEADS = 4
NA_HEAD_DIM = D_MODEL // 8
NA_WIDTH = NA_HEADS * NA_HEAD_DIM
NA_KH = 8
NA_KW = 16
AB_IN_WIDTH = FOURIER_WIDTH + 3 * NA_WIDTH
AB_OUT_WIDTH = FOURIER_WIDTH + NA_WIDTH
CONV_WIDTH = 3
XA_HEADS = 4
XA_HEAD_DIM = D_MODEL // XA_HEADS
D_FF = 2 * D_MODEL
N_EVEN = (DEPTH + 1) // 2
N_ODD = DEPTH // 2


def rms_norm_2(x, g):
    xf = x.astype(jnp.float32)
    y = xf * lax.rsqrt(jnp.mean(xf * xf, axis=-1, keepdims=True) + EPS)
    return (y * g.astype(jnp.float32)).astype(x.dtype)

def dwconv3_centred(x, w):
    xp = jnp.pad(x, ((0, 0), (1, 1), (0, 0)))
    return xp[:, :-2] * w[0] + xp[:, 1:-1] * w[1] + xp[:, 2:] * w[2]

def fourier_mix(u):
    f = jnp.fft.fft2(u.astype(jnp.float32), axes=(1, 3), norm="ortho")
    return jnp.real(f).astype(u.dtype)

def neighborhood_attention(q, k, v, rpb):
    B, S, H, dh = q.shape
    rows = S // GRID_W
    kh = min(NA_KH, rows)
    kw = NA_KW
    qg = q.reshape(B, rows, GRID_W, H, dh)
    kg = k.reshape(B, rows, GRID_W, H, dh)
    vg = v.reshape(B, rows, GRID_W, H, dh)
    cols = jnp.arange(GRID_W)
    col_start = jnp.clip(cols - kw // 2, 0, GRID_W - kw)
    col_idx = col_start[:, None] + jnp.arange(kw)[None, :]
    col_off = col_idx - cols[:, None] + (NA_KW - 1)
    scale = dh ** -0.5

    def one_row(i):
        rs = jnp.clip(i - kh // 2, 0, rows - kh)
        q_i = lax.dynamic_index_in_dim(qg, i, axis=1, keepdims=False)
        k_blk = lax.dynamic_slice_in_dim(kg, rs, kh, axis=1)
        v_blk = lax.dynamic_slice_in_dim(vg, rs, kh, axis=1)
        k_win = k_blk[:, :, col_idx]
        v_win = v_blk[:, :, col_idx]
        s = jnp.einsum('bjhd,brjchd->bhjrc', q_i, k_win).astype(jnp.float32) * scale
        row_off = rs + jnp.arange(kh) - i + (NA_KH - 1)
        bias = rpb[:, row_off][:, :, col_off]
        s = s + jnp.transpose(bias, (0, 2, 1, 3)).astype(jnp.float32)[None]
        p = jax.nn.softmax(s.reshape(B, H, GRID_W, kh * kw), axis=-1)
        p = p.reshape(B, H, GRID_W, kh, kw).astype(v.dtype)
        return jnp.einsum('bhjrc,brjchd->bjhd', p, v_win)

    out = lax.map(one_row, jnp.arange(rows))
    return jnp.moveaxis(out, 0, 1).reshape(B, S, H, dh)

def fourier_na_mixer(h, w_in, rpb, w_out):
    B, S, _ = h.shape
    z = h @ w_in
    zf = z[..., :FOURIER_WIDTH]
    q = z[..., FOURIER_WIDTH:FOURIER_WIDTH + NA_WIDTH].reshape(B, S, NA_HEADS, NA_HEAD_DIM)
    k = z[..., FOURIER_WIDTH + NA_WIDTH:FOURIER_WIDTH + 2 * NA_WIDTH].reshape(B, S, NA_HEADS, NA_HEAD_DIM)
    v = z[..., FOURIER_WIDTH + 2 * NA_WIDTH:].reshape(B, S, NA_HEADS, NA_HEAD_DIM)
    yf = fourier_mix(zf.reshape(B, S, FOURIER_GROUPS, FOURIER_GROUP_DIM)).reshape(B, S, FOURIER_WIDTH)
    ya = neighborhood_attention(q, k, v, rpb).reshape(B, S, NA_WIDTH)
    return jnp.concatenate([yf, ya], axis=-1) @ w_out

def short_gated_conv_mixer(h, w_in, conv_w, w_out):
    z = h @ w_in
    gate_b = z[..., :D_MODEL]
    gate_c = z[..., D_MODEL:2 * D_MODEL]
    u = z[..., 2 * D_MODEL:]
    return (gate_b * dwconv3_centred(gate_c * u, conv_w)) @ w_out

def memory_cross_attention(h, m, wq, wkv, wo):
    B, S, D = h.shape
    q = (h @ wq).reshape(B, S, XA_HEADS, XA_HEAD_DIM)
    kv = m @ wkv
    k = kv[..., :D].reshape(B, -1, XA_HEADS, XA_HEAD_DIM)
    v = kv[..., D:].reshape(B, -1, XA_HEADS, XA_HEAD_DIM)
    s = jnp.einsum('bshd,bmhd->bhsm', q, k).astype(jnp.float32) * (XA_HEAD_DIM ** -0.5)
    p = jax.nn.softmax(s, axis=-1).astype(v.dtype)
    o = jnp.einsum('bhsm,bmhd->bshd', p, v).reshape(B, S, D)
    return o @ wo

def conv_ffn(h, w_up, conv_w, conv_b, w_down):
    z = h @ w_up
    u = z[..., :D_FF]
    g = dwconv3_centred(z[..., D_FF:], conv_w) + conv_b
    return (jax.nn.gelu(g, approximate=False) * u) @ w_down

def second_inputs(seed: int = 0) -> dict:
    key = jax.random.key(seed)
    ks = jax.random.split(key, 24)
    f32 = jnp.float32
    nrm = lambda k, shape, fan_in: jax.random.normal(k, shape, f32) * (fan_in ** -0.5)
    gain = lambda k, shape: 1.0 + 0.1 * jax.random.normal(k, shape, f32)
    D = D_MODEL
    return {
        "x": jax.random.normal(ks[0], (BATCH, SEQ, D), f32),
        "mem": jax.random.normal(ks[1], (BATCH, N_MEM, D), f32),
        "mem_norm_g": gain(ks[2], (D,)),
        "mix_norm_g": gain(ks[3], (DEPTH, D)),
        "w_in_ab": nrm(ks[4], (N_EVEN, D, AB_IN_WIDTH), D),
        "rpb": 0.02 * jax.random.normal(ks[5], (N_EVEN, NA_HEADS, 2 * NA_KH - 1, 2 * NA_KW - 1), f32),
        "w_out_ab": nrm(ks[6], (N_EVEN, AB_OUT_WIDTH, D), AB_OUT_WIDTH),
        "w_in_c": nrm(ks[7], (N_ODD, D, 3 * D), D),
        "conv_c": nrm(ks[8], (N_ODD, CONV_WIDTH, D), CONV_WIDTH),
        "w_out_c": nrm(ks[9], (N_ODD, D, D), D),
        "xa_norm_g": gain(ks[10], (DEPTH, D)),
        "xa_wq": nrm(ks[11], (DEPTH, D, D), D),
        "xa_wkv": nrm(ks[12], (DEPTH, D, 2 * D), D),
        "xa_wo": nrm(ks[13], (DEPTH, D, D), D),
        "ffn_norm_g": gain(ks[14], (DEPTH, D)),
        "ffn_w_up": nrm(ks[15], (DEPTH, D, 2 * D_FF), D),
        "ffn_conv_w": nrm(ks[16], (DEPTH, CONV_WIDTH, D_FF), CONV_WIDTH),
        "ffn_conv_b": 0.02 * jax.random.normal(ks[17], (DEPTH, D_FF), f32),
        "ffn_w_down": nrm(ks[18], (DEPTH, D_FF, D), D_FF),
        "final_norm_g": gain(ks[19], (D,)),
    }

def second_block(x, mem, mem_norm_g, mix_norm_g, w_in_ab, rpb, w_out_ab, w_in_c, conv_c, w_out_c,
              xa_norm_g, xa_wq, xa_wkv, xa_wo, ffn_norm_g, ffn_w_up, ffn_conv_w, ffn_conv_b,
              ffn_w_down, final_norm_g):
    m = rms_norm_2(mem, mem_norm_g)
    h = x
    for layer in range(DEPTH):
        hn = rms_norm_2(h, mix_norm_g[layer])
        if layer % 2 == 0:
            j = layer // 2
            h = h + fourier_na_mixer(hn, w_in_ab[j], rpb[j], w_out_ab[j])
        else:
            j = layer // 2
            h = h + short_gated_conv_mixer(hn, w_in_c[j], conv_c[j], w_out_c[j])
        h = h + memory_cross_attention(rms_norm_2(h, xa_norm_g[layer]), m,
                                       xa_wq[layer], xa_wkv[layer], xa_wo[layer])
        h = h + conv_ffn(rms_norm_2(h, ffn_norm_g[layer]), ffn_w_up[layer],
                         ffn_conv_w[layer], ffn_conv_b[layer], ffn_w_down[layer])
    return rms_norm_2(h, final_norm_g)


def setup_inputs(seed=0):
    out = dict(first_inputs(seed))
    for name, value in second_inputs(seed + 1).items():
        if name != "x":
            out[name + "_2"] = value
    return out


def reference(
    x, w_in_a, w_out_a, w_in_b, w_out_b, w_in_c, w_out_c, lambda_q1, lambda_k1, lambda_q2,
    lambda_k2, subln_g, ln_g, ln_b, mem_2, mem_norm_g_2, mix_norm_g_2, w_in_ab_2, rpb_2,
    w_out_ab_2, w_in_c_2, conv_c_2, w_out_c_2, xa_norm_g_2, xa_wq_2, xa_wkv_2, xa_wo_2,
    ffn_norm_g_2, ffn_w_up_2, ffn_conv_w_2, ffn_conv_b_2, ffn_w_down_2, final_norm_g_2,
):
    x = first_block(
        x, w_in_a, w_out_a, w_in_b, w_out_b, w_in_c, w_out_c, lambda_q1, lambda_k1, lambda_q2,
        lambda_k2, subln_g, ln_g, ln_b,
    )
    return second_block(
        x, mem_2, mem_norm_g_2, mix_norm_g_2, w_in_ab_2, rpb_2, w_out_ab_2, w_in_c_2, conv_c_2,
        w_out_c_2, xa_norm_g_2, xa_wq_2, xa_wkv_2, xa_wo_2, ffn_norm_g_2, ffn_w_up_2,
        ffn_conv_w_2, ffn_conv_b_2, ffn_w_down_2, final_norm_g_2,
    )


_drawn_inputs = setup_inputs


def setup_inputs(seed=0):
    import zlib

    import numpy as np

    out = dict(_drawn_inputs(seed))
    spreads = {}
    factors = {'rpb_2': 8.0, 'xa_norm_g_2': 3.354, 'ffn_conv_b_2': 3.534}
    for name, (base, spread) in spreads.items():
        noise = np.random.default_rng([zlib.crc32(name.encode()), seed]).standard_normal(out[name].shape)
        drawn = base * np.exp(spread * noise) if base else spread * noise
        out[name] = __import__('jax').numpy.asarray(drawn.astype(out[name].dtype))
    for name, factor in factors.items():
        out[name] = (out[name] * factor).astype(out[name].dtype)
    return out
```

```python
import math
from contextlib import ExitStack

import numpy as np

import concourse.bass as bass
from concourse import mybir

F32 = mybir.dt.float32
F32R = mybir.dt.float32r
ALU = mybir.AluOpType
ACT = mybir.ActivationFunctionType

P = 128
D = 1024
S = 256
KT = D // P
CW = 256
CHUNK = 64
TOPK = min(256, S // 4)
ALPHA = (2.0 * 2) ** 0.25
HD = 64
NH = D // HD
IH = 8
GW = 64
LN_EPS, RMS_EPS = 1e-5, 1e-6
NEG = -1.0e30
TAKEN = -3.0e38
RAW_SLOTS = 4
NA_SCALE = float(P) ** -0.5
XA_SCALE = float(CW) ** -0.5

VEC = {}
_at = 0
for _name, _n in (("ln_g0", 8), ("ln_g1", 8), ("ln_b0", 8), ("ln_b1", 8), ("mem", 8), ("mix0", 8), ("mix1", 8),
                  ("xa0", 8), ("xa1", 8), ("ffn0", 8), ("ffn1", 8), ("fin", 8), ("conv_c", 24),
                  ("fconv0", 48), ("fconv1", 48), ("fbias0", 16), ("fbias1", 16)):
    VEC[_name] = _at
    _at += _n
NVEC = _at

CST = {}
_at = 0
for _name, _n in (("ident", 128), ("cos", 256), ("sin", 256), ("adm", 512), ("before", 384), ("beforeneg", 384),
                  ("tri", 128), ("colneg", 256)):
    CST[_name] = (_at, _at + _n)
    _at += _n
NCST = _at


class Phase:
    pass


def schedule():
    phases, at, count = {}, 0, {"act": 0, "dve": 0}
    order = []

    def add(name, chunks, reader, outs=None, deep=1):
        nonlocal at
        p = Phase()
        p.name, p.n0, p.n, p.deep, p.reader = name, at, chunks, deep, reader
        p.outs = outs if outs is not None else chunks // deep
        p.base = count[reader]
        p.end = p.base + p.outs
        count[reader] += p.outs
        p.pair = 2 * (len(order) % 2)
        p.before = order[-2] if len(order) >= 2 else None
        at += chunks
        phases[name] = p
        order.append(p)

    add("ki", 0, "act", 1)
    add("qi", 2, "act")
    add("qa", 4, "act")
    add("ka", 4, "act")
    add("va", 4, "act")
    add("ga", 4, "act")
    add("attA", 0, "dve", 8)
    add("oa", 4, "dve")
    add("qb", 4, "act")
    add("kb", 4, "act")
    add("vb", 4, "act")
    add("gb", 4, "act")
    add("attB", 0, "dve", 8)
    add("ob", 4, "dve")
    add("zf", 2, "act")
    add("qn", 2, "dve")
    add("kn", 2, "dve")
    add("vn", 2, "act")
    add("fourier", 0, "dve", 4)
    add("attN", 0, "dve", 4)
    add("oab", 4, "dve")
    for l in "01":
        if l == "1":
            add("cb", 4, "dve")
            add("cc", 4, "dve")
            add("cu", 4, "dve")
            add("oc", 4, "dve")
        add("kx" + l, 4, "act")
        add("vx" + l, 4, "act")
        add("qx" + l, 4, "dve")
        add("attX" + l, 0, "dve", 4)
        add("ox" + l, 4, "dve")
        add("fu" + l, 8, "dve")
        add("fg" + l, 8, "dve")
        add("fd" + l, 8, "dve", deep=2)
    return phases, at


PH, NCHUNK = schedule()


def bases(*uses):
    table, n = {}, 0
    for name, times in uses:
        table[name] = n
        n += times
    return table


XBASE = bases(*[(u, 4) for u in ("first", "B", "mix0", "xa0", "ffn0", "mix1", "xa1", "ffn1")])
GBASE = bases(("A", 8), ("B", 8), ("ffn0", 8), ("conv", 4), ("ffn1", 8))
YBASE = bases(("A", 8), ("B", 8), ("F", 4), ("N", 4), ("X0", 4), ("ffn0", 8), ("conv", 4), ("X1", 4), ("ffn1", 8))
UBASE = bases(("A", 16), ("N", 4), ("X0", 4), ("X1", 4))
OBASE = bases(("A", 16), ("B", 16), ("F", 4), ("N", 4), ("X0", 4), ("X1", 4))
CBASE = bases(("ffn0", 8), ("conv", 4), ("ffn1", 8))
GEBASE = bases(("ffn0", 8), ("ffn1", 8))
STAT = bases(*[(u, 1) for u in ("mean0", "var0", "mem", "mean1", "var1", "mix0", "xa0", "ffn0", "mix1", "xa1",
                                "ffn1", "fin")])
POW = bases(*[(u, 1) for u in ("var0", "mem", "var1", "mix0", "xa0", "ffn0", "mix1", "xa1", "ffn1", "fin")])
RBS = bases(*[(u, 1) for u in ("mem", "mix0", "xa0", "ffn0", "mix1", "xa1", "ffn1")])
SQ = bases(*[(u, 4) for u in POW])


def build(nc, w, xt, memt, vecs, cst, wki, wwi, dft, rpb, out):
    ctx = ExitStack()
    with ctx:
        def sb(name, shape, dt=F32):
            return ctx.enter_context(nc.sbuf_tensor(name, shape, dt))

        def sem(name):
            return ctx.enter_context(nc.semaphore(name))

        raw = sb("raw", [P, RAW_SLOTS, KT, CW])
        wh = sb("wh", [P, 2, KT, CW], F32R)
        wl = sb("wl", [P, 2, KT, CW], F32R)
        h = sb("h", [P, KT, S])
        xh = sb("xh", [P, KT, S], F32R)
        xl = sb("xl", [P, KT, S], F32R)
        yh = sb("yh", [P, 2 * KT, S], F32R)
        yl = sb("yl", [P, 2 * KT, S], F32R)
        qz = sb("qz", [P, NH, S])
        kt = sb("kt", [P, KT, S])
        v = sb("v", [P, 2, D])
        gt = sb("gt", [P, KT, S])
        work = sb("work", [P, 12 * 512])
        cs = sb("cs", [P, NCST])
        vec = sb("vec", [P, NVEC])
        ones = sb("ones", [P, P])
        half = sb("half", [P, 2])
        acc = sb("acc", [P, 2, S])
        rb = sb("rb", [P, S])
        diag = sb("diag", [P, 2, P])
        stat = sb("stat", [P, 2])
        rt = sb("rt", [P, 2])
        wi = sb("wi", [P, 2, IH])
        top8 = sb("top8", [P, 2, 8])
        nmax = sb("nmax", [P, 28, 2])
        esum = sb("esum", [P, 28, 2])
        erec = sb("erec", [P, 28, 2])
        bank = [ctx.enter_context(nc.psum_tensor(f"bank{i}", [P, 512], F32)) for i in range(8)]
        m_scratch = nc.dram_tensor("m_scratch", [2, P, KT * S], F32, kind="Internal").ap()

        def wk(i):
            return work[:, 512 * i:512 * i + 512]

        def wk3(i):
            return wk(i).rearrange("p (a b) -> p a b", a=2)

        def c_(name):
            a, b = CST[name]
            return cs[:, a:b]

        def vc(name, j):
            return vec[:, VEC[name] + j:VEC[name] + j + 1]

        def b3(i):
            return bank[i][:, :].rearrange("p (a b) -> p a b", a=2)

        ident, cosT, sinT = c_("ident"), c_("cos"), c_("sin")
        adm = c_("adm").rearrange("p (a b) -> p a b", a=2)
        qiz = gt
        ki = xh_ki = work[:, 11 * 512:11 * 512 + 256]
        kiw = v[:, :, :].rearrange("p a b -> p (a b)")[:, 0:KT * P].rearrange("p (k n) -> p k n", k=KT)
        wiw = v[:, :, :].rearrange("p a b -> p (a b)")[:, KT * P:KT * P + KT * IH].rearrange("p (k n) -> p k n", k=KT)
        nabias = qz[:, 4:12, :].rearrange("p (h t) s -> p h t s", t=2)
        u_tok = qz[:, 12:16, :].rearrange("p a b -> p (a b)").rearrange("p (t n) -> p t n", t=2)
        gflat = gt[:, :, :].rearrange("p a b -> p (a b)")
        dft_s = gflat[:, 0:1024].rearrange("p (t n) -> p t n", t=2)
        dft_c = gflat[:, 1024:1280]
        score, selneg = wk3(8), wk3(9)
        cpad = [work[:, 516 * i:516 * i + 516].rearrange("p (a b) -> p a b", a=2) for i in range(2)]

        raw_full = [sem(f"raw_full{i}") for i in range(RAW_SLOTS)]
        const_in, x_in, kiw_in = sem("const_in"), sem("x_in"), sem("kiw_in")
        mem_in, m_saved, m_back = sem("mem_in"), sem("m_saved"), sem("m_back")
        rpb_in, dft_in, stored = sem("rpb_in"), sem("dft_in"), sem("stored")
        hi_ready, lo_ready = sem("hi_ready"), sem("lo_ready")
        w_used = sem("w_used")
        act_evac, dve_evac = sem("act_evac"), sem("dve_evac")
        evac = {"act": act_evac, "dve": dve_evac}
        filled = sem("filled")
        ki_full, wi_full, wi_ready = sem("ki_full"), sem("wi_full"), sem("wi_ready")
        rope_rot, rope_cos, rope_done = sem("rope_rot"), sem("rope_cos"), sem("rope_done")
        is_full, rel_ready, is_added = sem("is_full"), sem("rel_ready"), sem("is_added")
        picked = sem("picked")
        x_hi, x_lo = sem("x_hi"), sem("x_lo")
        sq_ready, acc_done = sem("sq_ready"), sem("acc_done")
        st_full, st_read, st_pow, st_diag = sem("st_full"), sem("st_read"), sem("st_pow"), sem("st_diag")
        bc_full, rb_ready = sem("bc_full"), sem("rb_ready")
        s_full, s_read, e_done, p_ready = sem("s_full"), sem("s_read"), sem("e_done"), sem("p_ready")
        t_full, t_evac, o_full = sem("t_full"), sem("t_evac"), sem("o_full")
        y_hi, g_lo = sem("y_hi"), sem("g_lo")
        z_full, z_abs, z_ln, z_sp = sem("z_full"), sem("z_abs"), sem("z_ln"), sem("z_sp")
        z_masked, z_neg, c_full, z_arg, z_prob = sem("z_masked"), sem("z_neg"), sem("c_full"), sem("z_arg"), sem("z_prob")
        f_full, f_copied = sem("f_full"), sem("f_copied")
        ln_c, ln_g, ln_h = sem("ln_c"), sem("ln_g"), sem("ln_h")
        gate_in, cv_ready, ge_ready, pf_ready = sem("gate_in"), sem("cv_ready"), sem("ge_ready"), sem("pf_ready")
        m_norm, m_hi, m_lo = sem("m_norm"), sem("m_hi"), sem("m_lo")
        bias_ready, zero_ready, padded = sem("bias_ready"), sem("zero_ready"), sem("padded")
        chain_act, chain_dve, chain_pool = sem("chain_act"), sem("chain_dve"), sem("chain_pool")
        fin_ready = sem("fin_ready")

        class Chain:
            def __init__(self, eng, s):
                self.eng, self.s, self.n = eng, s, 0

            def __call__(self, ins):
                self.n += 1
                ins.then_inc(self.s, 1)
                self.eng.wait_ge(self.s, self.n)

        block = ctx.enter_context(nc.Block())

        @block.sync
        def _(sp):
            def load(n, slot):
                sp.dma_start(raw[:, slot, :, :], w[n]).then_inc(raw_full[slot], 16)

            for n in range(RAW_SLOTS):
                load(n, n)
            rest = NCHUNK - RAW_SLOTS
            with sp.Fori(1, 1 + rest // RAW_SLOTS) as i:
                for c in range(RAW_SLOTS):
                    sp.wait_ge(lo_ready, 2 * RAW_SLOTS * i - 2 * RAW_SLOTS + 2 * c + 2)
                    sp.dma_start(raw[:, c, :, :],
                                 w[bass.ds(RAW_SLOTS * i + c, 1)].rearrange("o p k n -> (o p) k n")
                                 ).then_inc(raw_full[c], 16)
            for n in range(NCHUNK - rest % RAW_SLOTS, NCHUNK):
                sp.wait_ge(lo_ready, 2 * (n - RAW_SLOTS) + 2)
                load(n, n % RAW_SLOTS)
            for c in range(4):
                sp.wait_ge(fin_ready, 2 * c + 2)
                sp.dma_start(out[:, 2 * c:2 * c + 2, :], gt[:, 2 * c:2 * c + 2, :]).then_inc(stored, 16)
            sp.wait_ge(stored, 64)
            sp.wait_ge(m_saved, 32)

        @block.tensor
        def _(pe):
            def enter(p):
                if p.before is not None:
                    pe.wait_ge(evac[p.before.reader], p.before.end)

            def project(name, oh, ol, ready, tok=False, hooks={}, tile0=0):
                p = PH[name]
                enter(p)
                per = 2 * p.deep

                def round_(i, first):
                    for c in range(per):
                        n = per * i + (p.n0 + c)
                        slot = (p.n0 + c) % 2
                        b = b3(p.pair + c // p.deep)
                        k0 = (c % p.deep) * KT
                        if c % p.deep == 0 and not first:
                            pe.wait_ge(evac[p.reader], 2 * i + (p.base + c // p.deep - 1))
                        for j in range(2):
                            if tok and j == 0:
                                pe.wait_ge(lo_ready, 2 * n + 2)
                            if not tok:
                                pe.wait_ge(lo_ready, 2 * n + (j + 1))
                            for k in range(KT):
                                if j == 0 and c < p.deep and ready(k0 + k):
                                    pe.wait_ge(*ready(k0 + k))
                                kk, part = tile0 + k0 + k, slice(j * P, j * P + P)
                                if tok:
                                    ops = (oh[:, kk, part], ol[:, kk, part], wh[:, slot, k, :], wl[:, slot, k, :])
                                else:
                                    ops = (wh[:, slot, k, part], wl[:, slot, k, part], oh[:, kk, :], ol[:, kk, :])
                                mm = split_product(b[:, j, :], *ops, k0 + k == 0 and (p.deep == 1 or j == 0),
                                                   k0 + k == KT * p.deep - 1, p.deep > 1)
                            if not tok:
                                mm.then_inc(w_used, 1)
                            elif j == 1:
                                mm.then_inc(w_used, 2)
                            if first and (c, j) in hooks:
                                hooks[(c, j)]()

                rounds = p.n // per
                if hooks or p.base < 2:
                    round_(0, True)
                    for i in range(1, rounds if rounds < 3 else 1):
                        round_(i, False)
                    if rounds >= 3:
                        with pe.Fori(1, rounds) as i:
                            round_(i, False)
                elif rounds == 1:
                    round_(0, True)
                else:
                    with pe.Fori(0, rounds) as i:
                        round_(i, False)

            def split_product(o, ah, al, bh, bl, start, stop, skip):
                pe.matmul(o, ah, bh, start=start, stop=False, skip_group_check=skip)
                pe.matmul(o, ah, bl, start=False, stop=False, skip_group_check=skip)
                return pe.matmul(o, al, bh, start=False, stop=stop, skip_group_check=skip)

            def stats(name):
                pe.wait_ge(acc_done, 3 * STAT[name] + 3)
                for t in range(2):
                    for e in range(2):
                        mm = pe.matmul(bank[4][:, t:t + 1], acc[:, e, t * P:t * P + P], ones[:, 0:1],
                                       start=(e == 0), stop=(e == 1))
                mm.then_inc(st_full, 1)

            def bcast(name):
                pe.wait_ge(st_diag, 2 * STAT[name] + 2)
                pe.matmul(bank[5][:, 0:S], ones[:, :], diag[:, :, :].rearrange("p a b -> p (a b)"),
                          start=True, stop=True).then_inc(bc_full, 1)

            def x_ready(use):
                return lambda k: (x_lo, XBASE[use] + k // 2 + 1) if k % 2 == 0 else None

            nothing = lambda k: None

            def soft_attention(name, heads, score_ops, value_ops, group, p):
                u0 = UBASE[name]
                enter(p)

                def scores(a):
                    u = u0 + a
                    if a >= 2:
                        pe.wait_ge(s_read, 2 * (u - 1))
                    for t in range(2):
                        ops = score_ops(a, t)
                        for j, (l, r) in enumerate(ops):
                            mm = pe.matmul(b3(4 + a % 2)[:, t, :], l, r, start=(j == 0), stop=(j == len(ops) - 1))
                    mm.then_inc(s_full, 1)

                def turn(a):
                    u = u0 + a
                    pe.wait_ge(p_ready, 2 * u + 2)
                    if a >= 2:
                        pe.wait_ge(t_evac, u - 1)
                    pr = wk3((2, 3, 6)[a % 3])
                    for s in range(2):
                        for t in range(2):
                            mm = pe.transpose(b3(6 + a % 2)[:, s, t * P:t * P + P], pr[:, t, s * P:s * P + P], ident)
                    mm.then_inc(t_full, 1)

                def values(a):
                    u = u0 + a
                    pe.wait_ge(t_evac, u + 1)
                    g = a // group
                    if a % group == 0 and g >= 2:
                        pe.wait_ge(dve_evac, p.base + g - 1)
                    for o, sl in value_ops(a, p.pair + g % 2):
                        for s in range(2):
                            mm = pe.matmul(o, v[:, s, sl], wk3(4 + a % 2)[:, s, :], start=(s == 0), stop=(s == 1))
                    mm.then_inc(o_full, 1)

                for t in range(heads + 3):
                    if t < heads:
                        scores(t)
                    if 2 <= t < heads + 2:
                        turn(t - 2)
                    if t >= 3:
                        values(t - 3)

            def norm_hooks(name):
                return {(0, 0): lambda: stats(name), (0, 1): lambda: bcast(name)}

            pe.wait_ge(x_in, 16)
            pe.wait_ge(kiw_in, 32)
            pe.wait_ge(filled, 2)
            for k in range(KT):
                mm = pe.matmul(bank[0][:, 0:S], kiw[:, k, :], h[:, k, :], start=(k == 0), stop=(k == KT - 1))
            mm.then_inc(ki_full, 1)
            for t in range(2):
                for k in range(KT):
                    mm = pe.matmul(bank[4][:, 8 * t:8 * t + IH], h[:, k, t * P:t * P + P], wiw[:, k, :],
                                   start=(k == 0), stop=(k == KT - 1))
            mm.then_inc(wi_full, 1)
            project("qi", xh, xl, x_ready("first"))
            project("qa", xh, xl, nothing)
            pe.wait_ge(rope_done, 3)
            pe.wait_ge(wi_ready, 1)
            for a in range(IH):
                if a >= 2:
                    pe.wait_ge(rel_ready, a - 1)
                for t in range(2):
                    mm = pe.matmul(b3(4 + a % 2)[:, t, :], qiz[:, a, t * P:t * P + P], ki, start=True, stop=True)
                mm.then_inc(is_full, 1)
            project("ka", xh, xl, nothing)
            project("va", xh, xl, nothing, tok=True)
            project("ga", xh, xl, nothing)

            pe.wait_ge(rel_ready, IH)
            pe.wait_ge(rope_done, 11)
            pe.wait_ge(act_evac, PH["va"].end)
            soft_attention("A", NH, lambda a, t: [(qz[:, a, t * P:t * P + P], kt[:, a // 2, :])],
                           lambda a, b: [(bank[b][HD * (a % 2):HD * (a % 2) + HD, 0:S], slice(HD * a, HD * a + HD))],
                           2, PH["attA"])
            project("oa", yh, yl, lambda k: (g_lo, GBASE["A"] + k + 1))
            for name in ("mean0", "var0"):
                stats(name)
                bcast(name)
            project("qb", xh, xl, x_ready("B"))
            project("kb", xh, xl, nothing)
            stats("mem")
            bcast("mem")
            project("vb", xh, xl, nothing, tok=True)
            project("gb", xh, xl, nothing)

            pe.wait_ge(act_evac, PH["vb"].end)
            pb = PH["attB"]
            enter(pb)
            tri = c_("tri")
            LATE = slice(P, S)

            def z_scores(a):
                if a >= 2:
                    pe.wait_ge(z_neg, a - 1)
                b = bank[4 + a % 2]
                pe.matmul(b[:, 0:S], kt[:, a // 2, 0:P], qz[:, a, :], start=True, stop=True)
                pe.matmul(b[:, S:S + P], kt[:, a // 2, LATE], qz[:, a, LATE], start=True, stop=True).then_inc(z_full, 1)

            def z_sums(a):
                pe.wait_ge(z_masked, a + 1)
                if a >= 2:
                    pe.wait_ge(z_arg, a - 1)
                b, sp_ = bank[6 + a % 2], wk(4 + a % 2)
                pe.matmul(b[:, 0:P], tri, sp_[:, 0:P], start=True, stop=True)
                pe.matmul(b[:, P:S], tri, sp_[:, P:S], start=True, stop=False)
                pe.matmul(b[:, P:S], ones[:, :], sp_[:, S:S + P], start=False, stop=True)
                pe.matmul(b[:, S:S + P], tri, sp_[:, S:S + P], start=True, stop=True).then_inc(c_full, 1)

            def z_values(a):
                pe.wait_ge(z_prob, a + 1)
                g = a // 2
                if a % 2 == 0 and g >= 2:
                    pe.wait_ge(dve_evac, pb.base + g - 1)
                r = slice(HD * (a % 2), HD * (a % 2) + HD)
                b, pr, cols = bank[pb.pair + g % 2], wk(8 + a % 2), slice(HD * a, HD * a + HD)
                pe.matmul(b[r, 0:P], v[:, 0, cols], pr[:, 0:P], start=True, stop=True)
                pe.matmul(b[r, P:S], v[:, 0, cols], pr[:, P:S], start=True, stop=False)
                pe.matmul(b[r, P:S], v[:, 1, cols], pr[:, S:S + P], start=False, stop=True).then_inc(o_full, 1)

            for t in range(NH + 4):
                if t < NH:
                    z_scores(t)
                if 2 <= t < NH + 2:
                    z_sums(t - 2)
                if t >= 4:
                    z_values(t - 4)
            project("ob", yh, yl, lambda k: (g_lo, GBASE["B"] + k + 1))
            for name in ("mean1", "var1"):
                stats(name)
                bcast(name)

            project("zf", xh, xl, x_ready("mix0"), tok=True, hooks=norm_hooks("mix0"))
            project("qn", xh, xl, nothing)
            project("kn", xh, xl, nothing)
            project("vn", xh, xl, nothing, tok=True)
            pe.wait_ge(act_evac, PH["zf"].end)
            pe.wait_ge(dft_in, 32)
            pf = PH["fourier"]
            enter(pf)

            def f_tokens(g):
                if g >= 2:
                    pe.wait_ge(f_copied, g - 1)
                for t in range(2):
                    mm = pe.matmul(bank[6 + g % 2][:, :], u_tok[:, t, g * P:g * P + P], dft_s[:, t, :],
                                   start=(t == 0), stop=(t == 1))
                mm.then_inc(f_full, 1)

            def f_channels(g):
                pe.wait_ge(f_copied, g + 1)
                if g >= 2:
                    pe.wait_ge(dve_evac, pf.base + g - 1)
                b = bank[pf.pair + g % 2]
                pe.matmul(b[:, 0:S], dft_c[:, 0:P], wk(g % 2)[:, 0:S], start=True, stop=False)
                pe.matmul(b[:, 0:S], dft_c[:, P:S], wk(g % 2)[:, S:2 * S], start=False, stop=True).then_inc(o_full, 1)

            for g in range(5):
                if g < 4:
                    f_tokens(g)
                if g >= 1:
                    f_channels(g - 1)
            pe.wait_ge(dve_evac, PH["kn"].end)
            pe.wait_ge(act_evac, PH["vn"].end)
            pn = PH["attN"]
            soft_attention("N", 4, lambda a, t: [(qz[:, a, t * P:t * P + P], kt[:, a, :])],
                           lambda a, b: [(bank[b][:, 0:S], slice(P * a, P * a + P))], 1, pn)
            project("oab", yh, yl, lambda k: (dve_evac, (pf.base + k if k < 4 else pn.base + k - 4) + 1))

            for l in "01":
                if l == "1":
                    project("cb", xh, xl, x_ready("mix1"), hooks=norm_hooks("mix1"))
                    project("cc", xh, xl, nothing)
                    project("cu", xh, xl, nothing)
                    project("oc", yh, yl, lambda k: (g_lo, GBASE["conv"] + k // 2 + 1) if k % 2 == 0 else None)
                if l == "0":
                    m_ready = lambda k: (m_lo, k // 2 + 1) if k % 2 == 0 else None
                else:
                    m_ready = lambda k: (m_back, 32) if k == 0 else None
                project("kx" + l, yh, yl, m_ready, tile0=KT)
                project("vx" + l, yh, yl, nothing, tok=True, tile0=KT)
                stats("xa" + l)
                project("qx" + l, xh, xl, x_ready("xa" + l), hooks={(0, 0): lambda l=l: bcast("xa" + l)})
                pe.wait_ge(act_evac, PH["vx" + l].end)
                pe.wait_ge(dve_evac, PH["qx" + l].end)
                pa = PH["attX" + l]
                soft_attention("X" + l, 4,
                               lambda a, t: [(qz[:, 2 * a + j, t * P:t * P + P], kt[:, 2 * a + j, :]) for j in range(2)],
                               lambda a, b: [(b3(b)[:, j, :], slice(CW * a + P * j, CW * a + P * j + P)) for j in range(2)],
                               1, pa)
                project("ox" + l, yh, yl,
                        lambda k, pa=pa: (dve_evac, pa.base + k // 2 + 1) if k % 2 == 0 else None)
                project("fu" + l, xh, xl, x_ready("ffn" + l), hooks=norm_hooks("ffn" + l))
                project("fg" + l, xh, xl, nothing)
                project("fd" + l, yh, yl,
                        lambda k, l=l: (g_lo, GBASE["ffn" + l] + k // 2 + 1) if k % 2 == 0 else None)
            stats("fin")
            bcast("fin")

        @block.scalar
        def _(act):
            chain = Chain(act, chain_act)

            def hi(h_):
                if h_ >= 2 * NCHUNK:
                    return
                n, j = divmod(h_, 2)
                if j == 0:
                    act.wait_ge(raw_full[n % RAW_SLOTS], 16 * (n // RAW_SLOTS + 1))
                if h_ >= 4:
                    act.wait_ge(w_used, h_ - 3)
                part = slice(j * P, j * P + P)
                act.activation(wh[:, n % 2, :, part], raw[:, n % RAW_SLOTS, :, part], ACT.Copy).then_inc(hi_ready, 1)

            def chunks(name, evacuate=None):
                p = PH[name]
                for c in range(p.n):
                    n = p.n0 + c
                    hi(2 * n + 3)
                    hi(2 * n + 4)
                    if c % p.deep == p.deep - 1 and evacuate is not None:
                        if p.reader == "act":
                            act.wait_ge(w_used, 2 * n + 2)
                        evacuate(c // p.deep, b3(p.pair + c // p.deep % 2))

            def rope_raw(r, src, width):
                if r >= 2:
                    act.wait_ge(rope_done, r - 1)
                act.activation(wk(r % 2)[:, 0:width], src, ACT.Copy).then_inc(act_evac, 1)

            def flat(b):
                return b.rearrange("p a b -> p (a b)")

            def square(stat, c, src):
                i = 3 * STAT[stat]
                if i + (1 if c >= 2 else 0) > 0:
                    act.wait_ge(acc_done, i + (1 if c >= 2 else 0))
                act.activation(wk3(10 + c % 2), src, ACT.Square).then_inc(sq_ready, 1)

            def x_high(c, gain):
                for j in range(2):
                    m = 2 * c + j
                    if gain is None:
                        ins = act.activation(xh[:, m, :], h[:, m, :], ACT.Copy)
                    else:
                        ins = act.activation(xh[:, m, :], h[:, m, :], ACT.Copy, scale=vc(gain, m))
                ins.then_inc(x_hi, 1)

            def residual(name, stat, gain):
                p = PH[name]
                for c in range(p.n):
                    n = p.n0 + c
                    hi(2 * n + 3)
                    hi(2 * n + 4)
                    if c % p.deep == p.deep - 1:
                        o = c // p.deep
                        act.wait_ge(dve_evac, p.base + o + 1)
                        if gain is not None:
                            x_high(o, gain)
                        square(stat, o, h[:, 2 * o:2 * o + 2, :])

            def spread(name):
                act.wait_ge(bc_full, STAT[name] + 1)
                act.activation(rb[:, :], bank[5][:, 0:S], ACT.Copy).then_inc(rb_ready, 1)

            def y_high(key, i, dst, src, s_, value):
                act.wait_ge(s_, value)
                act.activation(dst, src, ACT.Copy).then_inc(y_hi, 1)

            def soft_attention(name, heads, p, high, lag):
                u0, ob = UBASE[name], OBASE[name]
                for t in range(heads + lag):
                    if t < heads:
                        u = u0 + t
                        if t >= 3:
                            act.wait_ge(t_full, u - 2)
                        for q in range(2):
                            act.wait_ge(s_read, 2 * u + q + 1)
                            act.activation(wk3((2, 3, 6)[t % 3])[:, q, :], wk3(t % 2)[:, q, :], ACT.Exp,
                                           bias=nmax[:, u, q:q + 1], scale=-1.0,
                                           accum_out=esum[:, u, q:q + 1]).then_inc(e_done, 1)
                    if 2 <= t < heads + 2:
                        a = t - 2
                        u = u0 + a
                        act.wait_ge(t_full, u + 1)
                        if a >= 2:
                            act.wait_ge(o_full, ob + a - 1)
                        act.activation(wk(4 + a % 2), bank[6 + a % 2][:, :], ACT.Copy).then_inc(t_evac, 1)
                    high(t)

            def gated_high(key, p, t, lag):
                if t >= lag and (t - lag) % 2 == 0 and (t - lag) // 2 < 8:
                    g = (t - lag) // 2
                    act.wait_ge(dve_evac, p.base + g + 1)
                    act.activation(yh[:, g, :], wk(10 + g % 2)[:, 0:S], ACT.Copy).then_inc(y_hi, 1)

            act.dma_start(h[:, :, :], xt).then_inc(x_in, 16)
            act.dma_start(kiw, wki).then_inc(kiw_in, 16)
            act.dma_start(wiw, wwi).then_inc(kiw_in, 16)
            act.dma_start(cs[:, :], cst).then_inc(const_in, 16)
            act.dma_start(vec[:, :], vecs).then_inc(const_in, 16)
            act.wait_ge(x_in, 16)
            for c in range(4):
                x_high(c, None)
            for h_ in range(3):
                hi(h_)
            act.wait_ge(ki_full, 1)
            rope_raw(0, bank[0][:, 0:S], S)
            chunks("qi", lambda c, b: rope_raw(1 + c, flat(b), 2 * S))
            chunks("qa", lambda c, b: rope_raw(3 + c, flat(b), 2 * S))
            for a in range(IH):
                act.wait_ge(is_full, a + 1)
                if a >= 2:
                    act.wait_ge(is_added, 2 * a - 2)
                act.activation(wk(6 + a % 2), bank[4 + a % 2][:, :], ACT.Relu, scale=HD ** -0.5).then_inc(rel_ready, 1)
            chunks("ka", lambda c, b: rope_raw(7 + c, flat(b), 2 * S))

            def v_copy(c, b):
                act.activation(v[:, :, CW * c:CW * c + CW], b, ACT.Copy).then_inc(act_evac, 1)

            def k_copy(c, b):
                act.activation(kt[:, 2 * c:2 * c + 2, :], b, ACT.Copy).then_inc(act_evac, 1)

            def gate(c, b):
                act.activation(gt[:, 2 * c:2 * c + 2, :], b, ACT.Silu).then_inc(act_evac, 1)

            chunks("va", v_copy)
            chunks("ga", gate)
            soft_attention("A", NH, PH["attA"], lambda t: gated_high("A", PH["attA"], t, 5), 5)
            chunks("oa")

            def layer_norm(l, gain, stat):
                var = "var" + l
                i = int(l)
                for c in range(4):
                    act.wait_ge(ln_c, 4 * i + c + 1)
                    square(var, c, h[:, 2 * c:2 * c + 2, :])
                for m in range(KT):
                    act.wait_ge(ln_g, 8 * i + m + 1)
                    act.activation(h[:, m, :], h[:, m, :], ACT.Identity, bias=vc("ln_b" + l, m)).then_inc(ln_h, 1)
                    if m % 2:
                        act.wait_ge(ln_h, 8 * i + m + 1)
                        x_high(m // 2, gain)
                        if stat is not None:
                            square(stat, m // 2, h[:, m - 1:m + 1, :])

            layer_norm("0", None, None)
            act.wait_ge(e_done, 32)
            act.dma_start(work[:, 0:KT * S], memt).then_inc(mem_in, 16)

            def q_scaled(c, b):
                act.activation(qz[0:HD, 4 * c:4 * c + 4:2, :], b[0:HD], ACT.Copy, scale=HD ** -0.5)
                act.activation(qz[HD:P, 4 * c + 1:4 * c + 4:2, :], b[HD:P], ACT.Copy, scale=HD ** -0.5).then_inc(act_evac, 1)

            chunks("qb", q_scaled)
            act.wait_ge(mem_in, 16)
            memv = work[:, 0:KT * S].rearrange("p (k s) -> p k s", k=KT)

            def kb(c, b):
                k_copy(c, b)
                square("mem", c, memv[:, 2 * c:2 * c + 2, :])

            chunks("kb", kb)
            spread("mem")

            def vb(c, b):
                v_copy(c, b)
                act.wait_ge(m_norm, 2 * c + 2)
                act.activation(yh[:, KT + 2 * c:KT + 2 * c + 2, :], memv[:, 2 * c:2 * c + 2, :], ACT.Copy).then_inc(m_hi, 1)

            chunks("vb", vb)
            chunks("gb", gate)
            act.wait_ge(m_lo, 4)
            act.dma_start(m_scratch[0], yh[:, KT:, :].bitcast(F32).rearrange("p k s -> p (k s)")).then_inc(m_saved, 16)
            act.dma_start(m_scratch[1], yl[:, KT:, :].bitcast(F32).rearrange("p k s -> p (k s)")).then_inc(m_saved, 16)

            ZW = S + P
            pb = PH["attB"]
            for t in range(NH + 5):
                if t < NH:
                    z = wk(t % 2)[:, 0:ZW]
                    act.wait_ge(z_full, t + 1)
                    if t >= 2:
                        act.wait_ge(z_sp, t - 1)
                    act.activation(z, bank[4 + t % 2][:, 0:ZW], ACT.Abs).then_inc(z_abs, 1)
                    act.wait_ge(z_abs, t + 1)
                    chain(act.activation(z, z, ACT.Exp, scale=-1.0))
                    act.activation(z, z, ACT.Ln, bias=1.0).then_inc(z_ln, 1)
                if 3 <= t < NH + 3:
                    a = t - 3
                    pr = wk(8 + a % 2)[:, 0:ZW]
                    act.wait_ge(z_arg, a + 1)
                    act.activation(pr, pr, ACT.Exp).then_inc(z_prob, 1)
                gated_high("B", pb, t, 6)

            act.wait_ge(o_full, OBASE["B"] + NH)
            act.dma_start(nabias.rearrange("p h t s -> p (h t s)"), rpb).then_inc(rpb_in, 16)
            act.dma_start(gflat[:, 0:1024], dft[:, 0:1024]).then_inc(dft_in, 16)
            act.dma_start(gflat[:, 1024:1280], dft[:, 1024:1280]).then_inc(dft_in, 16)
            chunks("ob")
            layer_norm("1", "mix0", "mix0")

            def scaled_tokens(dst):
                def f(c, b):
                    act.wait_ge(st_pow, POW["mix0"] + 1)
                    for t in range(2):
                        ins = act.activation(dst[:, t, CW * c:CW * c + CW], b[:, t, :], ACT.Copy, scale=rt[:, t:t + 1])
                    ins.then_inc(act_evac, 1)
                return f

            chunks("zf", scaled_tokens(u_tok))
            spread("mix0")
            chunks("qn")
            chunks("kn")
            chunks("vn", scaled_tokens(v))
            pf = PH["fourier"]
            for g in range(5):
                if g < 4:
                    act.wait_ge(f_full, g + 1)
                    if g >= 2:
                        act.wait_ge(o_full, OBASE["F"] + g - 1)
                    act.activation(wk(g % 2), bank[6 + g % 2][:, :], ACT.Copy).then_inc(f_copied, 1)
                if g >= 1:
                    a = g - 1
                    y_high("F", a, yh[:, a, :], bank[pf.pair + a % 2][:, 0:S], o_full, OBASE["F"] + a + 1)

            def plain_high(name, heads, tiles, first):
                p = PH["att" + name]

                def f(t):
                    if t >= 4:
                        a = t - 4
                        act.wait_ge(o_full, OBASE[name] + a + 1)
                        act.activation(yh[:, first + tiles * a:first + tiles * a + tiles, :],
                                       b3(p.pair + a % 2)[:, 0:tiles, :], ACT.Copy).then_inc(y_hi, 1)
                return f

            soft_attention("N", 4, PH["attN"], plain_high("N", 4, 1, 4), 4)
            residual("oab", "xa0", "xa0")

            def products(key, n, name, gelu):
                def high(c):
                    act.wait_ge(pf_ready, CBASE[key] + c + 1)
                    act.activation(yh[:, 2 * c:2 * c + 2, :], wk3(7 + c % 2), ACT.Copy).then_inc(y_hi, 1)

                p = PH[name]
                for c in range(p.n):
                    hi(2 * (p.n0 + c) + 3)
                    hi(2 * (p.n0 + c) + 4)
                    if gelu:
                        act.wait_ge(cv_ready, CBASE[key] + c + 1)
                        if c >= 2:
                            act.wait_ge(pf_ready, CBASE[key] + c - 1)
                        act.activation(wk(5 + c % 2), wk(3 + c % 2), ACT.Gelu).then_inc(ge_ready, 1)
                    if c >= 1:
                        high(c - 1)
                high(p.n - 1)

            for l in "01":
                if l == "1":
                    fd = PH["fd0"]
                    act.wait_ge(w_used, 2 * (fd.n0 + fd.n))
                    act.wait_ge(m_saved, 32)
                    act.dma_start(yh[:, KT:, :].bitcast(F32).rearrange("p k s -> p (k s)"), m_scratch[0]).then_inc(m_back, 16)
                    act.dma_start(yl[:, KT:, :].bitcast(F32).rearrange("p k s -> p (k s)"), m_scratch[1]).then_inc(m_back, 16)
                    spread("mix1")
                    chunks("cb")
                    chunks("cc")
                    products("conv", 4, "cu", False)
                    residual("oc", "xa1", "xa1")
                chunks("kx" + l, k_copy)
                chunks("vx" + l, v_copy)
                spread("xa" + l)
                chunks("qx" + l)
                soft_attention("X" + l, 4, PH["attX" + l], plain_high("X" + l, 4, 2, 0), 4)
                residual("ox" + l, "ffn" + l, "ffn" + l)
                spread("ffn" + l)
                chunks("fu" + l)
                products("ffn" + l, 8, "fg" + l, True)
                if l == "0":
                    residual("fd0", "mix1", "mix1")
                else:
                    residual("fd1", "fin", None)

        @block.vector
        def _(dve):
            chain = Chain(dve, chain_dve)

            def both(*instructions):
                for ins in instructions:
                    chain.n += 1
                    ins.then_inc(chain_dve, 1)
                dve.wait_ge(chain_dve, chain.n)

            def lo(h_):
                if h_ >= 2 * NCHUNK:
                    return
                n, j = divmod(h_, 2)
                dve.wait_ge(hi_ready, h_ + 1)
                part = slice(j * P, j * P + P)
                dve.tensor_tensor(wl[:, n % 2, :, part], raw[:, n % RAW_SLOTS, :, part],
                                  wh[:, n % 2, :, part].bitcast(F32), ALU.subtract).then_inc(lo_ready, 1)

            def chunks(name, evacuate=None, between=None):
                p = PH[name]
                for c in range(p.n):
                    n = p.n0 + c
                    lo(2 * n + 3)
                    lo(2 * n + 4)
                    if c % p.deep == p.deep - 1 and evacuate is not None:
                        dve.wait_ge(w_used, 2 * n + 2)
                        evacuate(c // p.deep, b3(p.pair + c // p.deep % 2))
                    if between is not None:
                        between(c)

            def rotate(r, width):
                dve.wait_ge(act_evac, r + 1)
                if r >= 2:
                    dve.wait_ge(rope_done, r - 1)
                n = width // S
                for q in range(4):
                    to, frm = slice(32 * q, 32 * q + 32), slice(32 * (q ^ 1), 32 * (q ^ 1) + 32)
                    sines = sinT[frm, :].unsqueeze(1).broadcast_to([32, n, S])
                    ins = dve.tensor_tensor(wk(4 + r % 2)[to, 0:width].rearrange("p (a b) -> p a b", a=n),
                                            wk(r % 2)[frm, 0:width].rearrange("p (a b) -> p a b", a=n),
                                            sines, ALU.mult)
                ins.then_inc(rope_rot, 1)

            def x_low(c, use, gain):
                dve.wait_ge(x_hi, XBASE[use] + c + 1)
                if gain is None:
                    dve.tensor_tensor(xl[:, 2 * c:2 * c + 2, :], h[:, 2 * c:2 * c + 2, :],
                                      xh[:, 2 * c:2 * c + 2, :].bitcast(F32), ALU.subtract).then_inc(x_lo, 1)
                    return
                for j in range(2):
                    m = 2 * c + j
                    ins = dve.scalar_tensor_tensor(xl[:, m, :], h[:, m, :], vc(gain, m), xh[:, m, :].bitcast(F32),
                                                   ALU.mult, ALU.subtract)
                ins.then_inc(x_lo, 1)

            def diagonal(name, src):
                for t in range(2):
                    dve.tensor_scalar(diag[:, t, :], ident, src[:, t:t + 1], None, ALU.mult).then_inc(st_diag, 1)

            def inverse_rms(name, eps):
                dve.wait_ge(st_full, STAT[name] + 1)
                dve.tensor_scalar(stat[:, :], bank[4][:, 0:2], 1.0 / D, eps, ALU.mult, ALU.add).then_inc(st_read, 1)
                dve.wait_ge(st_pow, POW[name] + 1)
                diagonal(name, rt)

            def residual(name, use, gain, alpha=None):
                p = PH[name]
                for c in range(p.n):
                    n = p.n0 + c
                    lo(2 * n + 3)
                    lo(2 * n + 4)
                    if c % p.deep == p.deep - 1:
                        o = c // p.deep
                        dve.wait_ge(w_used, 2 * n + 2)
                        hc, b = h[:, 2 * o:2 * o + 2, :], b3(p.pair + o % 2)
                        if alpha is None:
                            dve.tensor_tensor(hc, b, hc, ALU.add).then_inc(dve_evac, 1)
                        else:
                            hf = hc.rearrange("p a b -> p (a b)")
                            dve.scalar_tensor_tensor(hf, hf, alpha, bank[p.pair + o % 2][:, :], ALU.mult,
                                                     ALU.add).then_inc(dve_evac, 1)
                        if use is not None and o >= 1:
                            x_low(o - 1, use, gain)
                if use is not None:
                    x_low(3, use, gain)

            def soft_attention(name, heads, bias, scale, extra, lag):
                u0 = UBASE[name]
                for t in range(heads + lag):
                    if t < heads:
                        u = u0 + t
                        dve.wait_ge(s_full, u + 1)
                        if t >= 2:
                            dve.wait_ge(e_done, 2 * u - 2)
                        for q in range(2):
                            dve.tensor_tensor_reduce(wk3(t % 2)[:, q, :], b3(4 + t % 2)[:, q, :], bias(t)[:, q, :],
                                                     -scale, 3.0e38, ALU.add, ALU.min,
                                                     nmax[:, u, q:q + 1]).then_inc(s_read, 1)
                    if 1 <= t < heads + 1:
                        u = u0 + t - 1
                        dve.wait_ge(e_done, 2 * u + 2)
                        chain(dve.reciprocal(erec[:, u, :], esum[:, u, :]))
                        pr = wk3((2, 3, 6)[(t - 1) % 3])
                        for q in range(2):
                            dve.tensor_scalar(pr[:, q, :], pr[:, q, :], erec[:, u, q:q + 1], None,
                                              ALU.mult).then_inc(p_ready, 1)
                    extra(t)

            def gated(key, p, lag):
                def f(t):
                    if t >= lag and (t - lag) % 2 == 0 and (t - lag) // 2 < 8:
                        g = (t - lag) // 2
                        dve.wait_ge(o_full, OBASE[key] + 2 * g + 2)
                        if g >= 2:
                            dve.wait_ge(g_lo, GBASE[key] + g - 1)
                        dve.tensor_tensor(wk(10 + g % 2)[:, 0:S], bank[p.pair + g % 2][:, 0:S], gt[:, g, :],
                                          ALU.mult).then_inc(dve_evac, 1)
                return f

            def plain_low(name, tiles, first):
                p = PH["att" + name]

                def f(t):
                    if t >= 4:
                        a = t - 4
                        m = slice(first + tiles * a, first + tiles * a + tiles)
                        dve.wait_ge(y_hi, YBASE[name] + a + 1)
                        dve.tensor_tensor(yl[:, m, :], b3(p.pair + a % 2)[:, 0:tiles, :], yh[:, m, :].bitcast(F32),
                                          ALU.subtract).then_inc(dve_evac, 1)
                return f

            for c in range(4):
                x_low(c, "first", None)
            for h_ in range(3):
                lo(h_)
            dve.wait_ge(const_in, 32)
            rotate(0, S)
            dve.wait_ge(wi_full, 1)
            dve.tensor_scalar(wi[:, :, :].rearrange("p a b -> p (a b)"), bank[4][:, 0:2 * IH], IH ** -0.5, None,
                              ALU.mult).then_inc(wi_ready, 1)
            chunks("qi", lambda c, b: rotate(1 + c, 2 * S))
            chunks("qa", lambda c, b: rotate(3 + c, 2 * S))
            dve.wait_ge(wi_ready, 1)
            for a in range(IH):
                dve.wait_ge(rel_ready, a + 1)
                for t in range(2):
                    if a >= 1:
                        dve.wait_ge(is_added, 2 * a - 1 + t)
                    dve.scalar_tensor_tensor(score[:, t, :], wk3(6 + a % 2)[:, t, :], wi[:, t, a:a + 1],
                                             (score if a else adm)[:, t, :], ALU.mult, ALU.add).then_inc(is_added, 1)
            dve.wait_ge(is_added, 2 * IH)
            chunks("ka", lambda c, b: rotate(7 + c, 2 * S))

            def pick(c):
                both(*[dve.max(top8[:, t, :], score[:, t, :]) for t in range(2)])
                both(*[dve.match_replace(score[:, t, :], top8[:, t, :], score[:, t, :], TAKEN) for t in range(2)])

            assert TOPK == 8 * 8
            chunks("va", between=pick)
            chunks("ga", between=lambda c: pick(4 + c))
            chain(dve.tensor_scalar(selneg, score, 0.5 * TAKEN, NEG, ALU.is_gt, ALU.mult))
            soft_attention("A", NH, lambda a: selneg, HD ** -0.5, gated("A", PH["attA"], 5), 5)

            def layer_norm(l, use, gain):
                i = int(l)
                dve.wait_ge(st_full, STAT["mean" + l] + 1)
                chain(dve.tensor_scalar(stat[:, :], bank[4][:, 0:2], 1.0 / D, None, ALU.mult))
                diagonal("mean" + l, stat)
                dve.wait_ge(bc_full, STAT["mean" + l] + 1)
                for c in range(4):
                    hc = h[:, 2 * c:2 * c + 2, :]
                    dve.tensor_tensor(hc, hc, bank[5][:, 0:S].unsqueeze(1).broadcast_to([P, 2, S]),
                                      ALU.subtract).then_inc(ln_c, 1)
                dve.wait_ge(ln_c, 4 * i + 4)
                inverse_rms("var" + l, LN_EPS)
                dve.wait_ge(bc_full, STAT["var" + l] + 1)
                for m in range(KT):
                    dve.scalar_tensor_tensor(h[:, m, :], h[:, m, :], vc("ln_g" + l, m), bank[5][:, 0:S], ALU.mult,
                                             ALU.mult).then_inc(ln_g, 1)
                for c in range(4):
                    x_low(c, use, gain)

            residual("oa", None, None, ALPHA)
            layer_norm("0", "B", None)
            chunks("qb")
            chunks("kb")
            inverse_rms("mem", RMS_EPS)
            memv = work[:, 0:KT * S].rearrange("p (k s) -> p k s", k=KT)

            def mem(c):
                if c == 0:
                    dve.wait_ge(rb_ready, 1)
                for m in (2 * c, 2 * c + 1):
                    dve.scalar_tensor_tensor(memv[:, m, :], memv[:, m, :], vc("mem", m), rb[:, :], ALU.mult,
                                             ALU.mult).then_inc(m_norm, 1)
                if c >= 1:
                    mem_low(c - 1)

            def mem_low(c):
                dve.wait_ge(m_hi, c + 1)
                dve.tensor_tensor(yl[:, KT + 2 * c:KT + 2 * c + 2, :], memv[:, 2 * c:2 * c + 2, :],
                                  yh[:, KT + 2 * c:KT + 2 * c + 2, :].bitcast(F32), ALU.subtract).then_inc(m_lo, 1)

            chunks("vb", between=mem)
            mem_low(3)
            chunks("gb")

            ZW = S + P
            zgate = gated("B", PH["attB"], 5)
            for t in range(NH + 5):
                if 2 <= t < NH + 2:
                    a = t - 2
                    dve.wait_ge(c_full, a + 1)
                    if a >= 2:
                        dve.wait_ge(o_full, OBASE["B"] + a - 1)
                    dve.wait_ge(z_neg, a + 1)
                    dve.tensor_tensor(wk(8 + a % 2)[:, 0:ZW], wk(6 + a % 2)[:, 0:ZW], bank[6 + a % 2][:, 0:ZW],
                                      ALU.subtract).then_inc(z_arg, 1)
                if t < NH:
                    b = bank[4 + t % 2][:, 0:ZW]
                    dve.wait_ge(z_ln, t + 1)
                    if t >= 2:
                        dve.wait_ge(z_masked, t - 1)
                    dve.scalar_tensor_tensor(wk(2 + t % 2)[:, 0:ZW], b, 0.0, wk(t % 2)[:, 0:ZW], ALU.max,
                                             ALU.add).then_inc(z_sp, 1)
                    if t >= 2:
                        dve.wait_ge(z_arg, t - 1)
                    dve.tensor_tensor(wk(6 + t % 2)[:, 0:ZW], b, c_("beforeneg"), ALU.add).then_inc(z_neg, 1)
                zgate(t)
            residual("ob", None, None, ALPHA)
            layer_norm("1", "mix0", "mix0")

            def bias(c):
                dve.wait_ge(rpb_in, 16)
                for t in range(2):
                    dve.scalar_tensor_tensor(nabias[:, c, t, :], nabias[:, c, t, :], 1.0 / NA_SCALE, c_("colneg"),
                                             ALU.mult, ALU.add).then_inc(bias_ready, 1)

            def times_rb(dst):
                def f(c, b):
                    dve.tensor_tensor(dst[:, 2 * c:2 * c + 2, :], b, rb[:, :].unsqueeze(1).broadcast_to([P, 2, S]),
                                      ALU.mult).then_inc(dve_evac, 1)
                return f

            inverse_rms("mix0", RMS_EPS)
            chunks("zf", between=bias)
            dve.wait_ge(rb_ready, RBS["mix0"] + 1)
            chunks("qn", times_rb(qz), between=lambda c: bias(2 + c))
            chunks("kn", times_rb(kt))
            chunks("vn")
            pf = PH["fourier"]
            for g in range(4):
                dve.wait_ge(y_hi, YBASE["F"] + g + 1)
                dve.tensor_tensor(yl[:, g, :], bank[pf.pair + g % 2][:, 0:S], yh[:, g, :].bitcast(F32),
                                  ALU.subtract).then_inc(dve_evac, 1)
            dve.wait_ge(bias_ready, 8)
            soft_attention("N", 4, lambda a: nabias[:, a, :, :], NA_SCALE, plain_low("N", 1, 4), 4)
            residual("oab", "xa0", "xa0")

            def convolve(key, c, w0, bias_, buf):
                i = CBASE[key] + c
                cv, cp = wk3(3 + c % 2), cpad[c % 2]
                if c >= 2:
                    if bias_ is not None:
                        dve.wait_ge(ge_ready, GEBASE[key] + c - 1)
                    else:
                        dve.wait_ge(pf_ready, i - 1)
                first = []
                for j in range(2):
                    m = 2 * c + j
                    first.append(dve.tensor_scalar(cv[:, j, :], cp[:, j, 1:S + 1], vc(w0, buf + m),
                                                   vc(bias_, m) if bias_ is not None else 0.0, ALU.mult, ALU.add))
                both(*first)
                both(*[dve.scalar_tensor_tensor(cv[:, j, :], cp[:, j, 0:S], vc(w0, 2 * c + j), cv[:, j, :], ALU.mult,
                                                ALU.add) for j in range(2)])
                for j in range(2):
                    ins = dve.scalar_tensor_tensor(cv[:, j, :], cp[:, j, 2:S + 2], vc(w0, 2 * buf + 2 * c + j),
                                                   cv[:, j, :], ALU.mult, ALU.add)
                ins.then_inc(cv_ready, 1)

            for l in "01":
                if l == "1":
                    inverse_rms("mix1", RMS_EPS)
                    dve.wait_ge(rb_ready, RBS["mix1"] + 1)
                    chunks("cb", times_rb(qz))
                    chunks("cc", times_rb(kt))
                    pc = PH["cu"]
                    for c in range(pc.n):
                        n = pc.n0 + c
                        lo(2 * n + 3)
                        lo(2 * n + 4)
                        dve.wait_ge(w_used, 2 * n + 2)
                        if c >= 2:
                            dve.wait_ge(gate_in, c - 1)
                        dve.tensor_tensor(wk3(5 + c % 2), b3(pc.pair + c % 2), rb[:, :].unsqueeze(1).broadcast_to([P, 2, S]),
                                          ALU.mult).then_inc(dve_evac, 1)
                        if c >= 1:
                            dve.wait_ge(gate_in, c)
                            convolve("conv", c - 1, "conv_c", None, 8)
                    dve.wait_ge(gate_in, 4)
                    convolve("conv", 3, "conv_c", None, 8)
                    residual("oc", "xa1", "xa1")
                chunks("kx" + l)
                chunks("vx" + l)
                inverse_rms("xa" + l, RMS_EPS)
                dve.wait_ge(rb_ready, RBS["xa" + l] + 1)
                chunks("qx" + l, times_rb(qz))
                dve.wait_ge(zero_ready, 1)
                soft_attention("X" + l, 4, lambda a: adm, XA_SCALE, plain_low("X" + l, 2, 0), 4)
                residual("ox" + l, "ffn" + l, "ffn" + l)
                inverse_rms("ffn" + l, RMS_EPS)
                dve.wait_ge(rb_ready, RBS["ffn" + l] + 1)
                chunks("fu" + l, times_rb(qz))
                dve.wait_ge(padded, 4 + 4 * int(l))

                def gate_chunk(c, b, l=l):
                    dve.tensor_tensor(cpad[c % 2][:, :, 1:S + 1], b, rb[:, :].unsqueeze(1).broadcast_to([P, 2, S]),
                                      ALU.mult).then_inc(dve_evac, 1)
                    dve.wait_ge(dve_evac, PH["fg" + l].base + c + 1)
                    convolve("ffn" + l, c, "fconv" + l, "fbias" + l, 16)

                chunks("fg" + l, gate_chunk)
                if l == "0":
                    residual("fd0", "mix1", "mix1")
                else:
                    residual("fd1", None, None)
            inverse_rms("fin", RMS_EPS)
            dve.wait_ge(bc_full, STAT["fin"] + 1)
            for m in range(KT):
                dve.scalar_tensor_tensor(gt[:, m, :], h[:, m, :], vc("fin", m), bank[5][:, 0:S], ALU.mult,
                                         ALU.mult).then_inc(fin_ready, 1)

        @block.gpsimd
        def _(pool):
            chain = Chain(pool, chain_pool)
            pool.memset(ones[:, :], 1.0).then_inc(filled, 1)
            pool.memset(half[:, :], -0.5).then_inc(filled, 1)
            pool.memset(qiz[:, :, :], 0.0).then_inc(filled, 1)
            pool.memset(qz[0:HD, 1:NH:2, :], 0.0).then_inc(filled, 1)
            pool.wait_ge(filled, 4)
            pool.memset(qz[HD:P, 0:NH:2, :], 0.0).then_inc(filled, 1)
            pool.wait_ge(filled, 5)

            def rope(r, width, targets):
                n = width // S
                t1 = wk(2 + r % 2)[:, 0:width].rearrange("p (a b) -> p a b", a=n)
                t2 = wk(4 + r % 2)[:, 0:width].rearrange("p (a b) -> p a b", a=n)
                pool.wait_ge(act_evac, r + 1)
                pool.tensor_tensor(t1, wk(r % 2)[:, 0:width].rearrange("p (a b) -> p a b", a=n),
                                   cosT.unsqueeze(1).broadcast_to([P, n, S]), ALU.mult).then_inc(rope_cos, 1)
                pool.wait_ge(rope_cos, r + 1)
                pool.wait_ge(rope_rot, r + 1)
                for dst, rows in targets:
                    if rows.start > 0:
                        chain(ins)
                    ins = pool.tensor_tensor(dst, t1[rows], t2[rows], ALU.add)
                ins.then_inc(rope_done, 1)
                pool.wait_ge(rope_done, r + 1)

            def heads(dst, c):
                return [(dst[0:HD, 4 * c:4 * c + 4:2, :], slice(0, HD)), (dst[HD:P, 4 * c + 1:4 * c + 4:2, :], slice(HD, P))]

            def sum_up(name, source):
                first = source(0)
                for c in range(1, 4):
                    if c >= 2:
                        pool.wait_ge(acc_done, 3 * STAT[name] + c - 1)
                    a = first if c == 1 else acc[:, :, :]
                    pool.tensor_tensor(acc[:, :, :], a, source(c), ALU.add).then_inc(acc_done, 1)

            def squares(name):
                def source(c):
                    pool.wait_ge(sq_ready, SQ[name] + c + 1)
                    return wk3(10 + c % 2)
                return source

            def stream(name):
                def source(c):
                    pool.wait_ge(dve_evac, PH[name].base + c + 1)
                    return h[:, 2 * c:2 * c + 2, :]
                return source

            def power(name):
                pool.wait_ge(st_read, POW[name] + 1)
                pool.tensor_tensor(rt[:, :], stat[:, :], half[:, :], ALU.pow).then_inc(st_pow, 1)

            def norm(name):
                sum_up(name, squares(name))
                power(name)

            def gated_low(key, g):
                pool.wait_ge(y_hi, YBASE[key] + g + 1)
                pool.tensor_tensor(yl[:, g, :], wk(10 + g % 2)[:, 0:S], yh[:, g, :].bitcast(F32),
                                   ALU.subtract).then_inc(g_lo, 1)

            def product(key, c, a, b):
                if c >= 2:
                    pool.wait_ge(g_lo, GBASE[key] + c - 1)
                pool.tensor_tensor(wk3(7 + c % 2), a, b, ALU.mult).then_inc(pf_ready, 1)

            def product_low(key, c):
                pool.wait_ge(y_hi, YBASE[key] + c + 1)
                pool.tensor_tensor(yl[:, 2 * c:2 * c + 2, :], wk3(7 + c % 2), yh[:, 2 * c:2 * c + 2, :].bitcast(F32),
                                   ALU.subtract).then_inc(g_lo, 1)

            def ffn_products(key):
                for c in range(8):
                    pool.wait_ge(ge_ready, GEBASE[key] + c + 1)
                    product(key, c, wk3(5 + c % 2), qz[:, 2 * c:2 * c + 2, :])
                    if c >= 1:
                        product_low(key, c - 1)
                product_low(key, 7)

            def pads(name):
                pool.wait_ge(o_full, OBASE[name] + 4)
                pool.wait_ge(e_done, 2 * UBASE[name] + 8)
                for b in cpad:
                    for col in (0, S + 1):
                        pool.memset(b[:, :, col:col + 1], 0.0).then_inc(padded, 1)

            pool.wait_ge(const_in, 32)
            rope(0, S, [(ki.unsqueeze(1), slice(0, P))])
            for c in range(2):
                rope(1 + c, 2 * S, heads(qiz, c))
            for c in range(4):
                rope(3 + c, 2 * S, heads(qz, c))
            for c in range(4):
                rope(7 + c, 2 * S, [(kt[:, 2 * c:2 * c + 2, :], slice(0, P))])
            for g in range(8):
                gated_low("A", g)
            sum_up("mean0", stream("oa"))
            norm("var0")
            pool.memset(adm, 0.0).then_inc(zero_ready, 1)
            norm("mem")
            for t in range(NH + 6):
                if t < NH:
                    pool.wait_ge(z_sp, t + 1)
                    if t >= 2:
                        pool.wait_ge(c_full, t - 1)
                    ZW = S + P
                    pool.tensor_tensor(wk(4 + t % 2)[:, 0:ZW], wk(2 + t % 2)[:, 0:ZW], c_("before"),
                                       ALU.mult).then_inc(z_masked, 1)
                if t >= 6 and t % 2 == 0:
                    gated_low("B", (t - 6) // 2)
            sum_up("mean1", stream("ob"))
            norm("var1")
            norm("mix0")
            norm("xa0")
            pads("X0")
            norm("ffn0")
            ffn_products("ffn0")
            norm("mix1")
            for c in range(5):
                if c < 4:
                    pool.wait_ge(dve_evac, PH["cu"].base + c + 1)
                    if c >= 2:
                        pool.wait_ge(cv_ready, CBASE["conv"] + c - 1)
                    pool.tensor_tensor(cpad[c % 2][:, :, 1:S + 1], wk3(5 + c % 2), kt[:, 2 * c:2 * c + 2, :],
                                       ALU.mult).then_inc(gate_in, 1)
                if c >= 1:
                    a = c - 1
                    pool.wait_ge(cv_ready, CBASE["conv"] + a + 1)
                    product("conv", a, wk3(3 + a % 2), qz[:, 2 * a:2 * a + 2, :])
                if c >= 2:
                    product_low("conv", c - 2)
            product_low("conv", 3)
            norm("xa1")
            pads("X1")
            norm("ffn1")
            ffn_products("ffn1")
            norm("fin")


def tables():
    p = np.arange(P)
    cst = np.zeros((P, NCST), np.float32)

    def put(name, a):
        cst[:, CST[name][0]:CST[name][1]] = a.reshape(P, -1)

    put("ident", np.eye(P))
    inv = (1.0 / (np.float32(10000.0) ** (np.arange(0, HD, 2, dtype=np.float32) / np.float32(HD)))).astype(np.float32)
    ang = (np.arange(S, dtype=np.float32)[None, :] * inv[p % 32][:, None]).astype(np.float32)
    put("cos", np.cos(ang))
    put("sin", np.where((p // 32 % 2 == 0)[:, None], 1, -1) * np.sin(ang))
    s = np.arange(S)
    q = np.arange(2)[None, :] * P + p[:, None]
    put("adm", np.where(s[None, None, :] // CHUNK <= q[:, :, None] // CHUNK, 0.0, NEG))
    before = np.concatenate([p[:, None] < s[None, :], p[:, None] < p[None, :]], 1)
    put("before", before.astype(np.float32))
    put("beforeneg", np.where(before, 0.0, NEG))
    put("tri", (p[:, None] >= p[None, :]).astype(np.float32))
    start = np.clip(p % GW - 8, 0, GW - 16)[:, None]
    col = (s % GW)[None, :]
    put("colneg", np.where((col >= start) & (col < start + 16), 0.0, NEG))
    dft = np.zeros((P, 1280), np.float32)
    tok = (np.arange(2)[None, :, None] * P + p[:, None, None]) * s[None, None, :] % S
    a = 2 * np.pi * tok / S
    dft[:, 0:1024] = np.concatenate([np.cos(a), np.sin(a)], 2).reshape(P, -1)
    a = 2 * np.pi * (p[:, None] * p[None, :] % P) / P
    scale = 1.0 / math.sqrt(S * P)
    dft[:, 1024:1152] = np.cos(a) * scale
    dft[:, 1152:1280] = -np.sin(a) * scale
    return cst, dft


def neighbourhood_bias(rpb):
    s = np.arange(S)
    q = np.arange(2)[None, :] * P + np.arange(P)[:, None]
    dr = s[None, None, :] // GW - q[:, :, None] // GW + 7
    dc = np.clip(s[None, None, :] % GW - q[:, :, None] % GW + 15, 0, 30)
    return np.ascontiguousarray(rpb[:, dr, dc].transpose(1, 0, 2, 3)).reshape(P, -1)


def kernel(**inputs):
    import concourse.bacc as bacc
    from concourse.bass_utils import run_bass_kernel_spmd as run

    x = {k: np.asarray(a) for k, a in inputs.items()}

    def tiled(a):
        return np.ascontiguousarray(a.reshape(-1, P, a.shape[-1]).transpose(1, 0, 2))

    def cols(a, lo, hi):
        return [tiled(a[r:r + D, c:c + CW]) for c in range(lo, hi, CW) for r in range(0, a.shape[0], D)]

    wa, wb = x["w_in_a"][0], x["w_in_b"][0]
    IQ = 4 * D
    chunks = cols(wa, IQ, IQ + 512) + cols(wa, 0, 4 * D) + cols(x["w_out_a"][0], 0, D)
    chunks += cols(wb, 0, 4 * D) + cols(x["w_out_b"][0], 0, D)
    chunks += cols(x["w_in_ab_2"][0], 0, 2048) + cols(x["w_out_ab_2"][0], 0, D)
    for l in range(2):
        if l == 1:
            chunks += cols(x["w_in_c_2"][0], 0, 3 * D) + cols(x["w_out_c_2"][0], 0, D)
        chunks += cols(x["xa_wkv_2"][l], 0, 2 * D) + cols(x["xa_wq_2"][l], 0, D) + cols(x["xa_wo_2"][l], 0, D)
        chunks += cols(x["ffn_w_up_2"][l], 0, 4 * D) + cols(x["ffn_w_down_2"][l], 0, D)
    w = np.stack(chunks)
    assert w.shape == (NCHUNK, P, KT, CW)
    wki = tiled(np.concatenate([wa[:, IQ + 520:IQ + 584]] * 2, 1))
    wwi = tiled(wa[:, IQ + 512:IQ + 520])

    vecs = np.zeros((P, NVEC), np.float32)

    def put(name, a):
        a = np.ascontiguousarray(a).reshape(-1, P).T
        vecs[:, VEC[name]:VEC[name] + a.shape[1]] = a

    for l in range(2):
        put(f"ln_g{l}", x["ln_g"][l])
        put(f"ln_b{l}", x["ln_b"][l])
        put(f"mix{l}", x["mix_norm_g_2"][l])
        put(f"xa{l}", x["xa_norm_g_2"][l])
        put(f"ffn{l}", x["ffn_norm_g_2"][l])
        put(f"fconv{l}", x["ffn_conv_w_2"][l])
        put(f"fbias{l}", x["ffn_conv_b_2"][l])
    put("mem", x["mem_norm_g_2"])
    put("fin", x["final_norm_g_2"])
    put("conv_c", x["conv_c_2"][0])
    cst, dft = tables()

    nc = bacc.Bacc("TRN2", target_bir_lowering=False, num_devices=1)
    arrays = {
        "w": w, "xt": tiled(x["x"][0].T), "memt": tiled(x["mem_2"][0].T).reshape(P, -1), "vecs": vecs, "cst": cst,
        "wki": wki, "wwi": wwi, "dft": dft, "rpb": neighbourhood_bias(x["rpb_2"][0]),
    }
    args = [nc.dram_tensor(k, a.shape, F32, kind="ExternalInput").ap() for k, a in arrays.items()]
    args.append(nc.dram_tensor("y", (P, KT, S), F32, kind="ExternalOutput").ap())
    build(nc, *args)
    r = run(nc, [arrays], core_ids=[0])
    y = r.results[0]["y"]
    return np.ascontiguousarray(y.transpose(2, 1, 0)).reshape(1, S, D)
```

```python
import math
from contextlib import ExitStack

import numpy as np

import concourse.bass as bass
from concourse import mybir

F32 = mybir.dt.float32
F32R = mybir.dt.float32r
ALU = mybir.AluOpType
ACT = mybir.ActivationFunctionType

P = 128
D = 1024
S = 256
KT = D // P
CW = 256
CHUNK = 64
TOPK = min(256, S // 4)
ALPHA = (2.0 * 2) ** 0.25
HD = 64
NH = D // HD
IH = 8
GW = 64
LN_EPS, RMS_EPS = 1e-5, 1e-6
NEG = -1.0e30
TAKEN = -3.0e38
RAW_SLOTS = 4
NA_SCALE = float(P) ** -0.5
XA_SCALE = float(CW) ** -0.5

VEC = {}
_at = 0
for _name, _n in (("ln_g0", 8), ("ln_g1", 8), ("ln_b0", 8), ("ln_b1", 8), ("mem", 8), ("mix0", 8), ("mix1", 8),
                  ("xa0", 8), ("xa1", 8), ("ffn0", 8), ("ffn1", 8), ("fin", 8), ("conv_c", 24),
                  ("fconv0", 48), ("fconv1", 48), ("fbias0", 16), ("fbias1", 16)):
    VEC[_name] = _at
    _at += _n
NVEC = _at

CST = {}
_at = 0
for _name, _n in (("ident", 128), ("cos", 256), ("sin", 256), ("adm", 512), ("before", 384), ("beforeneg", 384),
                  ("tri", 128), ("colneg", 256)):
    CST[_name] = (_at, _at + _n)
    _at += _n
NCST = _at


class Phase:
    pass


def schedule():
    phases, at, count = {}, 0, {"act": 0, "dve": 0}
    order = []

    def add(name, chunks, reader, outs=None, deep=1):
        nonlocal at
        p = Phase()
        p.name, p.n0, p.n, p.deep, p.reader = name, at, chunks, deep, reader
        p.outs = outs if outs is not None else chunks // deep
        p.base = count[reader]
        p.end = p.base + p.outs
        count[reader] += p.outs
        p.pair = 2 * (len(order) % 2)
        p.before = order[-2] if len(order) >= 2 else None
        at += chunks
        phases[name] = p
        order.append(p)

    add("qi", 2, "act")
    add("ki", 0, "act", 1)
    add("qa", 4, "act")
    add("ka", 4, "act")
    add("va", 4, "act")
    add("ga", 4, "act")
    add("attA", 0, "dve", 8)
    add("oa", 4, "dve")
    add("kx0", 4, "dve")
    add("qb", 4, "act")
    add("kb", 4, "act")
    add("vb", 4, "act")
    add("gb", 4, "act")
    add("attB", 0, "dve", 8)
    add("ob", 4, "dve")
    add("kx1", 4, "dve")
    add("zf", 2, "act")
    add("qn", 2, "dve")
    add("kn", 2, "dve")
    add("vn", 2, "act")
    add("fourier", 0, "dve", 4)
    add("attN", 0, "dve", 4)
    add("oab", 4, "dve")
    for l in "01":
        if l == "1":
            add("cb", 4, "dve")
            add("cc", 4, "dve")
            add("cu", 4, "dve")
        add("vx" + l, 4, "act")
        if l == "1":
            add("oc", 4, "dve")
        add("qx" + l, 4, "dve")
        add("attX" + l, 0, "dve", 4)
        add("ox" + l, 4, "dve")
        add("fu" + l, 8, "dve")
        add("fg" + l, 8, "dve")
        add("fd" + l, 8, "dve", deep=2)
    return phases, at


PH, NCHUNK = schedule()


def bases(*uses):
    table, n = {}, 0
    for name, times in uses:
        table[name] = n
        n += times
    return table


XBASE = bases(*[(u, 4) for u in ("first", "B", "mix0", "xa0", "ffn0", "mix1", "xa1", "ffn1")])
GBASE = bases(("A", 8), ("B", 8), ("ffn0", 8), ("conv", 4), ("ffn1", 8))
YBASE = bases(("A", 8), ("B", 8), ("F", 4), ("N", 4), ("X0", 4), ("ffn0", 8), ("conv", 4), ("X1", 4), ("ffn1", 8))
UBASE = bases(("A", 16), ("N", 4), ("X0", 4), ("X1", 4))
OBASE = bases(("A", 16), ("B", 16), ("F", 4), ("N", 4), ("X0", 4), ("X1", 4))
CBASE = bases(("ffn0", 8), ("conv", 4), ("ffn1", 8))
GEBASE = bases(("ffn0", 8), ("ffn1", 8))
STAT = bases(*[(u, 1) for u in ("mem", "mean0", "var0", "mean1", "var1", "mix0", "xa0", "ffn0", "mix1", "xa1",
                                "ffn1", "fin")])
POW = bases(*[(u, 1) for u in ("mem", "var0", "var1", "mix0", "xa0", "ffn0", "mix1", "xa1", "ffn1", "fin")])
RBS = bases(*[(u, 1) for u in ("mem", "mix0", "xa0", "ffn0", "mix1", "xa1", "ffn1")])
SQ = bases(*[(u, 4) for u in POW])


def build(nc, w, xt, memt, vecs, cst, wki, wwi, dft, rpb, out):
    ctx = ExitStack()
    with ctx:
        def sb(name, shape, dt=F32):
            return ctx.enter_context(nc.sbuf_tensor(name, shape, dt))

        def sem(name):
            return ctx.enter_context(nc.semaphore(name))

        raw = sb("raw", [P, RAW_SLOTS, KT, CW])
        wh = sb("wh", [P, 2, KT, CW], F32R)
        wl = sb("wl", [P, 2, KT, CW], F32R)
        h = sb("h", [P, KT, S])
        xh = sb("xh", [P, KT, S], F32R)
        xl = sb("xl", [P, KT, S], F32R)
        yh = sb("yh", [P, 2 * KT, S], F32R)
        yl = sb("yl", [P, 2 * KT, S], F32R)
        qz = sb("qz", [P, NH, S])
        kt = sb("kt", [P, KT, S])
        v = sb("v", [P, 2, D])
        gt = sb("gt", [P, KT, S])
        work = sb("work", [P, 12 * 512])
        cs = sb("cs", [P, NCST])
        vec = sb("vec", [P, NVEC])
        ones = sb("ones", [P, P])
        half = sb("half", [P, 2])
        acc = sb("acc", [P, 2, S])
        rb = sb("rb", [P, S])
        rb_m = sb("rb_m", [P, S])
        rt_m = sb("rt_m", [P, 2])
        diag = sb("diag", [P, 2, P])
        stat = sb("stat", [P, 2])
        rt = sb("rt", [P, 2])
        wi = sb("wi", [P, 2, IH])
        top8 = sb("top8", [P, 2, 8])
        nmax = sb("nmax", [P, 28, 2])
        esum = sb("esum", [P, 28, 2])
        erec = sb("erec", [P, 28, 2])
        bank = [ctx.enter_context(nc.psum_tensor(f"bank{i}", [P, 512], F32)) for i in range(8)]
        k_scratch = nc.dram_tensor("k_scratch", [2, P, KT * S], F32, kind="Internal").ap()
        m_scratch = nc.dram_tensor("m_scratch", [2, P, KT * S], F32, kind="Internal").ap()

        def wk(i):
            return work[:, 512 * i:512 * i + 512]

        def wk3(i):
            return wk(i).rearrange("p (a b) -> p a b", a=2)

        def c_(name):
            a, b = CST[name]
            return cs[:, a:b]

        def vc(name, j):
            return vec[:, VEC[name] + j:VEC[name] + j + 1]

        def b3(i):
            return bank[i][:, :].rearrange("p (a b) -> p a b", a=2)

        ident, cosT, sinT = c_("ident"), c_("cos"), c_("sin")
        adm = c_("adm").rearrange("p (a b) -> p a b", a=2)
        qiz = gt
        ki = work[:, 11 * 512:11 * 512 + 256]
        kiw = v[:, :, :].rearrange("p a b -> p (a b)")[:, 0:KT * P].rearrange("p (k n) -> p k n", k=KT)
        wiw = v[:, :, :].rearrange("p a b -> p (a b)")[:, KT * P:KT * P + KT * IH].rearrange("p (k n) -> p k n", k=KT)
        nabias = qz[:, 4:12, :].rearrange("p (h t) s -> p h t s", t=2)
        u_tok = qz[:, 12:16, :].rearrange("p a b -> p (a b)").rearrange("p (t n) -> p t n", t=2)
        gflat = gt[:, :, :].rearrange("p a b -> p (a b)")
        dft_s = gflat[:, 0:1024].rearrange("p (t n) -> p t n", t=2)
        dft_c = gflat[:, 1024:1280]
        m_raw = gt
        score, selneg = wk3(8), wk3(9)
        cpad = [work[:, 516 * i:516 * i + 516].rearrange("p (a b) -> p a b", a=2) for i in range(2)]

        raw_full = [sem(f"raw_full{i}") for i in range(RAW_SLOTS)]
        const_in, x_in, kiw_in = sem("const_in"), sem("x_in"), sem("kiw_in")
        mem_in, m_saved, m_back = sem("mem_in"), sem("m_saved"), sem("m_back")
        k_saved, k_back = sem("k_saved"), sem("k_back")
        rpb_in, dft_in, stored = sem("rpb_in"), sem("dft_in"), sem("stored")
        hi_ready, lo_ready = sem("hi_ready"), sem("lo_ready")
        w_used = sem("w_used")
        act_evac, dve_evac = sem("act_evac"), sem("dve_evac")
        evac = {"act": act_evac, "dve": dve_evac}
        filled = sem("filled")
        ki_full, wi_full, wi_ready = sem("ki_full"), sem("wi_full"), sem("wi_ready")
        rope_rot, rope_cos, rope_done = sem("rope_rot"), sem("rope_cos"), sem("rope_done")
        is_full, rel_ready, is_added = sem("is_full"), sem("rel_ready"), sem("is_added")
        picked = sem("picked")
        x_hi, x_lo = sem("x_hi"), sem("x_lo")
        sq_ready, acc_done = sem("sq_ready"), sem("acc_done")
        st_full, st_read, st_pow, st_diag = sem("st_full"), sem("st_read"), sem("st_pow"), sem("st_diag")
        bc_full, rb_ready = sem("bc_full"), sem("rb_ready")
        s_full, s_read, e_done, p_ready = sem("s_full"), sem("s_read"), sem("e_done"), sem("p_ready")
        t_full, t_evac, o_full = sem("t_full"), sem("t_evac"), sem("o_full")
        y_hi, g_lo = sem("y_hi"), sem("g_lo")
        z_full, z_abs, z_ln, z_sp = sem("z_full"), sem("z_abs"), sem("z_ln"), sem("z_sp")
        z_masked, z_neg, c_full, z_arg, z_prob = sem("z_masked"), sem("z_neg"), sem("c_full"), sem("z_arg"), sem("z_prob")
        f_full, f_copied = sem("f_full"), sem("f_copied")
        ln_c, ln_g, ln_h = sem("ln_c"), sem("ln_g"), sem("ln_h")
        gate_in, centre_ready, cv_ready, ge_ready, pf_ready = sem("gate_in"), sem("centre_ready"), sem("cv_ready"), sem("ge_ready"), sem("pf_ready")
        m_hi, m_lo = sem("m_hi"), sem("m_lo")
        bias_ready, zero_ready, padded = sem("bias_ready"), sem("zero_ready"), sem("padded")
        chain_act, chain_dve, chain_pool = sem("chain_act"), sem("chain_dve"), sem("chain_pool")
        fin_ready = sem("fin_ready")

        class Chain:
            def __init__(self, eng, s):
                self.eng, self.s, self.n = eng, s, 0

            def __call__(self, ins):
                self.n += 1
                ins.then_inc(self.s, 1)
                self.eng.wait_ge(self.s, self.n)

        block = ctx.enter_context(nc.Block())

        @block.sync
        def _(sp):
            def load(n, slot):
                sp.dma_start(raw[:, slot, :, :], w[n]).then_inc(raw_full[slot], 16)

            sp.dma_start(h[:, :, :], xt).then_inc(x_in, 16)
            load(0, 0)
            load(1, 1)
            sp.dma_start(kiw, wki).then_inc(kiw_in, 16)
            sp.dma_start(wiw, wwi).then_inc(kiw_in, 16)
            load(2, 2)
            sp.dma_start(cs[:, :], cst).then_inc(const_in, 16)
            sp.dma_start(vec[:, :], vecs).then_inc(const_in, 16)
            load(3, 3)
            rest = NCHUNK - RAW_SLOTS
            with sp.Fori(1, 1 + rest // RAW_SLOTS) as i:
                for c in range(RAW_SLOTS):
                    sp.wait_ge(lo_ready, 2 * RAW_SLOTS * i - 2 * RAW_SLOTS + 2 * c + 2)
                    sp.dma_start(raw[:, c, :, :],
                                 w[bass.ds(RAW_SLOTS * i + c, 1)].rearrange("o p k n -> (o p) k n")
                                 ).then_inc(raw_full[c], 16)
            for n in range(NCHUNK - rest % RAW_SLOTS, NCHUNK):
                sp.wait_ge(lo_ready, 2 * (n - RAW_SLOTS) + 2)
                load(n, n % RAW_SLOTS)
            for c in range(4):
                sp.wait_ge(fin_ready, 2 * c + 2)
                sp.dma_start(out[:, 2 * c:2 * c + 2, :], gt[:, 2 * c:2 * c + 2, :]).then_inc(stored, 16)
            sp.wait_ge(stored, 64)
            sp.wait_ge(m_saved, 32)
            sp.wait_ge(k_saved, 32)

        @block.tensor
        def _(pe):
            def enter(p):
                if p.before is not None:
                    pe.wait_ge(evac[p.before.reader], p.before.end)

            def project(name, oh, ol, ready, tok=False, hooks={}, tile0=0):
                p = PH[name]
                enter(p)
                per = 2 * p.deep

                def round_(i, first, hooks=hooks):
                    for c in range(per):
                        n = per * i + (p.n0 + c)
                        slot = (p.n0 + c) % 2
                        b = b3(p.pair + c // p.deep)
                        k0 = (c % p.deep) * KT
                        if c % p.deep == 0 and not first:
                            pe.wait_ge(evac[p.reader], 2 * i + (p.base + c // p.deep - 1))
                        for j in range(2):
                            if tok and j == 0:
                                pe.wait_ge(lo_ready, 2 * n + 2)
                            if not tok:
                                pe.wait_ge(lo_ready, 2 * n + (j + 1))
                            for k in range(KT):
                                if j == 0 and c < p.deep and ready(k0 + k):
                                    pe.wait_ge(*ready(k0 + k))
                                kk, part = tile0 + k0 + k, slice(j * P, j * P + P)
                                if tok:
                                    ops = (oh[:, kk, part], ol[:, kk, part], wh[:, slot, k, :], wl[:, slot, k, :])
                                else:
                                    ops = (wh[:, slot, k, part], wl[:, slot, k, part], oh[:, kk, :], ol[:, kk, :])
                                mm = split_product(b[:, j, :], *ops, k0 + k == 0 and (p.deep == 1 or j == 0),
                                                   k0 + k == KT * p.deep - 1, p.deep > 1)
                                if hooks and k < KT - 1 and (per * i + c, j, k) in hooks:
                                    hooks[per * i + c, j, k]()
                            if not tok:
                                mm.then_inc(w_used, 1)
                            elif j == 1:
                                mm.then_inc(w_used, 2)
                            if hooks and (per * i + c, j, KT - 1) in hooks:
                                hooks[per * i + c, j, KT - 1]()

                rounds = p.n // per
                if hooks or p.base < 2:
                    once = rounds if rounds < 3 else 1
                    for i in range(once):
                        round_(i, i == 0)
                    if once < rounds:
                        with pe.Fori(once, rounds) as i:
                            round_(i, False, {})
                elif rounds == 1:
                    round_(0, True)
                else:
                    with pe.Fori(0, rounds) as i:
                        round_(i, False)

            def split_product(o, ah, al, bh, bl, start, stop, skip):
                pe.matmul(o, ah, bh, start=start, stop=False, skip_group_check=skip)
                pe.matmul(o, ah, bl, start=False, stop=False, skip_group_check=skip)
                return pe.matmul(o, al, bh, start=False, stop=stop, skip_group_check=skip)

            def stats(name):
                pe.wait_ge(acc_done, 3 * STAT[name] + 3)
                for t in range(2):
                    for e in range(2):
                        mm = pe.matmul(bank[4][:, t:t + 1], acc[:, e, t * P:t * P + P], ones[:, 0:1],
                                       start=(e == 0), stop=(e == 1))
                mm.then_inc(st_full, 1)

            def bcast(name):
                pe.wait_ge(st_diag, 2 * STAT[name] + 2)
                pe.matmul(bank[5][:, 0:S], ones[:, :], diag[:, :, :].rearrange("p a b -> p (a b)"),
                          start=True, stop=True).then_inc(bc_full, 1)

            def x_ready(use):
                return lambda k: (x_lo, XBASE[use] + k // 2 + 1) if k % 2 == 0 else None

            nothing = lambda k: None

            def soft_attention(name, heads, score_ops, value_ops, group, p):
                u0 = UBASE[name]
                enter(p)

                def scores(a):
                    u = u0 + a
                    if a >= 2:
                        pe.wait_ge(s_read, 2 * (u - 1))
                    for t in range(2):
                        ops = score_ops(a, t)
                        for j, (l, r) in enumerate(ops):
                            mm = pe.matmul(b3(4 + a % 2)[:, t, :], l, r, start=(j == 0), stop=(j == len(ops) - 1))
                    mm.then_inc(s_full, 1)

                def turn(a):
                    u = u0 + a
                    pe.wait_ge(p_ready, 2 * u + 2)
                    if a >= 2:
                        pe.wait_ge(t_evac, u - 1)
                    pr = wk3((2, 3, 6)[a % 3])
                    for s in range(2):
                        for t in range(2):
                            mm = pe.transpose(b3(6 + a % 2)[:, s, t * P:t * P + P], pr[:, t, s * P:s * P + P], ident)
                    mm.then_inc(t_full, 1)

                def values(a):
                    u = u0 + a
                    pe.wait_ge(t_evac, u + 1)
                    g = a // group
                    if a % group == 0 and g >= 2:
                        pe.wait_ge(dve_evac, p.base + g - 1)
                    for o, sl in value_ops(a, p.pair + g % 2):
                        for s in range(2):
                            mm = pe.matmul(o, v[:, s, sl], wk3(4 + a % 2)[:, s, :], start=(s == 0), stop=(s == 1))
                    mm.then_inc(o_full, 1)

                for t in range(heads + 3):
                    if t < heads:
                        scores(t)
                    if 2 <= t < heads + 2:
                        turn(t - 2)
                    if t >= 3:
                        values(t - 3)

            def norm_hooks(name):
                return {(0, 0, 7): lambda: stats(name), (0, 1, 7): lambda: bcast(name)}

            def layer_norm_hooks(l):
                return {(0, 0, 5): lambda: stats("mean" + l), (0, 1, 3): lambda: bcast("mean" + l),
                        (2, 0, 0): lambda: stats("var" + l), (2, 1, 0): lambda: bcast("var" + l)}

            project("qi", xh, xl, x_ready("first"))
            pe.wait_ge(kiw_in, 32)
            for k in range(KT):
                mm = pe.matmul(bank[PH["ki"].pair][:, 0:S], kiw[:, k, :], h[:, k, :], start=(k == 0), stop=(k == KT - 1))
            mm.then_inc(ki_full, 1)
            for t in range(2):
                for k in range(KT):
                    mm = pe.matmul(bank[4][:, 8 * t:8 * t + IH], h[:, k, t * P:t * P + P], wiw[:, k, :],
                                   start=(k == 0), stop=(k == KT - 1))
            mm.then_inc(wi_full, 1)
            project("qa", xh, xl, nothing)
            pe.wait_ge(rope_done, 3)
            pe.wait_ge(wi_ready, 1)
            for a in range(IH):
                if a >= 2:
                    pe.wait_ge(rel_ready, a - 1)
                for t in range(2):
                    mm = pe.matmul(b3(4 + a % 2)[:, t, :], qiz[:, a, t * P:t * P + P], ki, start=True, stop=True)
                mm.then_inc(is_full, 1)
            project("ka", xh, xl, nothing)
            project("va", xh, xl, nothing, tok=True)
            pe.wait_ge(rel_ready, IH)
            pe.wait_ge(filled, 2)
            project("ga", xh, xl, nothing, hooks={(0, 0, 7): lambda: stats("mem"), (1, 0, 7): lambda: bcast("mem")})

            pe.wait_ge(rb_ready, RBS["mem"] + 1)
            pe.wait_ge(rope_done, 11)
            pe.wait_ge(act_evac, PH["va"].end)
            soft_attention("A", NH, lambda a, t: [(qz[:, a, t * P:t * P + P], kt[:, a // 2, :])],
                           lambda a, b: [(bank[b][HD * (a % 2):HD * (a % 2) + HD, 0:S], slice(HD * a, HD * a + HD))],
                           2, PH["attA"])
            project("oa", yh, yl, lambda k: (g_lo, GBASE["A"] + k + 1))
            project("kx0", yh, yl, lambda k: (m_lo, k // 2 + 1) if k % 2 == 0 else None, tile0=KT,
                    hooks=layer_norm_hooks("0"))
            project("qb", xh, xl, x_ready("B"))
            project("kb", xh, xl, nothing)
            project("vb", xh, xl, nothing, tok=True)
            project("gb", xh, xl, nothing)

            pe.wait_ge(act_evac, PH["vb"].end)
            pb = PH["attB"]
            enter(pb)
            tri = c_("tri")
            LATE = slice(P, S)

            def z_scores(a):
                if a >= 2:
                    pe.wait_ge(z_neg, a - 1)
                b = bank[4 + a % 2]
                pe.matmul(b[:, 0:S], kt[:, a // 2, 0:P], qz[:, a, :], start=True, stop=True)
                pe.matmul(b[:, S:S + P], kt[:, a // 2, LATE], qz[:, a, LATE], start=True, stop=True).then_inc(z_full, 1)

            def z_sums(a):
                pe.wait_ge(z_masked, a + 1)
                if a >= 2:
                    pe.wait_ge(z_arg, a - 1)
                b, sp_ = bank[6 + a % 2], wk(4 + a % 2)
                pe.matmul(b[:, 0:P], tri, sp_[:, 0:P], start=True, stop=True)
                pe.matmul(b[:, P:S], tri, sp_[:, P:S], start=True, stop=False)
                pe.matmul(b[:, P:S], ones[:, :], sp_[:, S:S + P], start=False, stop=True)
                pe.matmul(b[:, S:S + P], tri, sp_[:, S:S + P], start=True, stop=True).then_inc(c_full, 1)

            def z_values(a):
                pe.wait_ge(z_prob, a + 1)
                g = a // 2
                if a % 2 == 0 and g >= 2:
                    pe.wait_ge(dve_evac, pb.base + g - 1)
                r = slice(HD * (a % 2), HD * (a % 2) + HD)
                b, pr, cols = bank[pb.pair + g % 2], wk(8 + a % 2), slice(HD * a, HD * a + HD)
                pe.matmul(b[r, 0:P], v[:, 0, cols], pr[:, 0:P], start=True, stop=True)
                pe.matmul(b[r, P:S], v[:, 0, cols], pr[:, P:S], start=True, stop=False)
                pe.matmul(b[r, P:S], v[:, 1, cols], pr[:, S:S + P], start=False, stop=True).then_inc(o_full, 1)

            for t in range(NH + 4):
                if t < NH:
                    z_scores(t)
                if 2 <= t < NH + 2:
                    z_sums(t - 2)
                if t >= 4:
                    z_values(t - 4)
            project("ob", yh, yl, lambda k: (g_lo, GBASE["B"] + k + 1))
            project("kx1", yh, yl, nothing, tile0=KT, hooks=layer_norm_hooks("1"))

            project("zf", xh, xl, x_ready("mix0"), tok=True, hooks=norm_hooks("mix0"))
            project("qn", xh, xl, nothing)
            project("kn", xh, xl, nothing)
            project("vn", xh, xl, nothing, tok=True)
            pe.wait_ge(act_evac, PH["zf"].end)
            pe.wait_ge(dft_in, 32)
            pf = PH["fourier"]
            enter(pf)

            def f_tokens(g):
                if g >= 2:
                    pe.wait_ge(f_copied, g - 1)
                for t in range(2):
                    mm = pe.matmul(bank[6 + g % 2][:, :], u_tok[:, t, g * P:g * P + P], dft_s[:, t, :],
                                   start=(t == 0), stop=(t == 1))
                mm.then_inc(f_full, 1)

            def f_channels(g):
                pe.wait_ge(f_copied, g + 1)
                if g >= 2:
                    pe.wait_ge(dve_evac, pf.base + g - 1)
                b = bank[pf.pair + g % 2]
                pe.matmul(b[:, 0:S], dft_c[:, 0:P], wk(g % 2)[:, 0:S], start=True, stop=False)
                pe.matmul(b[:, 0:S], dft_c[:, P:S], wk(g % 2)[:, S:2 * S], start=False, stop=True).then_inc(o_full, 1)

            for g in range(5):
                if g < 4:
                    f_tokens(g)
                if g >= 1:
                    f_channels(g - 1)
            pe.wait_ge(dve_evac, PH["kn"].end)
            pe.wait_ge(act_evac, PH["vn"].end)
            pn = PH["attN"]
            soft_attention("N", 4, lambda a, t: [(qz[:, a, t * P:t * P + P], kt[:, a, :])],
                           lambda a, b: [(bank[b][:, 0:S], slice(P * a, P * a + P))], 1, pn)
            project("oab", yh, yl, lambda k: (dve_evac, (pf.base + k if k < 4 else pn.base + k - 4) + 1))

            for l in "01":
                if l == "1":
                    project("cb", xh, xl, x_ready("mix1"), hooks=norm_hooks("mix1"))
                    project("cc", xh, xl, nothing)
                    project("cu", xh, xl, nothing)
                    pe.wait_ge(m_back, 32)
                project("vx" + l, yh, yl, nothing, tok=True, tile0=KT)
                if l == "1":
                    project("oc", yh, yl, lambda k: (g_lo, GBASE["conv"] + k // 2 + 1) if k % 2 == 0 else None)
                project("qx" + l, xh, xl, x_ready("xa" + l), hooks=norm_hooks("xa" + l))
                pe.wait_ge(k_back, 16 * int(l) + 16)
                pe.wait_ge(act_evac, PH["vx" + l].end)
                pe.wait_ge(dve_evac, PH["qx" + l].end)
                pa = PH["attX" + l]
                soft_attention("X" + l, 4,
                               lambda a, t: [(qz[:, 2 * a + j, t * P:t * P + P], kt[:, 2 * a + j, :]) for j in range(2)],
                               lambda a, b: [(b3(b)[:, j, :], slice(CW * a + P * j, CW * a + P * j + P)) for j in range(2)],
                               1, pa)
                project("ox" + l, yh, yl,
                        lambda k, pa=pa: (dve_evac, pa.base + k // 2 + 1) if k % 2 == 0 else None)
                project("fu" + l, xh, xl, x_ready("ffn" + l), hooks=norm_hooks("ffn" + l))
                project("fg" + l, xh, xl, nothing)
                project("fd" + l, yh, yl,
                        lambda k, l=l: (g_lo, GBASE["ffn" + l] + k // 2 + 1) if k % 2 == 0 else None)
            stats("fin")
            bcast("fin")

        @block.scalar
        def _(act):
            chain = Chain(act, chain_act)

            def hi(h_):
                if h_ >= 2 * NCHUNK:
                    return
                n, j = divmod(h_, 2)
                if j == 0:
                    act.wait_ge(raw_full[n % RAW_SLOTS], 16 * (n // RAW_SLOTS + 1))
                if h_ >= 4:
                    act.wait_ge(w_used, h_ - 3)
                part = slice(j * P, j * P + P)
                act.activation(wh[:, n % 2, :, part], raw[:, n % RAW_SLOTS, :, part], ACT.Copy).then_inc(hi_ready, 1)

            def chunks(name, evacuate=None, split=0):
                p = PH[name]
                for c in range(p.n):
                    n = p.n0 + c
                    for j in range(2):
                        if 2 * c + j >= split:
                            hi(2 * n + 3 + j)
                    if c % p.deep == p.deep - 1 and evacuate is not None:
                        if p.reader == "act":
                            act.wait_ge(w_used, 2 * n + 2)
                        evacuate(c // p.deep, b3(p.pair + c // p.deep % 2))

            def rope_raw(r, src, width):
                if r >= 2:
                    act.wait_ge(rope_done, r - 1)
                act.activation(wk(r % 2)[:, 0:width], src, ACT.Copy).then_inc(act_evac, 1)

            def flat(b):
                return b.rearrange("p a b -> p (a b)")

            def square(stat, c, src):
                i = 3 * STAT[stat]
                if i + (1 if c >= 2 else 0) > 0:
                    act.wait_ge(acc_done, i + (1 if c >= 2 else 0))
                act.activation(wk3(10 + c % 2), src, ACT.Square).then_inc(sq_ready, 1)

            def x_high(c, gain):
                for j in range(2):
                    m = 2 * c + j
                    if gain is None:
                        ins = act.activation(xh[:, m, :], h[:, m, :], ACT.Copy)
                    else:
                        ins = act.activation(xh[:, m, :], h[:, m, :], ACT.Copy, scale=vc(gain, m))
                ins.then_inc(x_hi, 1)

            def residual(name, stat, gain, split=0):
                p = PH[name]
                for c in range(p.n):
                    n = p.n0 + c
                    for j in range(2):
                        if 2 * c + j >= split:
                            hi(2 * n + 3 + j)
                    if c % p.deep == p.deep - 1:
                        o = c // p.deep
                        act.wait_ge(dve_evac, p.base + o + 1)
                        if gain is not None:
                            x_high(o, gain)
                        square(stat, o, h[:, 2 * o:2 * o + 2, :])

            def spread(name, dst=rb):
                act.wait_ge(bc_full, STAT[name] + 1)
                act.activation(dst[:, :], bank[5][:, 0:S], ACT.Copy).then_inc(rb_ready, 1)

            def y_high(key, i, dst, src, s_, value):
                act.wait_ge(s_, value)
                act.activation(dst, src, ACT.Copy).then_inc(y_hi, 1)

            def soft_attention(name, heads, p, high, lag):
                u0, ob = UBASE[name], OBASE[name]
                for t in range(heads + lag):
                    if t < heads:
                        u = u0 + t
                        if t >= 3:
                            act.wait_ge(t_full, u - 2)
                        for q in range(2):
                            act.wait_ge(s_read, 2 * u + q + 1)
                            act.activation(wk3((2, 3, 6)[t % 3])[:, q, :], wk3(t % 2)[:, q, :], ACT.Exp,
                                           bias=nmax[:, u, q:q + 1], scale=-1.0,
                                           accum_out=esum[:, u, q:q + 1]).then_inc(e_done, 1)
                    if 2 <= t < heads + 2:
                        a = t - 2
                        u = u0 + a
                        act.wait_ge(t_full, u + 1)
                        if a >= 2:
                            act.wait_ge(o_full, ob + a - 1)
                        act.activation(wk(4 + a % 2), bank[6 + a % 2][:, :], ACT.Copy).then_inc(t_evac, 1)
                    high(t)

            def gated_high(key, p, t, lag):
                if t >= lag and (t - lag) % 2 == 0 and (t - lag) // 2 < 8:
                    g = (t - lag) // 2
                    act.wait_ge(dve_evac, p.base + g + 1)
                    act.activation(yh[:, g, :], wk(10 + g % 2)[:, 0:S], ACT.Copy).then_inc(y_hi, 1)

            act.wait_ge(x_in, 16)
            for c in range(4):
                x_high(c, None)
            for h_ in range(3):
                hi(h_)
            chunks("qi", lambda c, b: rope_raw(c, flat(b), 2 * S))
            act.wait_ge(ki_full, 1)
            rope_raw(2, bank[PH["ki"].pair][:, 0:S], S)
            chunks("qa", lambda c, b: rope_raw(3 + c, flat(b), 2 * S))
            for a in range(IH):
                act.wait_ge(is_full, a + 1)
                if a >= 2:
                    act.wait_ge(is_added, 2 * a - 2)
                act.activation(wk(6 + a % 2), bank[4 + a % 2][:, :], ACT.Relu, scale=HD ** -0.5).then_inc(rel_ready, 1)
            act.wait_ge(is_full, IH)
            act.dma_start(m_raw[:, :, :].rearrange("p k s -> p (k s)"), memt).then_inc(mem_in, 16)

            def ka(c, b):
                rope_raw(7 + c, flat(b), 2 * S)
                if c == 3:
                    act.wait_ge(mem_in, 16)
                    for q in range(2):
                        square("mem", q, m_raw[:, 2 * q:2 * q + 2, :])

            chunks("ka", ka)

            def v_copy(c, b):
                act.activation(v[:, :, CW * c:CW * c + CW], b, ACT.Copy).then_inc(act_evac, 1)

            def k_copy(c, b):
                act.activation(kt[:, 2 * c:2 * c + 2, :], b, ACT.Copy).then_inc(act_evac, 1)

            def gate(c, b):
                act.activation(gt[:, 2 * c:2 * c + 2, :], b, ACT.Silu).then_inc(act_evac, 1)

            def va(c, b):
                v_copy(c, b)
                for m in (2 * c, 2 * c + 1):
                    ins = act.activation(yh[:, KT + m, :], m_raw[:, m, :], ACT.Copy, scale=vc("mem", m))
                ins.then_inc(m_hi, 1)
                if c < 2:
                    square("mem", 2 + c, m_raw[:, 4 + 2 * c:6 + 2 * c, :])

            def ga(c, b):
                act.wait_ge(m_lo, c + 1)
                gate(c, b)
                if c == 2:
                    spread("mem", rb_m)

            chunks("va", va)
            act.wait_ge(sq_ready, SQ["mem"] + 4)
            chunks("ga", ga)
            soft_attention("A", NH, PH["attA"], lambda t: gated_high("A", PH["attA"], t, 5), 5)
            act.wait_ge(m_lo, 4)
            act.dma_start(m_scratch[0], yh[:, KT:, :].bitcast(F32).rearrange("p k s -> p (k s)")).then_inc(m_saved, 16)
            act.dma_start(m_scratch[1], yl[:, KT:, :].bitcast(F32).rearrange("p k s -> p (k s)")).then_inc(m_saved, 16)
            chunks("oa")

            def layer_norm(l, filler, gain, stat):
                p = PH[filler]
                for c in range(p.n):
                    n = p.n0 + c
                    if c < 3:
                        hi(2 * n + 3)
                    hi(2 * n + 4)
                    if c == 0:
                        centred(l)
                    if c == 2:
                        shifted(l, range(0, 4), gain, stat)
                        hi(2 * n + 5)
                        shifted(l, range(4, 8), gain, stat)

            def centred(l):
                for c in range(4):
                    act.wait_ge(ln_c, 4 * int(l) + c + 1)
                    square("var" + l, c, h[:, 2 * c:2 * c + 2, :])

            def shifted(l, tiles, gain, stat):
                i = int(l)
                for m in tiles:
                    act.wait_ge(ln_g, 8 * i + m + 1)
                    act.activation(h[:, m, :], h[:, m, :], ACT.Identity, bias=vc("ln_b" + l, m)).then_inc(ln_h, 1)
                    if m % 2:
                        act.wait_ge(ln_h, 8 * i + m + 1)
                        x_high(m // 2, gain)
                        if stat is not None:
                            square(stat, m // 2, h[:, m - 1:m + 1, :])

            layer_norm("0", "kx0", None, None)
            act.wait_ge(dve_evac, PH["kx0"].end)
            act.dma_start(k_scratch[0], kt[:, :, :].rearrange("p k s -> p (k s)")).then_inc(k_saved, 16)

            def q_scaled(c, b):
                act.activation(qz[0:HD, 4 * c:4 * c + 4:2, :], b[0:HD], ACT.Copy, scale=HD ** -0.5)
                act.activation(qz[HD:P, 4 * c + 1:4 * c + 4:2, :], b[HD:P], ACT.Copy, scale=HD ** -0.5).then_inc(act_evac, 1)

            chunks("qb", q_scaled)
            act.wait_ge(k_saved, 16)
            chunks("kb", k_copy)
            chunks("vb", v_copy)
            chunks("gb", gate)

            ZW = S + P
            pb = PH["attB"]
            act.preload_act_table_set("natural_log_exp_and_others")
            for t in range(NH + 5):
                if t < NH:
                    z = wk(t % 2)[:, 0:ZW]
                    act.wait_ge(z_full, t + 1)
                    if t >= 2:
                        act.wait_ge(z_sp, t - 1)
                    act.activation(z, bank[4 + t % 2][:, 0:ZW], ACT.Abs).then_inc(z_abs, 1)
                    act.wait_ge(z_abs, t + 1)
                    chain(act.activation(z, z, ACT.Exp, scale=-1.0))
                    act.activation(z, z, ACT.Ln, bias=1.0).then_inc(z_ln, 1)
                if 3 <= t < NH + 3:
                    a = t - 3
                    pr = wk(8 + a % 2)[:, 0:ZW]
                    act.wait_ge(z_arg, a + 1)
                    act.activation(pr, pr, ACT.Exp).then_inc(z_prob, 1)
                gated_high("B", pb, t, 6)

            act.wait_ge(o_full, OBASE["B"] + NH)
            act.dma_start(nabias.rearrange("p h t s -> p (h t s)"), rpb).then_inc(rpb_in, 16)
            act.dma_start(gflat[:, 0:1024], dft[:, 0:1024]).then_inc(dft_in, 16)
            act.dma_start(gflat[:, 1024:1280], dft[:, 1024:1280]).then_inc(dft_in, 16)
            chunks("ob")
            layer_norm("1", "kx1", "mix0", "mix0")
            act.wait_ge(dve_evac, PH["kx1"].end)
            act.dma_start(k_scratch[1], kt[:, :, :].rearrange("p k s -> p (k s)")).then_inc(k_saved, 16)

            def scaled_tokens(dst):
                def f(c, b):
                    act.wait_ge(st_pow, POW["mix0"] + 1)
                    for t in range(2):
                        ins = act.activation(dst[:, t, CW * c:CW * c + CW], b[:, t, :], ACT.Copy, scale=rt[:, t:t + 1])
                    ins.then_inc(act_evac, 1)
                return f

            def memory_values(c, b):
                for t in range(2):
                    ins = act.activation(v[:, t, CW * c:CW * c + CW], b[:, t, :], ACT.Copy, scale=rt_m[:, t:t + 1])
                ins.then_inc(act_evac, 1)

            chunks("zf", scaled_tokens(u_tok))
            spread("mix0")
            chunks("qn")
            chunks("kn")
            chunks("vn", scaled_tokens(v))
            pf = PH["fourier"]
            for g in range(5):
                if g < 4:
                    act.wait_ge(f_full, g + 1)
                    if g >= 2:
                        act.wait_ge(o_full, OBASE["F"] + g - 1)
                    act.activation(wk(g % 2), bank[6 + g % 2][:, :], ACT.Copy).then_inc(f_copied, 1)
                if g >= 1:
                    a = g - 1
                    y_high("F", a, yh[:, a, :], bank[pf.pair + a % 2][:, 0:S], o_full, OBASE["F"] + a + 1)

            def plain_high(name, heads, tiles, first):
                p = PH["att" + name]

                def f(t):
                    if t >= 4:
                        a = t - 4
                        act.wait_ge(o_full, OBASE[name] + a + 1)
                        act.activation(yh[:, first + tiles * a:first + tiles * a + tiles, :],
                                       b3(p.pair + a % 2)[:, 0:tiles, :], ACT.Copy).then_inc(y_hi, 1)
                return f

            soft_attention("N", 4, PH["attN"], plain_high("N", 4, 1, 4), 4)
            act.dma_start(kt[:, :, :].rearrange("p k s -> p (k s)"), k_scratch[0]).then_inc(k_back, 16)
            residual("oab", "xa0", "xa0")

            def products(key, name, l=None):
                p = PH[name]
                taps, tiles = ("fconv" + l, 16) if l else ("conv_c", 8)

                def centre(c):
                    cv, cp = wk3(3 + c % 2), cpad[c % 2]
                    if l:
                        act.wait_ge(dve_evac, p.base + c + 1)
                    else:
                        act.wait_ge(gate_in, c + 1)
                        if c >= 2:
                            act.wait_ge(pf_ready, CBASE[key] + c - 1)
                    for j in range(2):
                        m = 2 * c + j
                        if l:
                            ins = act.activation(cv[:, j, :], cp[:, j, 1:S + 1], ACT.Identity, scale=vc(taps, tiles + m),
                                                 bias=vc("fbias" + l, m))
                        else:
                            ins = act.activation(cv[:, j, :], cp[:, j, 1:S + 1], ACT.Copy, scale=vc(taps, tiles + m))
                    ins.then_inc(centre_ready, 1)

                def gelu(c):
                    if not l:
                        return
                    act.wait_ge(cv_ready, CBASE[key] + c + 1)
                    if c >= 2:
                        act.wait_ge(pf_ready, CBASE[key] + c - 1)
                    act.activation(wk(5 + c % 2), wk(3 + c % 2), ACT.Gelu).then_inc(ge_ready, 1)

                def high(c):
                    act.wait_ge(pf_ready, CBASE[key] + c + 1)
                    act.activation(yh[:, 2 * c:2 * c + 2, :], wk3(7 + c % 2), ACT.Copy).then_inc(y_hi, 1)

                for c in range(p.n + 1):
                    n = p.n0 + c
                    hi(2 * n + 3)
                    if c == p.n and not l:
                        hi(2 * n + 4)
                    if c >= 1:
                        centre(c - 1)
                    if c < p.n:
                        hi(2 * n + 4)
                    if c >= 1:
                        gelu(c - 1)
                    if c >= 2:
                        high(c - 2)
                    if c == p.n:
                        hi(2 * n + (4 if l else 5))
                high(p.n - 1)

            for l in "01":
                if l == "1":
                    fd = PH["fd0"]
                    act.wait_ge(w_used, 2 * (fd.n0 + fd.n))
                    act.wait_ge(m_saved, 32)
                    act.dma_start(yh[:, KT:, :].bitcast(F32).rearrange("p k s -> p (k s)"), m_scratch[0]).then_inc(m_back, 16)
                    act.dma_start(yl[:, KT:, :].bitcast(F32).rearrange("p k s -> p (k s)"), m_scratch[1]).then_inc(m_back, 16)
                    spread("mix1")
                    chunks("cb")
                    chunks("cc")
                    products("conv", "cu")
                    act.wait_ge(gate_in, 4)
                    act.dma_start(kt[:, :, :].rearrange("p k s -> p (k s)"), k_scratch[1]).then_inc(k_back, 16)
                    chunks("vx1", memory_values, split=3)
                    residual("oc", "xa1", "xa1")
                else:
                    chunks("vx0", memory_values)
                spread("xa" + l)
                chunks("qx" + l)
                soft_attention("X" + l, 4, PH["attX" + l], plain_high("X" + l, 4, 2, 0), 4)
                residual("ox" + l, "ffn" + l, "ffn" + l)
                spread("ffn" + l)
                chunks("fu" + l)
                products("ffn" + l, "fg" + l, l)
                if l == "0":
                    residual("fd0", "mix1", "mix1", split=2)
                else:
                    residual("fd1", "fin", None, split=2)

        @block.vector
        def _(dve):
            chain = Chain(dve, chain_dve)

            def both(*instructions):
                for ins in instructions:
                    chain.n += 1
                    ins.then_inc(chain_dve, 1)
                dve.wait_ge(chain_dve, chain.n)

            def lo(h_):
                if h_ >= 2 * NCHUNK:
                    return
                n, j = divmod(h_, 2)
                dve.wait_ge(hi_ready, h_ + 1)
                part = slice(j * P, j * P + P)
                dve.tensor_tensor(wl[:, n % 2, :, part], raw[:, n % RAW_SLOTS, :, part],
                                  wh[:, n % 2, :, part].bitcast(F32), ALU.subtract).then_inc(lo_ready, 1)

            def chunks(name, evacuate=None, between=None, split=0):
                p = PH[name]
                for c in range(p.n):
                    n = p.n0 + c
                    for j in range(2):
                        if 2 * c + j >= split:
                            lo(2 * n + 3 + j)
                    if c % p.deep == p.deep - 1 and evacuate is not None:
                        dve.wait_ge(w_used, 2 * n + 2)
                        evacuate(c // p.deep, b3(p.pair + c // p.deep % 2))
                    if between is not None:
                        between(c)

            def rotate(r, width):
                dve.wait_ge(act_evac, r + 1)
                if r >= 2:
                    dve.wait_ge(rope_done, r - 1)
                n = width // S
                for q in range(4):
                    to, frm = slice(32 * q, 32 * q + 32), slice(32 * (q ^ 1), 32 * (q ^ 1) + 32)
                    sines = sinT[frm, :].unsqueeze(1).broadcast_to([32, n, S])
                    ins = dve.tensor_tensor(wk(4 + r % 2)[to, 0:width].rearrange("p (a b) -> p a b", a=n),
                                            wk(r % 2)[frm, 0:width].rearrange("p (a b) -> p a b", a=n),
                                            sines, ALU.mult)
                ins.then_inc(rope_rot, 1)

            def x_low(c, use, gain):
                dve.wait_ge(x_hi, XBASE[use] + c + 1)
                if gain is None:
                    dve.tensor_tensor(xl[:, 2 * c:2 * c + 2, :], h[:, 2 * c:2 * c + 2, :],
                                      xh[:, 2 * c:2 * c + 2, :].bitcast(F32), ALU.subtract).then_inc(x_lo, 1)
                    return
                for j in range(2):
                    m = 2 * c + j
                    ins = dve.scalar_tensor_tensor(xl[:, m, :], h[:, m, :], vc(gain, m), xh[:, m, :].bitcast(F32),
                                                   ALU.mult, ALU.subtract)
                ins.then_inc(x_lo, 1)

            def diagonal(name, src):
                for t in range(2):
                    dve.tensor_scalar(diag[:, t, :], ident, src[:, t:t + 1], None, ALU.mult).then_inc(st_diag, 1)

            def inverse_rms(name, eps):
                dve.wait_ge(st_full, STAT[name] + 1)
                dve.tensor_scalar(stat[:, :], bank[4][:, 0:2], 1.0 / D, eps, ALU.mult, ALU.add).then_inc(st_read, 1)
                dve.wait_ge(st_pow, POW[name] + 1)
                diagonal(name, rt_m if name == "mem" else rt)

            def residual(name, use, gain, alpha=None, split=0):
                p = PH[name]
                for c in range(p.n):
                    n = p.n0 + c
                    for j in range(2):
                        if 2 * c + j >= split:
                            lo(2 * n + 3 + j)
                    if c % p.deep == p.deep - 1:
                        o = c // p.deep
                        dve.wait_ge(w_used, 2 * n + 2)
                        hc, b = h[:, 2 * o:2 * o + 2, :], b3(p.pair + o % 2)
                        if alpha is None:
                            dve.tensor_tensor(hc, b, hc, ALU.add).then_inc(dve_evac, 1)
                        else:
                            hf = hc.rearrange("p a b -> p (a b)")
                            dve.scalar_tensor_tensor(hf, hf, alpha, bank[p.pair + o % 2][:, :], ALU.mult,
                                                     ALU.add).then_inc(dve_evac, 1)
                        if use is not None and o >= 1:
                            x_low(o - 1, use, gain)
                if use is not None:
                    x_low(3, use, gain)

            def soft_attention(name, heads, bias, scale, extra, lag):
                u0 = UBASE[name]
                for t in range(heads + lag):
                    if t < heads:
                        u = u0 + t
                        dve.wait_ge(s_full, u + 1)
                        if t >= 2:
                            dve.wait_ge(e_done, 2 * u - 2)
                        for q in range(2):
                            dve.tensor_tensor_reduce(wk3(t % 2)[:, q, :], b3(4 + t % 2)[:, q, :], bias(t)[:, q, :],
                                                     -scale, 3.0e38, ALU.add, ALU.min,
                                                     nmax[:, u, q:q + 1]).then_inc(s_read, 1)
                    if 1 <= t < heads + 1:
                        u = u0 + t - 1
                        dve.wait_ge(e_done, 2 * u + 2)
                        chain(dve.reciprocal(erec[:, u, :], esum[:, u, :]))
                        pr = wk3((2, 3, 6)[(t - 1) % 3])
                        for q in range(2):
                            dve.tensor_scalar(pr[:, q, :], pr[:, q, :], erec[:, u, q:q + 1], None,
                                              ALU.mult).then_inc(p_ready, 1)
                    extra(t)

            def gated(key, p, lag):
                def f(t):
                    if t >= lag and (t - lag) % 2 == 0 and (t - lag) // 2 < 8:
                        g = (t - lag) // 2
                        dve.wait_ge(o_full, OBASE[key] + 2 * g + 2)
                        if g >= 2:
                            dve.wait_ge(g_lo, GBASE[key] + g - 1)
                        dve.tensor_tensor(wk(10 + g % 2)[:, 0:S], bank[p.pair + g % 2][:, 0:S], gt[:, g, :],
                                          ALU.mult).then_inc(dve_evac, 1)
                return f

            def plain_low(name, tiles, first):
                p = PH["att" + name]

                def f(t):
                    if t >= 4:
                        a = t - 4
                        m = slice(first + tiles * a, first + tiles * a + tiles)
                        dve.wait_ge(y_hi, YBASE[name] + a + 1)
                        dve.tensor_tensor(yl[:, m, :], b3(p.pair + a % 2)[:, 0:tiles, :], yh[:, m, :].bitcast(F32),
                                          ALU.subtract).then_inc(dve_evac, 1)
                return f

            for c in range(4):
                x_low(c, "first", None)
            for h_ in range(3):
                lo(h_)
            dve.wait_ge(const_in, 32)
            chunks("qi", lambda c, b: rotate(c, 2 * S))
            rotate(2, S)
            dve.wait_ge(wi_full, 1)
            dve.tensor_scalar(wi[:, :, :].rearrange("p a b -> p (a b)"), bank[4][:, 0:2 * IH], IH ** -0.5, None,
                              ALU.mult).then_inc(wi_ready, 1)
            chunks("qa", lambda c, b: rotate(3 + c, 2 * S))
            dve.wait_ge(wi_ready, 1)
            for a in range(IH):
                dve.wait_ge(rel_ready, a + 1)
                for t in range(2):
                    if a >= 1:
                        dve.wait_ge(is_added, 2 * a - 1 + t)
                    dve.scalar_tensor_tensor(score[:, t, :], wk3(6 + a % 2)[:, t, :], wi[:, t, a:a + 1],
                                             (score if a else adm)[:, t, :], ALU.mult, ALU.add).then_inc(is_added, 1)
            dve.wait_ge(is_added, 2 * IH)
            chunks("ka", lambda c, b: rotate(7 + c, 2 * S))

            def pick(c):
                both(*[dve.max(top8[:, t, :], score[:, t, :]) for t in range(2)])
                both(*[dve.match_replace(score[:, t, :], top8[:, t, :], score[:, t, :], TAKEN) for t in range(2)])

            assert TOPK == 8 * 8
            def va(c):
                dve.wait_ge(m_hi, c + 1)
                for m in (2 * c, 2 * c + 1):
                    ins = dve.scalar_tensor_tensor(yl[:, KT + m, :], m_raw[:, m, :], vc("mem", m),
                                                   yh[:, KT + m, :].bitcast(F32), ALU.mult, ALU.subtract)
                ins.then_inc(m_lo, 1)
                pick(c)

            chunks("va", between=va)

            def ga(c):
                if c == 0:
                    inverse_rms("mem", RMS_EPS)
                pick(4 + c)

            chunks("ga", between=ga)
            chain(dve.tensor_scalar(selneg, score, 0.5 * TAKEN, NEG, ALU.is_gt, ALU.mult))
            soft_attention("A", NH, lambda a: selneg, HD ** -0.5, gated("A", PH["attA"], 5), 5)

            def layer_norm(l, filler, use, gain):
                i = int(l)
                p = PH[filler]
                for c in range(p.n):
                    n = p.n0 + c
                    if c == 2:
                        inverse_rms("var" + l, LN_EPS)
                    if c < 3:
                        lo(2 * n + 3)
                    if c == 0:
                        dve.wait_ge(st_full, STAT["mean" + l] + 1)
                        chain(dve.tensor_scalar(stat[:, :], bank[4][:, 0:2], 1.0 / D, None, ALU.mult))
                        diagonal("mean" + l, stat)
                    if c == 2:
                        dve.wait_ge(bc_full, STAT["var" + l] + 1)
                        for m in range(KT):
                            dve.scalar_tensor_tensor(h[:, m, :], h[:, m, :], vc("ln_g" + l, m), bank[5][:, 0:S], ALU.mult,
                                                     ALU.mult).then_inc(ln_g, 1)
                        for q in range(2):
                            x_low(q, use, gain)
                    lo(2 * n + 4)
                    if c == 0:
                        dve.wait_ge(bc_full, STAT["mean" + l] + 1)
                        for q in range(4):
                            hq = h[:, 2 * q:2 * q + 2, :]
                            dve.tensor_tensor(hq, hq, bank[5][:, 0:S].unsqueeze(1).broadcast_to([P, 2, S]),
                                              ALU.subtract).then_inc(ln_c, 1)
                        dve.wait_ge(ln_c, 4 * i + 4)
                    if c == 2:
                        lo(2 * n + 5)
                        for q in range(2, 4):
                            x_low(q, use, gain)
                    dve.wait_ge(w_used, 2 * n + 2)
                    dve.tensor_tensor(kt[:, 2 * c:2 * c + 2, :], b3(p.pair + c % 2),
                                      rb_m[:, :].unsqueeze(1).broadcast_to([P, 2, S]), ALU.mult).then_inc(dve_evac, 1)

            residual("oa", None, None, ALPHA)
            layer_norm("0", "kx0", "B", None)
            chunks("qb")
            chunks("kb")
            chunks("vb")
            chunks("gb")

            ZW = S + P
            zgate = gated("B", PH["attB"], 5)
            for t in range(NH + 5):
                if 2 <= t < NH + 2:
                    a = t - 2
                    dve.wait_ge(c_full, a + 1)
                    if a >= 2:
                        dve.wait_ge(o_full, OBASE["B"] + a - 1)
                    dve.wait_ge(z_neg, a + 1)
                    dve.tensor_tensor(wk(8 + a % 2)[:, 0:ZW], wk(6 + a % 2)[:, 0:ZW], bank[6 + a % 2][:, 0:ZW],
                                      ALU.subtract).then_inc(z_arg, 1)
                if t < NH:
                    b = bank[4 + t % 2][:, 0:ZW]
                    dve.wait_ge(z_ln, t + 1)
                    if t >= 2:
                        dve.wait_ge(z_masked, t - 1)
                    dve.scalar_tensor_tensor(wk(2 + t % 2)[:, 0:ZW], b, 0.0, wk(t % 2)[:, 0:ZW], ALU.max,
                                             ALU.add).then_inc(z_sp, 1)
                    if t >= 2:
                        dve.wait_ge(z_arg, t - 1)
                    dve.tensor_tensor(wk(6 + t % 2)[:, 0:ZW], b, c_("beforeneg"), ALU.add).then_inc(z_neg, 1)
                zgate(t)
            residual("ob", None, None, ALPHA)
            layer_norm("1", "kx1", "mix0", "mix0")

            def bias(c):
                dve.wait_ge(rpb_in, 16)
                for t in range(2):
                    dve.scalar_tensor_tensor(nabias[:, c, t, :], nabias[:, c, t, :], 1.0 / NA_SCALE, c_("colneg"),
                                             ALU.mult, ALU.add).then_inc(bias_ready, 1)

            def times_rb(dst):
                def f(c, b):
                    dve.tensor_tensor(dst[:, 2 * c:2 * c + 2, :], b, rb[:, :].unsqueeze(1).broadcast_to([P, 2, S]),
                                      ALU.mult).then_inc(dve_evac, 1)
                return f

            inverse_rms("mix0", RMS_EPS)
            chunks("zf", between=bias)
            dve.wait_ge(rb_ready, RBS["mix0"] + 1)
            chunks("qn", times_rb(qz), between=lambda c: bias(2 + c))
            dve.wait_ge(k_saved, 32)
            chunks("kn", times_rb(kt))
            chunks("vn")
            pf = PH["fourier"]
            for g in range(4):
                dve.wait_ge(y_hi, YBASE["F"] + g + 1)
                dve.tensor_tensor(yl[:, g, :], bank[pf.pair + g % 2][:, 0:S], yh[:, g, :].bitcast(F32),
                                  ALU.subtract).then_inc(dve_evac, 1)
            dve.wait_ge(bias_ready, 8)
            soft_attention("N", 4, lambda a: nabias[:, a, :, :], NA_SCALE, plain_low("N", 1, 4), 4)
            residual("oab", "xa0", "xa0")

            def convolution(key, c, taps, tiles):
                cv, cp = wk3(3 + c % 2), cpad[c % 2]

                dve.wait_ge(centre_ready, CBASE[key] + c + 1)
                both(*[dve.scalar_tensor_tensor(cv[:, j, :], cp[:, j, 0:S], vc(taps, 2 * c + j), cv[:, j, :], ALU.mult,
                                                ALU.add) for j in range(2)])
                for j in range(2):
                    ins = dve.scalar_tensor_tensor(cv[:, j, :], cp[:, j, 2:S + 2], vc(taps, 2 * tiles + 2 * c + j),
                                                   cv[:, j, :], ALU.mult, ALU.add)
                ins.then_inc(cv_ready, 1)

            def convolved(name, key, evacuate, taps, tiles):
                p = PH[name]
                for c in range(p.n):
                    n = p.n0 + c
                    lo(2 * n + 3)
                    if c >= 1:
                        convolution(key, c - 1, taps, tiles)
                    lo(2 * n + 4)
                    dve.wait_ge(w_used, 2 * n + 2)
                    evacuate(c, b3(p.pair + c % 2))
                if key == "conv":
                    lo(2 * (p.n0 + p.n) + 3)
                    lo(2 * (p.n0 + p.n) + 4)
                    convolution(key, p.n - 1, taps, tiles)
                    lo(2 * (p.n0 + p.n) + 5)
                else:
                    convolution(key, p.n - 1, taps, tiles)
                    lo(2 * (p.n0 + p.n) + 3)
                    lo(2 * (p.n0 + p.n) + 4)

            for l in "01":
                if l == "1":
                    inverse_rms("mix1", RMS_EPS)
                    dve.wait_ge(rb_ready, RBS["mix1"] + 1)
                    chunks("cb", times_rb(qz))
                    chunks("cc", times_rb(kt))

                    def scaled(c, b):
                        if c >= 2:
                            dve.wait_ge(gate_in, c - 1)
                        dve.tensor_tensor(wk3(5 + c % 2), b, rb[:, :].unsqueeze(1).broadcast_to([P, 2, S]),
                                          ALU.mult).then_inc(dve_evac, 1)

                    convolved("cu", "conv", scaled, "conv_c", 8)
                    chunks("vx1", split=3)
                    residual("oc", "xa1", "xa1")
                else:
                    chunks("vx0")
                inverse_rms("xa" + l, RMS_EPS)
                dve.wait_ge(rb_ready, RBS["xa" + l] + 1)
                chunks("qx" + l, times_rb(qz))
                dve.wait_ge(zero_ready, 1)
                soft_attention("X" + l, 4, lambda a: adm, XA_SCALE, plain_low("X" + l, 2, 0), 4)
                residual("ox" + l, "ffn" + l, "ffn" + l)
                inverse_rms("ffn" + l, RMS_EPS)
                dve.wait_ge(rb_ready, RBS["ffn" + l] + 1)
                chunks("fu" + l, times_rb(qz))
                dve.wait_ge(padded, 4 + 4 * int(l))

                def gate_chunk(c, b):
                    dve.tensor_tensor(cpad[c % 2][:, :, 1:S + 1], b, rb[:, :].unsqueeze(1).broadcast_to([P, 2, S]),
                                      ALU.mult).then_inc(dve_evac, 1)

                convolved("fg" + l, "ffn" + l, gate_chunk, "fconv" + l, 16)
                if l == "0":
                    residual("fd0", "mix1", "mix1", split=2)
                else:
                    residual("fd1", None, None, split=2)
            inverse_rms("fin", RMS_EPS)
            dve.wait_ge(bc_full, STAT["fin"] + 1)
            for m in range(KT):
                dve.scalar_tensor_tensor(gt[:, m, :], h[:, m, :], vc("fin", m), bank[5][:, 0:S], ALU.mult,
                                         ALU.mult).then_inc(fin_ready, 1)

        @block.gpsimd
        def _(pool):
            chain = Chain(pool, chain_pool)
            pool.memset(ones[:, :], 1.0).then_inc(filled, 1)
            pool.memset(half[:, :], -0.5).then_inc(filled, 1)
            pool.memset(qiz[:, :, :], 0.0).then_inc(filled, 1)
            pool.memset(qz[0:HD, 1:NH:2, :], 0.0).then_inc(filled, 1)
            pool.wait_ge(filled, 4)
            pool.memset(qz[HD:P, 0:NH:2, :], 0.0).then_inc(filled, 1)
            pool.wait_ge(filled, 5)

            def rope(r, width, targets):
                n = width // S
                t1 = wk(2 + r % 2)[:, 0:width].rearrange("p (a b) -> p a b", a=n)
                t2 = wk(4 + r % 2)[:, 0:width].rearrange("p (a b) -> p a b", a=n)
                pool.wait_ge(act_evac, r + 1)
                pool.tensor_tensor(t1, wk(r % 2)[:, 0:width].rearrange("p (a b) -> p a b", a=n),
                                   cosT.unsqueeze(1).broadcast_to([P, n, S]), ALU.mult).then_inc(rope_cos, 1)
                pool.wait_ge(rope_cos, r + 1)
                pool.wait_ge(rope_rot, r + 1)
                for dst, rows in targets:
                    if rows.start > 0:
                        chain(ins)
                    ins = pool.tensor_tensor(dst, t1[rows], t2[rows], ALU.add)
                ins.then_inc(rope_done, 1)
                pool.wait_ge(rope_done, r + 1)

            def heads(dst, c):
                return [(dst[0:HD, 4 * c:4 * c + 4:2, :], slice(0, HD)), (dst[HD:P, 4 * c + 1:4 * c + 4:2, :], slice(HD, P))]

            def sum_up(name, source):
                first = source(0)
                for c in range(1, 4):
                    if c >= 2:
                        pool.wait_ge(acc_done, 3 * STAT[name] + c - 1)
                    a = first if c == 1 else acc[:, :, :]
                    pool.tensor_tensor(acc[:, :, :], a, source(c), ALU.add).then_inc(acc_done, 1)

            def squares(name):
                def source(c):
                    pool.wait_ge(sq_ready, SQ[name] + c + 1)
                    return wk3(10 + c % 2)
                return source

            def stream(name):
                def source(c):
                    pool.wait_ge(dve_evac, PH[name].base + c + 1)
                    return h[:, 2 * c:2 * c + 2, :]
                return source

            def power(name):
                pool.wait_ge(st_read, POW[name] + 1)
                pool.tensor_tensor((rt_m if name == "mem" else rt)[:, :], stat[:, :], half[:, :], ALU.pow).then_inc(st_pow, 1)

            def norm(name):
                sum_up(name, squares(name))
                power(name)

            def gated_low(key, g):
                pool.wait_ge(y_hi, YBASE[key] + g + 1)
                pool.tensor_tensor(yl[:, g, :], wk(10 + g % 2)[:, 0:S], yh[:, g, :].bitcast(F32),
                                   ALU.subtract).then_inc(g_lo, 1)

            def product(key, c, a, b):
                if c >= 2:
                    pool.wait_ge(g_lo, GBASE[key] + c - 1)
                pool.tensor_tensor(wk3(7 + c % 2), a, b, ALU.mult).then_inc(pf_ready, 1)

            def product_low(key, c):
                pool.wait_ge(y_hi, YBASE[key] + c + 1)
                pool.tensor_tensor(yl[:, 2 * c:2 * c + 2, :], wk3(7 + c % 2), yh[:, 2 * c:2 * c + 2, :].bitcast(F32),
                                   ALU.subtract).then_inc(g_lo, 1)

            def ffn_products(key):
                for c in range(8):
                    pool.wait_ge(ge_ready, GEBASE[key] + c + 1)
                    product(key, c, wk3(5 + c % 2), qz[:, 2 * c:2 * c + 2, :])
                    if c >= 1:
                        product_low(key, c - 1)
                product_low(key, 7)

            def pads(name):
                pool.wait_ge(o_full, OBASE[name] + 4)
                pool.wait_ge(e_done, 2 * UBASE[name] + 8)
                for b in cpad:
                    for col in (0, S + 1):
                        pool.memset(b[:, :, col:col + 1], 0.0).then_inc(padded, 1)

            pool.wait_ge(const_in, 32)
            for c in range(2):
                rope(c, 2 * S, heads(qiz, c))
            rope(2, S, [(ki.unsqueeze(1), slice(0, P))])
            for c in range(4):
                rope(3 + c, 2 * S, heads(qz, c))
            for c in range(4):
                rope(7 + c, 2 * S, [(kt[:, 2 * c:2 * c + 2, :], slice(0, P))])
            norm("mem")
            for g in range(8):
                gated_low("A", g)
            sum_up("mean0", stream("oa"))
            norm("var0")
            pool.memset(adm, 0.0).then_inc(zero_ready, 1)
            for t in range(NH + 6):
                if t < NH:
                    pool.wait_ge(z_sp, t + 1)
                    if t >= 2:
                        pool.wait_ge(c_full, t - 1)
                    ZW = S + P
                    pool.tensor_tensor(wk(4 + t % 2)[:, 0:ZW], wk(2 + t % 2)[:, 0:ZW], c_("before"),
                                       ALU.mult).then_inc(z_masked, 1)
                if t >= 6 and t % 2 == 0:
                    gated_low("B", (t - 6) // 2)
            sum_up("mean1", stream("ob"))
            norm("var1")
            norm("mix0")
            norm("xa0")
            pads("X0")
            norm("ffn0")
            ffn_products("ffn0")
            norm("mix1")
            for c in range(5):
                if c < 4:
                    pool.wait_ge(dve_evac, PH["cu"].base + c + 1)
                    if c >= 2:
                        pool.wait_ge(cv_ready, CBASE["conv"] + c - 1)
                    pool.tensor_tensor(cpad[c % 2][:, :, 1:S + 1], wk3(5 + c % 2), kt[:, 2 * c:2 * c + 2, :],
                                       ALU.mult).then_inc(gate_in, 1)
                if c >= 1:
                    a = c - 1
                    pool.wait_ge(cv_ready, CBASE["conv"] + a + 1)
                    product("conv", a, wk3(3 + a % 2), qz[:, 2 * a:2 * a + 2, :])
                if c >= 2:
                    product_low("conv", c - 2)
            product_low("conv", 3)
            norm("xa1")
            pads("X1")
            norm("ffn1")
            ffn_products("ffn1")
            norm("fin")


def tables():
    p = np.arange(P)
    cst = np.zeros((P, NCST), np.float32)

    def put(name, a):
        cst[:, CST[name][0]:CST[name][1]] = a.reshape(P, -1)

    put("ident", np.eye(P))
    inv = (1.0 / (np.float32(10000.0) ** (np.arange(0, HD, 2, dtype=np.float32) / np.float32(HD)))).astype(np.float32)
    ang = (np.arange(S, dtype=np.float32)[None, :] * inv[p % 32][:, None]).astype(np.float32)
    put("cos", np.cos(ang))
    put("sin", np.where((p // 32 % 2 == 0)[:, None], 1, -1) * np.sin(ang))
    s = np.arange(S)
    q = np.arange(2)[None, :] * P + p[:, None]
    put("adm", np.where(s[None, None, :] // CHUNK <= q[:, :, None] // CHUNK, 0.0, NEG))
    before = np.concatenate([p[:, None] < s[None, :], p[:, None] < p[None, :]], 1)
    put("before", before.astype(np.float32))
    put("beforeneg", np.where(before, 0.0, NEG))
    put("tri", (p[:, None] >= p[None, :]).astype(np.float32))
    start = np.clip(p % GW - 8, 0, GW - 16)[:, None]
    col = (s % GW)[None, :]
    put("colneg", np.where((col >= start) & (col < start + 16), 0.0, NEG))
    dft = np.zeros((P, 1280), np.float32)
    tok = (np.arange(2)[None, :, None] * P + p[:, None, None]) * s[None, None, :] % S
    a = 2 * np.pi * tok / S
    dft[:, 0:1024] = np.concatenate([np.cos(a), np.sin(a)], 2).reshape(P, -1)
    a = 2 * np.pi * (p[:, None] * p[None, :] % P) / P
    scale = 1.0 / math.sqrt(S * P)
    dft[:, 1024:1152] = np.cos(a) * scale
    dft[:, 1152:1280] = -np.sin(a) * scale
    return cst, dft


def neighbourhood_bias(rpb):
    s = np.arange(S)
    q = np.arange(2)[None, :] * P + np.arange(P)[:, None]
    dr = s[None, None, :] // GW - q[:, :, None] // GW + 7
    dc = np.clip(s[None, None, :] % GW - q[:, :, None] % GW + 15, 0, 30)
    return np.ascontiguousarray(rpb[:, dr, dc].transpose(1, 0, 2, 3)).reshape(P, -1)


def kernel(**inputs):
    import concourse.bacc as bacc
    from concourse.bass_utils import run_bass_kernel_spmd as run

    x = {k: np.asarray(a) for k, a in inputs.items()}

    def tiled(a):
        return np.ascontiguousarray(a.reshape(-1, P, a.shape[-1]).transpose(1, 0, 2))

    def cols(a, lo, hi):
        return [tiled(a[r:r + D, c:c + CW]) for c in range(lo, hi, CW) for r in range(0, a.shape[0], D)]

    wa, wb = x["w_in_a"][0], x["w_in_b"][0]
    IQ = 4 * D
    kv = x["xa_wkv_2"]
    chunks = cols(wa, IQ, IQ + 512) + cols(wa, 0, 4 * D) + cols(x["w_out_a"][0], 0, D) + cols(kv[0], 0, D)
    chunks += cols(wb, 0, 4 * D) + cols(x["w_out_b"][0], 0, D) + cols(kv[1], 0, D)
    chunks += cols(x["w_in_ab_2"][0], 0, 2048) + cols(x["w_out_ab_2"][0], 0, D)
    for l in range(2):
        if l == 1:
            chunks += cols(x["w_in_c_2"][0], 0, 3 * D)
        chunks += cols(kv[l], D, 2 * D)
        if l == 1:
            chunks += cols(x["w_out_c_2"][0], 0, D)
        chunks += cols(x["xa_wq_2"][l], 0, D) + cols(x["xa_wo_2"][l], 0, D)
        chunks += cols(x["ffn_w_up_2"][l], 0, 4 * D) + cols(x["ffn_w_down_2"][l], 0, D)
    w = np.stack(chunks)
    assert w.shape == (NCHUNK, P, KT, CW)
    wki = tiled(np.concatenate([wa[:, IQ + 520:IQ + 584]] * 2, 1))
    wwi = tiled(wa[:, IQ + 512:IQ + 520])

    vecs = np.zeros((P, NVEC), np.float32)

    def put(name, a):
        a = np.ascontiguousarray(a).reshape(-1, P).T
        vecs[:, VEC[name]:VEC[name] + a.shape[1]] = a

    for l in range(2):
        put(f"ln_g{l}", x["ln_g"][l])
        put(f"ln_b{l}", x["ln_b"][l])
        put(f"mix{l}", x["mix_norm_g_2"][l])
        put(f"xa{l}", x["xa_norm_g_2"][l])
        put(f"ffn{l}", x["ffn_norm_g_2"][l])
        put(f"fconv{l}", x["ffn_conv_w_2"][l])
        put(f"fbias{l}", x["ffn_conv_b_2"][l])
    put("mem", x["mem_norm_g_2"])
    put("fin", x["final_norm_g_2"])
    put("conv_c", x["conv_c_2"][0])
    cst, dft = tables()

    nc = bacc.Bacc("TRN2", target_bir_lowering=False, num_devices=1)
    arrays = {
        "w": w, "xt": tiled(x["x"][0].T), "memt": tiled(x["mem_2"][0].T).reshape(P, -1), "vecs": vecs, "cst": cst,
        "wki": wki, "wwi": wwi, "dft": dft, "rpb": neighbourhood_bias(x["rpb_2"][0]),
    }
    args = [nc.dram_tensor(k, a.shape, F32, kind="ExternalInput").ap() for k, a in arrays.items()]
    args.append(nc.dram_tensor("y", (P, KT, S), F32, kind="ExternalOutput").ap())
    build(nc, *args)
    r = run(nc, [arrays], core_ids=[0])
    y = r.results[0]["y"]
    return np.ascontiguousarray(y.transpose(2, 1, 0)).reshape(1, S, D)
```

```python
import math
from contextlib import ExitStack

import numpy as np

import concourse.bass as bass
from concourse import mybir

F32 = mybir.dt.float32
F32R = mybir.dt.float32r
ALU = mybir.AluOpType
ACT = mybir.ActivationFunctionType

P = 128
D = 1024
S = 256
KT = D // P
CW = 256
CHUNK = 64
TOPK = min(256, S // 4)
ALPHA = (2.0 * 2) ** 0.25
HD = 64
NH = D // HD
IH = 8
GW = 64
LN_EPS, RMS_EPS = 1e-5, 1e-6
NEG = -1.0e30
TAKEN = -3.0e38
RAW_SLOTS = 4
NA_SCALE = float(P) ** -0.5
XA_SCALE = float(CW) ** -0.5

VEC = {}
_at = 0
for _name, _n in (("ln_g0", 8), ("ln_g1", 8), ("ln_b0", 8), ("ln_b1", 8), ("mem", 8), ("mix0", 8), ("mix1", 8),
                  ("xa0", 8), ("xa1", 8), ("ffn0", 8), ("ffn1", 8), ("fin", 8), ("conv_c", 24),
                  ("fconv0", 48), ("fconv1", 48), ("fbias0", 16), ("fbias1", 16)):
    VEC[_name] = _at
    _at += _n
NVEC = _at

CST = {}
_at = 0
for _name, _n in (("ident", 128), ("cos", 256), ("sin", 256), ("adm", 512), ("before", 384), ("beforeneg", 384),
                  ("tri", 128), ("colneg", 256)):
    CST[_name] = (_at, _at + _n)
    _at += _n
NCST = _at


WARM_UP = 16


class Phase:
    pass


def schedule():
    phases, at, count = {}, 0, {"act": 0, "dve": 0}
    order = []

    def add(name, chunks, reader, outs=None, deep=1):
        nonlocal at
        p = Phase()
        p.name, p.n0, p.n, p.deep, p.reader = name, at, chunks, deep, reader
        p.outs = outs if outs is not None else chunks // deep
        p.base = count[reader]
        p.end = p.base + p.outs
        count[reader] += p.outs
        p.pair = 2 * (len(order) % 2)
        p.before = order[-2] if len(order) >= 2 else None
        at += chunks
        phases[name] = p
        order.append(p)

    add("qi", 2, "act")
    add("ki", 0, "act", 1)
    add("qa", 4, "act")
    add("ka", 4, "act")
    add("ga", 4, "act")
    add("va", 4, "act")
    add("attA", 0, "dve", 8)
    add("oa", 4, "dve")
    add("kx0", 4, "dve")
    add("gb", 4, "act")
    add("qb", 4, "act")
    add("kb", 4, "act")
    add("vb", 4, "act")
    add("attB", 0, "dve", 8)
    add("ob", 4, "dve")
    add("kx1", 4, "dve")
    add("zf", 2, "act")
    add("qn", 2, "dve")
    add("kn", 2, "dve")
    add("vn", 2, "act")
    add("fourier", 0, "dve", 4)
    add("attN", 0, "dve", 4)
    add("oab", 4, "dve")
    for l in "01":
        if l == "1":
            add("cb", 4, "dve")
            add("cc", 4, "dve")
            add("cu", 4, "dve")
        add("vx" + l, 4, "act")
        if l == "1":
            add("oc", 4, "dve")
        add("qx" + l, 4, "dve")
        add("attX" + l, 0, "dve", 4)
        add("ox" + l, 4, "dve")
        add("fu" + l, 8, "dve")
        add("fg" + l, 8, "dve")
        add("fd" + l, 8, "dve", deep=2)
    return phases, at


PH, NCHUNK = schedule()


def bases(*uses):
    table, n = {}, 0
    for name, times in uses:
        table[name] = n
        n += times
    return table


XBASE = bases(*[(u, 4) for u in ("first", "B", "mix0", "xa0", "ffn0", "mix1", "xa1", "ffn1")])
GBASE = bases(("A", 8), ("B", 8), ("ffn0", 8), ("conv", 4), ("ffn1", 8))
YBASE = bases(("A", 8), ("B", 8), ("F", 4), ("N", 4), ("X0", 4), ("ffn0", 8), ("conv", 4), ("X1", 4), ("ffn1", 8))
UBASE = bases(("A", 16), ("N", 4), ("X0", 4), ("X1", 4))
OBASE = bases(("A", 16), ("B", 16), ("F", 4), ("N", 4), ("X0", 4), ("X1", 4))
CBASE = bases(("ffn0", 8), ("conv", 4), ("ffn1", 8))
GEBASE = bases(("ffn0", 8), ("ffn1", 8))
STAT = bases(*[(u, 1) for u in ("mem", "mean0", "var0", "mean1", "var1", "mix0", "xa0", "ffn0", "mix1", "xa1",
                                "ffn1", "fin")])
POW = bases(*[(u, 1) for u in ("mem", "var0", "var1", "mix0", "xa0", "ffn0", "mix1", "xa1", "ffn1", "fin")])
RBS = bases(*[(u, 1) for u in ("mem", "mix0", "xa0", "ffn0", "mix1", "xa1", "ffn1")])
SQ = bases(*[(u, 4) for u in POW])


def build(nc, w, xt, memt, vecs, cst, wki, wwi, dft, rpb, out):
    ctx = ExitStack()
    with ctx:
        def sb(name, shape, dt=F32):
            return ctx.enter_context(nc.sbuf_tensor(name, shape, dt))

        def sem(name):
            return ctx.enter_context(nc.semaphore(name))

        raw = sb("raw", [P, RAW_SLOTS, KT, CW])
        wh = sb("wh", [P, 2, KT, CW], F32R)
        wl = sb("wl", [P, 2, KT, CW], F32R)
        h = sb("h", [P, KT, S])
        xh = sb("xh", [P, KT, S], F32R)
        xl = sb("xl", [P, KT, S], F32R)
        yh = sb("yh", [P, 2 * KT, S], F32R)
        yl = sb("yl", [P, 2 * KT, S], F32R)
        qz = sb("qz", [P, NH, S])
        kt = sb("kt", [P, KT, S])
        v = sb("v", [P, 2, D])
        gt = sb("gt", [P, KT, S])
        work = sb("work", [P, 12 * 512])
        cs = sb("cs", [P, NCST])
        vec = sb("vec", [P, NVEC])
        ones = sb("ones", [P, P])
        half = sb("half", [P, 2])
        acc = sb("acc", [P, 2, S])
        rb = sb("rb", [P, S])
        rb_m = sb("rb_m", [P, S])
        rt_m = sb("rt_m", [P, 2])
        diag = sb("diag", [P, 2, P])
        stat = sb("stat", [P, 2])
        rt = sb("rt", [P, 2])
        wi = sb("wi", [P, 2, IH])
        top8 = sb("top8", [P, 2, 8])
        nmax = sb("nmax", [P, 28, 2])
        esum = sb("esum", [P, 28, 2])
        erec = sb("erec", [P, 28, 2])
        bank = [ctx.enter_context(nc.psum_tensor(f"bank{i}", [P, 512], F32)) for i in range(8)]
        k_scratch = nc.dram_tensor("k_scratch", [2, P, KT * S], F32, kind="Internal").ap()
        m_scratch = nc.dram_tensor("m_scratch", [2, P, KT * S], F32, kind="Internal").ap()

        def wk(i):
            return work[:, 512 * i:512 * i + 512]

        def wk3(i):
            return wk(i).rearrange("p (a b) -> p a b", a=2)

        def c_(name):
            a, b = CST[name]
            return cs[:, a:b]

        def vc(name, j):
            return vec[:, VEC[name] + j:VEC[name] + j + 1]

        def b3(i):
            return bank[i][:, :].rearrange("p (a b) -> p a b", a=2)

        ident, cosT, sinT = c_("ident"), c_("cos"), c_("sin")
        adm = c_("adm").rearrange("p (a b) -> p a b", a=2)
        qiz = gt
        ki = work[:, 11 * 512:11 * 512 + 256]
        kiw = v[:, :, :].rearrange("p a b -> p (a b)")[:, 0:KT * P].rearrange("p (k n) -> p k n", k=KT)
        wiw = v[:, :, :].rearrange("p a b -> p (a b)")[:, KT * P:KT * P + KT * IH].rearrange("p (k n) -> p k n", k=KT)
        nabias = qz[:, 4:12, :].rearrange("p (h t) s -> p h t s", t=2)
        u_tok = qz[:, 12:16, :].rearrange("p a b -> p (a b)").rearrange("p (t n) -> p t n", t=2)
        gflat = gt[:, :, :].rearrange("p a b -> p (a b)")
        dft_s = gflat[:, 0:1024].rearrange("p (t n) -> p t n", t=2)
        dft_c = gflat[:, 1024:1280]
        m_raw = v[:, :, :].rearrange("p a b -> p (a b)").rearrange("p (k s) -> p k s", k=KT)
        score, selneg = wk3(8), wk3(9)
        cpad = [work[:, 516 * i:516 * i + 516].rearrange("p (a b) -> p a b", a=2) for i in range(2)]

        raw_full = [sem(f"raw_full{i}") for i in range(RAW_SLOTS)]
        first_half = sem("first_half")
        const_in, x_in, kiw_in = sem("const_in"), sem("x_in"), sem("kiw_in")
        mem_in, m_saved, m_back = sem("mem_in"), sem("m_saved"), sem("m_back")
        k_saved, k_back = sem("k_saved"), sem("k_back")
        rpb_in, dft_in, stored = sem("rpb_in"), sem("dft_in"), sem("stored")
        hi_ready, lo_ready = sem("hi_ready"), sem("lo_ready")
        w_used = sem("w_used")
        act_evac, dve_evac = sem("act_evac"), sem("dve_evac")
        evac = {"act": act_evac, "dve": dve_evac}
        filled = sem("filled")
        ki_full, wi_full, wi_ready = sem("ki_full"), sem("wi_full"), sem("wi_ready")
        rope_rot, rope_cos, rope_done = sem("rope_rot"), sem("rope_cos"), sem("rope_done")
        is_full, rel_ready, is_added = sem("is_full"), sem("rel_ready"), sem("is_added")
        x_hi, x_lo = sem("x_hi"), sem("x_lo")
        sq_ready, acc_done = sem("sq_ready"), sem("acc_done")
        st_full, st_read, st_pow, st_diag = sem("st_full"), sem("st_read"), sem("st_pow"), sem("st_diag")
        bc_full, rb_ready = sem("bc_full"), sem("rb_ready")
        s_full, s_read, e_done, p_ready = sem("s_full"), sem("s_read"), sem("e_done"), sem("p_ready")
        t_full, t_evac, o_full = sem("t_full"), sem("t_evac"), sem("o_full")
        y_hi, g_lo = sem("y_hi"), sem("g_lo")
        z_full, z_abs, z_ln, z_sp = sem("z_full"), sem("z_abs"), sem("z_ln"), sem("z_sp")
        z_masked, z_neg, c_full, z_arg, z_prob = sem("z_masked"), sem("z_neg"), sem("c_full"), sem("z_arg"), sem("z_prob")
        f_full, f_copied = sem("f_full"), sem("f_copied")
        ln_c, ln_g, ln_h = sem("ln_c"), sem("ln_g"), sem("ln_h")
        gate_in, centre_ready, cv_ready = sem("gate_in"), sem("centre_ready"), sem("cv_ready")
        ge_ready, pf_ready = sem("ge_ready"), sem("pf_ready")
        m_hi, m_lo = sem("m_hi"), sem("m_lo")
        bias_ready, zero_ready, padded = sem("bias_ready"), sem("zero_ready"), sem("padded")
        chain_act, chain_dve, chain_pool = sem("chain_act"), sem("chain_dve"), sem("chain_pool")
        fin_ready = sem("fin_ready")

        class Chain:
            def __init__(self, eng, s):
                self.eng, self.s, self.n = eng, s, 0

            def __call__(self, ins):
                self.n += 1
                ins.then_inc(self.s, 1)
                self.eng.wait_ge(self.s, self.n)

        block = ctx.enter_context(nc.Block())

        @block.sync
        def _(sp):
            def load(n, slot):
                sp.dma_start(raw[:, slot, :, :], w[n]).then_inc(raw_full[slot], 16)

            sp.dma_start(raw[:, 0, :, 0:P], w[0][:, :, 0:P]).then_inc(first_half, 16)
            sp.dma_start(h[:, :, :], xt).then_inc(x_in, 16)
            sp.dma_start(raw[:, 0, :, P:CW], w[0][:, :, P:CW]).then_inc(raw_full[0], 16)
            load(1, 1)
            sp.dma_start(kiw, wki).then_inc(kiw_in, 16)
            sp.dma_start(wiw, wwi).then_inc(kiw_in, 16)
            load(2, 2)
            sp.dma_start(cs[:, :], cst).then_inc(const_in, 16)
            sp.dma_start(vec[:, :], vecs).then_inc(const_in, 16)
            load(3, 3)
            rest = NCHUNK - RAW_SLOTS
            with sp.Fori(1, 1 + rest // RAW_SLOTS) as i:
                for c in range(RAW_SLOTS):
                    sp.wait_ge(lo_ready, 2 * RAW_SLOTS * i - 2 * RAW_SLOTS + 2 * c + 2)
                    sp.dma_start(raw[:, c, :, :],
                                 w[bass.ds(RAW_SLOTS * i + c, 1)].rearrange("o p k n -> (o p) k n")
                                 ).then_inc(raw_full[c], 16)
            for n in range(NCHUNK - rest % RAW_SLOTS, NCHUNK):
                sp.wait_ge(lo_ready, 2 * (n - RAW_SLOTS) + 2)
                load(n, n % RAW_SLOTS)
            for c in range(4):
                sp.wait_ge(fin_ready, 2 * c + 2)
                sp.dma_start(out[:, 2 * c:2 * c + 2, :], gt[:, 2 * c:2 * c + 2, :]).then_inc(stored, 16)
            sp.wait_ge(stored, 64)
            sp.wait_ge(m_saved, 32)
            sp.wait_ge(k_saved, 32)

        @block.tensor
        def _(pe):
            def enter(p):
                if p.before is not None:
                    pe.wait_ge(evac[p.before.reader], p.before.end)

            def project(name, oh, ol, ready=None, tok=False, hooks={}, tile0=0):
                p = PH[name]
                enter(p)
                per = 2 * p.deep

                def round_(i, first, hooks=hooks):
                    for c in range(per):
                        n = per * i + (p.n0 + c)
                        slot = (p.n0 + c) % 2
                        b = b3(p.pair + c // p.deep)
                        k0 = (c % p.deep) * KT
                        early = ready if c < p.deep else None
                        if c % p.deep == 0 and not first:
                            pe.wait_ge(evac[p.reader], 2 * i + (p.base + c // p.deep - 1))

                        def product(k, q, j):
                            kk, part = tile0 + k0 + k, slice(j * P, j * P + P)
                            o_, w_ = (oh, oh, ol)[q], (wh, wl, wh)[q]
                            weights = w_[:, slot, k, :] if tok else w_[:, slot, k, part]
                            operand = o_[:, kk, part] if tok else o_[:, kk, :]
                            lhs, rhs = (operand, weights) if tok else (weights, operand)
                            both_open = p.deep > 1 or ready is not None and c == 0
                            return pe.matmul(b[:, j, :], lhs, rhs,
                                             start=k0 + k == 0 and q == 0 and (j == 0 or not both_open),
                                             stop=k0 + k == KT * p.deep - 1 and q == 2, skip_group_check=both_open)

                        def split_wait(j):
                            if tok and j == 0:
                                pe.wait_ge(lo_ready, 2 * n + 2)
                            if not tok:
                                pe.wait_ge(lo_ready, 2 * n + (j + 1))

                        def steps(j, tiles):
                            if early:
                                for k in tiles:
                                    if j == 0:
                                        pe.wait_ge(*early(k0 + k)[0])
                                    for q in range(2):
                                        product(k, q, j)
                            for k in tiles:
                                if early and j == 0:
                                    pe.wait_ge(*early(k0 + k)[1])
                                for q in range(2 if early else 0, 3):
                                    mm = product(k, q, j)
                                if k == KT - 1 and not tok:
                                    mm.then_inc(w_used, 1)
                                elif k == KT - 1 and j == 1:
                                    mm.then_inc(w_used, 2)
                                if hooks and (per * i + c, j, k) in hooks:
                                    hooks[per * i + c, j, k]()

                        if early:
                            for tiles in (range(KT - 2), range(KT - 2, KT)):
                                for j in range(2):
                                    if tiles[0] == 0:
                                        split_wait(j)
                                    steps(j, tiles)
                        else:
                            for j in range(2):
                                split_wait(j)
                                steps(j, range(KT))

                rounds = p.n // per
                if hooks or p.base < 2:
                    once = rounds if rounds < 3 else 1
                    for i in range(once):
                        round_(i, i == 0)
                    if once < rounds:
                        with pe.Fori(once, rounds) as i:
                            round_(i, False, {})
                elif rounds == 1:
                    round_(0, True)
                else:
                    with pe.Fori(0, rounds) as i:
                        round_(i, False)

            def stats(name):
                parts = [acc[:, e, :] for e in range(2)]
                if name == "fin":
                    pe.wait_ge(acc_done, 3 * STAT[name] + 2)
                    pe.wait_ge(sq_ready, SQ[name] + 4)
                    parts += [wk3(11)[:, e, :] for e in range(2)]
                else:
                    pe.wait_ge(acc_done, 3 * STAT[name] + 3)
                for t in range(2):
                    for e, part in enumerate(parts):
                        mm = pe.matmul(bank[4][:, t:t + 1], part[:, t * P:t * P + P], ones[:, 0:1],
                                       start=(e == 0), stop=(e == len(parts) - 1))
                mm.then_inc(st_full, 1)

            def bcast(name):
                pe.wait_ge(st_diag, 2 * STAT[name] + 2)
                pe.matmul(bank[5][:, 0:S], ones[:, :], diag[:, :, :].rearrange("p a b -> p (a b)"),
                          start=True, stop=True).then_inc(bc_full, 1)

            def x_ready(use):
                return lambda k: ((x_hi, XBASE[use] + k // 2 + 1), (x_lo, XBASE[use] + k // 2 + 1))

            def y_ready(key, low, base, tiles):
                return lambda k: ((y_hi, YBASE[key] + k // tiles + 1), (low, base + k // tiles + 1))

            def mixer_ready(k):
                return ((y_hi, YBASE["F"] + k + 1),
                        (dve_evac, (PH["fourier"].base + k if k < 4 else PH["attN"].base + k - 4) + 1))

            def scores(name, a):
                u = UBASE[name] + a
                if a >= 2:
                    pe.wait_ge(s_read, 2 * (u - 1))
                if name[0] == "X":
                    pe.wait_ge(dve_evac, PH["qx" + name[1]].base + a + 1)
                for t in range(2):
                    part = slice(t * P, t * P + P)
                    if name == "A":
                        ops = [(qz[:, a, part], kt[:, a // 2, :])]
                    elif name == "N":
                        ops = [(qz[:, a, part], kt[:, a, :])]
                    else:
                        ops = [(qz[:, 2 * a + j, part], kt[:, 2 * a + j, :]) for j in range(2)]
                    for j, (l, r) in enumerate(ops):
                        mm = pe.matmul(b3(4 + a % 2)[:, t, :], l, r, start=(j == 0), stop=(j == len(ops) - 1))
                mm.then_inc(s_full, 1)

            def soft_attention(name, heads, value_ops, group, p, values_in):
                u0 = UBASE[name]

                def turn(a):
                    u = u0 + a
                    pe.wait_ge(p_ready, 2 * u + 2)
                    if a >= 2:
                        pe.wait_ge(t_evac, u - 1)
                    pr = wk3((2, 3, 6)[a % 3])
                    for s in range(2):
                        for t in range(2):
                            mm = pe.transpose(b3(6 + a % 2)[:, s, t * P:t * P + P], pr[:, t, s * P:s * P + P], ident)
                    mm.then_inc(t_full, 1)

                def values(a):
                    u = u0 + a
                    pe.wait_ge(t_evac, u + 1)
                    g = a // group
                    if a % group == 0 and g >= 2:
                        pe.wait_ge(dve_evac, p.base + g - 1)
                    for o, sl in value_ops(a, p.pair + g % 2):
                        for s in range(2):
                            mm = pe.matmul(o, v[:, s, sl], wk3(4 + a % 2)[:, s, :], start=(s == 0), stop=(s == 1))
                    mm.then_inc(o_full, 1)

                for t in range(2, heads + 3):
                    if t < heads:
                        scores(name, t)
                    if 2 <= t < heads + 2:
                        turn(t - 2)
                    if t == 3:
                        enter(p)
                        pe.wait_ge(act_evac, PH[values_in].end)
                    if t >= 3:
                        values(t - 3)

            def norm_hooks(name):
                return {(0, 1, 7): lambda: stats(name), (1, 0, 5): lambda: bcast(name)}

            def layer_norm_hooks(l):
                return {(0, 0, 5): lambda: stats("mean" + l), (0, 1, 3): lambda: bcast("mean" + l),
                        (2, 0, 0): lambda: stats("var" + l), (2, 1, 0): lambda: bcast("var" + l)}

            pe.wait_ge(filled, 1)
            for i in range(WARM_UP):
                pe.matmul(bank[7][:, 0:P], ones[:, :], ones[:, :], start=True, stop=True)
            project("qi", xh, xl, x_ready("first"))
            pe.wait_ge(kiw_in, 32)
            for k in range(KT):
                mm = pe.matmul(bank[PH["ki"].pair][:, 0:S], kiw[:, k, :], h[:, k, :], start=(k == 0), stop=(k == KT - 1))
            mm.then_inc(ki_full, 1)

            def indexer_weights(t, k):
                mm = pe.matmul(bank[4][:, 8 * t:8 * t + IH], h[:, k, t * P:t * P + P], wiw[:, k, :],
                               start=(k == 0), stop=(k == KT - 1))
                if t == 1 and k == KT - 1:
                    mm.then_inc(wi_full, 1)

            project("qa", xh, xl, hooks={(t, 1, k): lambda t=t, k=k: indexer_weights(t, k)
                                         for t in range(2) for k in range(KT)})
            pe.wait_ge(rope_done, 3)
            pe.wait_ge(wi_ready, 1)
            for a in range(IH):
                if a >= 2:
                    pe.wait_ge(rel_ready, a - 1)
                for t in range(2):
                    mm = pe.matmul(b3(4 + a % 2)[:, t, :], qiz[:, a, t * P:t * P + P], ki, start=True, stop=True)
                mm.then_inc(is_full, 1)
            project("ka", xh, xl)
            pe.wait_ge(rel_ready, IH)
            pe.wait_ge(filled, 2)
            project("ga", xh, xl, hooks={(2, 1, 7): lambda: stats("mem")})

            def first_scores():
                pe.wait_ge(rope_done, 11)
                scores("A", 0)

            def second_scores():
                pe.wait_ge(rb_ready, RBS["mem"] + 1)
                scores("A", 1)

            project("va", xh, xl, tok=True, hooks={(1, 1, 7): lambda: bcast("mem"), (2, 1, 7): first_scores,
                                                   (3, 1, 3): second_scores})

            soft_attention("A", NH,
                           lambda a, b: [(bank[b][HD * (a % 2):HD * (a % 2) + HD, 0:S], slice(HD * a, HD * a + HD))],
                           2, PH["attA"], "va")
            project("oa", yh, yl, y_ready("A", g_lo, GBASE["A"], 1))
            pe.wait_ge(m_lo, 4)
            project("kx0", yh, yl, tile0=KT, hooks=layer_norm_hooks("0"))
            project("gb", xh, xl, x_ready("B"))
            project("qb", xh, xl)
            project("kb", xh, xl)

            tri = c_("tri")
            LATE = slice(P, S)

            def z_scores(a):
                if a >= 2:
                    pe.wait_ge(z_neg, a - 1)
                b = bank[4 + a % 2]
                pe.matmul(b[:, 0:S], kt[:, a // 2, 0:P], qz[:, a, :], start=True, stop=True)
                pe.matmul(b[:, S:S + P], kt[:, a // 2, LATE], qz[:, a, LATE], start=True, stop=True).then_inc(z_full, 1)

            def first_logits():
                pe.wait_ge(act_evac, PH["kb"].end)
                z_scores(0)

            project("vb", xh, xl, tok=True, hooks={(3, 0, 3): first_logits, (3, 1, 3): lambda: z_scores(1)})
            pb = PH["attB"]

            def z_sums(a):
                pe.wait_ge(z_masked, a + 1)
                if a >= 2:
                    pe.wait_ge(z_arg, a - 1)
                b, sp_ = bank[6 + a % 2], wk(4 + a % 2)
                pe.matmul(b[:, 0:P], tri, sp_[:, 0:P], start=True, stop=True)
                pe.matmul(b[:, P:S], tri, sp_[:, P:S], start=True, stop=False)
                pe.matmul(b[:, P:S], ones[:, :], sp_[:, S:S + P], start=False, stop=True)
                pe.matmul(b[:, S:S + P], tri, sp_[:, S:S + P], start=True, stop=True).then_inc(c_full, 1)

            def z_values(a):
                pe.wait_ge(z_prob, a + 1)
                g = a // 2
                if a % 2 == 0 and g >= 2:
                    pe.wait_ge(dve_evac, pb.base + g - 1)
                r = slice(HD * (a % 2), HD * (a % 2) + HD)
                b, pr, cols = bank[pb.pair + g % 2], wk(8 + a % 2), slice(HD * a, HD * a + HD)
                pe.matmul(b[r, 0:P], v[:, 0, cols], pr[:, 0:P], start=True, stop=True)
                pe.matmul(b[r, P:S], v[:, 0, cols], pr[:, P:S], start=True, stop=False)
                pe.matmul(b[r, P:S], v[:, 1, cols], pr[:, S:S + P], start=False, stop=True).then_inc(o_full, 1)

            for t in range(2, NH + 4):
                if t < NH:
                    z_scores(t)
                if 2 <= t < NH + 2:
                    z_sums(t - 2)
                if t == 4:
                    enter(pb)
                    pe.wait_ge(act_evac, PH["vb"].end)
                if t >= 4:
                    z_values(t - 4)
            project("ob", yh, yl, y_ready("B", g_lo, GBASE["B"], 1))
            project("kx1", yh, yl, tile0=KT, hooks=layer_norm_hooks("1"))

            project("zf", xh, xl, x_ready("mix0"), tok=True, hooks=norm_hooks("mix0"))
            project("qn", xh, xl)
            project("kn", xh, xl)
            project("vn", xh, xl, tok=True)
            pe.wait_ge(dve_evac, PH["kn"].end)
            for a in range(2):
                scores("N", a)
            pe.wait_ge(act_evac, PH["zf"].end)
            pe.wait_ge(dft_in, 32)
            pf = PH["fourier"]
            enter(pf)

            def f_tokens(g):
                if g >= 2:
                    pe.wait_ge(f_copied, g - 1)
                for t in range(2):
                    mm = pe.matmul(bank[6 + g % 2][:, :], u_tok[:, t, g * P:g * P + P], dft_s[:, t, :],
                                   start=(t == 0), stop=(t == 1))
                mm.then_inc(f_full, 1)

            def f_channels(g):
                pe.wait_ge(f_copied, g + 1)
                if g >= 2:
                    pe.wait_ge(dve_evac, pf.base + g - 1)
                b = bank[pf.pair + g % 2]
                pe.matmul(b[:, 0:S], dft_c[:, 0:P], wk(8 + g % 2)[:, 0:S], start=True, stop=False)
                pe.matmul(b[:, 0:S], dft_c[:, P:S], wk(8 + g % 2)[:, S:2 * S], start=False, stop=True).then_inc(o_full, 1)

            for g in range(5):
                if g < 4:
                    f_tokens(g)
                if g >= 1:
                    f_channels(g - 1)
            pn = PH["attN"]
            soft_attention("N", 4,
                           lambda a, b: [(bank[b][:, 0:S], slice(P * a, P * a + P))], 1, pn, "vn")
            project("oab", yh, yl, mixer_ready)

            for l in "01":
                if l == "1":
                    project("cb", xh, xl, x_ready("mix1"), hooks=norm_hooks("mix1"))
                    project("cc", xh, xl)
                    project("cu", xh, xl)
                    pe.wait_ge(m_back, 32)
                project("vx" + l, yh, yl, tok=True, tile0=KT)
                if l == "1":
                    project("oc", yh, yl, y_ready("conv", g_lo, GBASE["conv"], 2))

                def first_scores(a, l=l):
                    if a == 0:
                        pe.wait_ge(k_back, 16 * int(l) + 16)
                        pe.wait_ge(rb_ready, RBS["xa" + l] + 1)
                    scores("X" + l, a)

                project("qx" + l, xh, xl, x_ready("xa" + l),
                        hooks={**norm_hooks("xa" + l), (2, 1, 3): lambda: first_scores(0),
                               (3, 1, 3): lambda: first_scores(1)})
                pa = PH["attX" + l]
                soft_attention("X" + l, 4,
                               lambda a, b: [(b3(b)[:, j, :], slice(CW * a + P * j, CW * a + P * j + P)) for j in range(2)],
                               1, pa, "vx" + l)
                project("ox" + l, yh, yl, y_ready("X" + l, dve_evac, pa.base, 2))
                project("fu" + l, xh, xl, x_ready("ffn" + l), hooks=norm_hooks("ffn" + l))
                project("fg" + l, xh, xl)
                project("fd" + l, yh, yl, y_ready("ffn" + l, g_lo, GBASE["ffn" + l], 2))
            stats("fin")
            bcast("fin")

        @block.scalar
        def _(act):
            chain = Chain(act, chain_act)

            def hi(h_):
                if h_ >= 2 * NCHUNK:
                    return
                n, j = divmod(h_, 2)
                if h_ == 0:
                    act.wait_ge(first_half, 16)
                elif j == 0 or h_ == 1:
                    act.wait_ge(raw_full[n % RAW_SLOTS], 16 * (n // RAW_SLOTS + 1))
                if h_ >= 4:
                    act.wait_ge(w_used, h_ - 3)
                part = slice(j * P, j * P + P)
                act.activation(wh[:, n % 2, :, part], raw[:, n % RAW_SLOTS, :, part], ACT.Copy).then_inc(hi_ready, 1)

            def chunks(name, evacuate=None, split=0, last=None, hold=False):
                p = PH[name]
                for c in range(p.n):
                    n = p.n0 + c
                    for j in range(2):
                        if c == p.n - 1 and j == 1 and last is not None:
                            last()
                        if 2 * c + j >= split and not (hold and 2 * c + j == 2 * p.n - 1):
                            hi(2 * n + 3 + j)
                    if c % p.deep == p.deep - 1 and evacuate is not None:
                        if p.reader == "act":
                            act.wait_ge(w_used, 2 * n + 2)
                        evacuate(c // p.deep, b3(p.pair + c // p.deep % 2))

            def rope_raw(r, src, width):
                if r >= 2:
                    act.wait_ge(rope_done, r - 1)
                act.activation(wk(r % 2)[:, 0:width], src, ACT.Copy).then_inc(act_evac, 1)

            def flat(b):
                return b.rearrange("p a b -> p (a b)")

            def square(stat, c, src):
                i = 3 * STAT[stat]
                if i + (1 if c >= 2 else 0) > 0:
                    act.wait_ge(acc_done, i + (1 if c >= 2 else 0))
                act.activation(wk3(10 + c % 2), src, ACT.Square).then_inc(sq_ready, 1)

            def x_high(c, gain):
                if gain is None:
                    ins = act.activation(xh[:, 2 * c:2 * c + 2, :], h[:, 2 * c:2 * c + 2, :], ACT.Copy)
                else:
                    for m in (2 * c, 2 * c + 1):
                        ins = act.activation(xh[:, m, :], h[:, m, :], ACT.Copy, scale=vc(gain, m))
                ins.then_inc(x_hi, 1)

            def residual(name, stat, gain, split=0):
                p = PH[name]
                for c in range(p.n):
                    n = p.n0 + c
                    o = c // p.deep
                    for j in range(2):
                        if j == 1 and c % p.deep == 0 and o >= 1:
                            square(stat, o - 1, h[:, 2 * o - 2:2 * o, :])
                        if 2 * c + j >= split:
                            hi(2 * n + 3 + j)
                    if c % p.deep == p.deep - 1:
                        act.wait_ge(dve_evac, p.base + o + 1)
                        if gain is not None:
                            x_high(o, gain)
                square(stat, 3, h[:, 6:8, :])

            def spreading(name):
                def f(c, b):
                    if c == 0:
                        spread(name)
                return f

            def spread(name, dst=rb):
                act.wait_ge(bc_full, STAT[name] + 1)
                act.activation(dst[:, :], bank[5][:, 0:S], ACT.Copy).then_inc(rb_ready, 1)

            def exponentials(name, t):
                u = UBASE[name] + t
                if t >= 3:
                    act.wait_ge(t_full, u - 2)
                for q in range(2):
                    act.wait_ge(s_read, 2 * u + q + 1)
                    act.activation(wk3((2, 3, 6)[t % 3])[:, q, :], wk3(t % 2)[:, q, :], ACT.Exp,
                                   bias=nmax[:, u, q:q + 1], scale=-1.0,
                                   accum_out=esum[:, u, q:q + 1]).then_inc(e_done, 1)

            def soft_attention(name, heads, high, lag):
                u0, ob = UBASE[name], OBASE[name]
                for t in range(heads + lag):
                    if 2 <= t < heads + 2:
                        a = t - 2
                        u = u0 + a
                        act.wait_ge(t_full, u + 1)
                        if a >= 2:
                            act.wait_ge(o_full, ob + a - 1)
                        act.activation(wk(4 + a % 2), bank[6 + a % 2][:, :], ACT.Copy).then_inc(t_evac, 1)
                    if 1 <= t < heads:
                        exponentials(name, t)
                    high(t)
                hi(2 * PH["att" + name].n0 + 2)

            def gated_high(key, p, t, lag):
                if t >= lag and (t - lag) % 2 == 0 and (t - lag) // 2 < 8:
                    g = (t - lag) // 2
                    act.wait_ge(dve_evac, p.base + g + 1)
                    act.activation(yh[:, g, :], wk(10 + g % 2)[:, 0:S], ACT.Copy).then_inc(y_hi, 1)

            hi(0)
            act.wait_ge(x_in, 16)
            for c in range(4):
                x_high(c, None)
            hi(1)
            hi(2)
            chunks("qi", lambda c, b: rope_raw(c, flat(b), 2 * S))
            act.wait_ge(ki_full, 1)
            rope_raw(2, bank[PH["ki"].pair][:, 0:S], S)

            def qa(c, b):
                rope_raw(3 + c, flat(b), 2 * S)
                if c == 2:
                    act.wait_ge(wi_full, 1)
                    act.dma_start(m_raw.rearrange("p k s -> p (k s)"), memt).then_inc(mem_in, 16)

            chunks("qa", qa)
            for a in range(IH):
                act.wait_ge(is_full, a + 1)
                if a >= 2:
                    act.wait_ge(is_added, 2 * a - 2)
                act.activation(wk(6 + a % 2), bank[4 + a % 2][:, :], ACT.Relu, scale=HD ** -0.5).then_inc(rel_ready, 1)

            def ka(c, b):
                rope_raw(7 + c, flat(b), 2 * S)
                if c == 3:
                    act.wait_ge(mem_in, 16)
                    for q in range(2):
                        square("mem", q, m_raw[:, 2 * q:2 * q + 2, :])

            chunks("ka", ka)

            def v_copy(c, b):
                act.activation(v[:, :, CW * c:CW * c + CW], b, ACT.Copy).then_inc(act_evac, 1)

            def k_copy(c, b):
                act.activation(kt[:, 2 * c:2 * c + 2, :], b, ACT.Copy).then_inc(act_evac, 1)

            def gate(c, b):
                act.activation(gt[:, 2 * c:2 * c + 2, :], b, ACT.Silu).then_inc(act_evac, 1)

            def ga(c, b):
                gate(c, b)
                for m in (2 * c, 2 * c + 1):
                    ins = act.activation(yh[:, KT + m, :], m_raw[:, m, :], ACT.Copy, scale=vc("mem", m))
                ins.then_inc(m_hi, 1)
                if c < 2:
                    square("mem", 2 + c, m_raw[:, 4 + 2 * c:6 + 2 * c, :])

            def va(c, b):
                if c == 2:
                    spread("mem", rb_m)
                if c == 0:
                    act.wait_ge(m_lo, 4)
                v_copy(c, b)

            chunks("ga", ga)
            act.wait_ge(sq_ready, SQ["mem"] + 4)
            chunks("va", va, last=lambda: exponentials("A", 0), hold=True)
            soft_attention("A", NH, lambda t: gated_high("A", PH["attA"], t, 5), 5)
            act.wait_ge(m_lo, 4)
            act.dma_start(m_scratch[0], yh[:, KT:, :].bitcast(F32).rearrange("p k s -> p (k s)")).then_inc(m_saved, 16)
            act.dma_start(m_scratch[1], yl[:, KT:, :].bitcast(F32).rearrange("p k s -> p (k s)")).then_inc(m_saved, 16)
            chunks("oa")

            def layer_norm(l, filler, gain, stat):
                p = PH[filler]
                for c in range(p.n):
                    n = p.n0 + c
                    if c < 3:
                        hi(2 * n + 3)
                    hi(2 * n + 4)
                    if c == 0:
                        centred(l)
                    if c == 2:
                        shifted(l, range(0, 4), gain, stat)
                        hi(2 * n + 5)
                        shifted(l, range(4, 8), gain, stat)

            def centred(l):
                for c in range(4):
                    act.wait_ge(ln_c, 4 * int(l) + c + 1)
                    square("var" + l, c, h[:, 2 * c:2 * c + 2, :])

            def shifted(l, tiles, gain, stat):
                i = int(l)
                for m in tiles:
                    act.wait_ge(ln_g, 8 * i + m + 1)
                    act.activation(h[:, m, :], h[:, m, :], ACT.Identity, bias=vc("ln_b" + l, m)).then_inc(ln_h, 1)
                    if m % 2:
                        act.wait_ge(ln_h, 8 * i + m + 1)
                        x_high(m // 2, gain)
                        if stat is not None:
                            square(stat, m // 2, h[:, m - 1:m + 1, :])

            layer_norm("0", "kx0", None, None)

            def saving(l, evacuate):
                def f(c, b):
                    evacuate(c, b)
                    if c == 0:
                        act.wait_ge(dve_evac, PH["kx" + l].end)
                        act.dma_start(k_scratch[int(l)], kt[:, :, :].rearrange("p k s -> p (k s)")).then_inc(k_saved, 16)
                return f

            def q_scaled(c, b):
                act.activation(qz[0:HD, 4 * c:4 * c + 4:2, :], b[0:HD], ACT.Copy, scale=HD ** -0.5)
                act.activation(qz[HD:P, 4 * c + 1:4 * c + 4:2, :], b[HD:P], ACT.Copy, scale=HD ** -0.5).then_inc(act_evac, 1)

            chunks("gb", saving("0", gate))
            chunks("qb", q_scaled)
            act.wait_ge(k_saved, 16)
            chunks("kb", k_copy)

            ZW = S + P
            pb = PH["attB"]

            def z_soft(t):
                z = wk(t % 2)[:, 0:ZW]
                act.wait_ge(z_full, t + 1)
                if t >= 2:
                    act.wait_ge(z_sp, t - 1)
                act.activation(z, bank[4 + t % 2][:, 0:ZW], ACT.Abs).then_inc(z_abs, 1)
                act.wait_ge(z_abs, t + 1)
                chain(act.activation(z, z, ACT.Exp, scale=-1.0))
                act.activation(z, z, ACT.Ln, bias=1.0).then_inc(z_ln, 1)

            act.preload_act_table_set("natural_log_exp_and_others")

            def first_softs():
                for t in range(2):
                    z_soft(t)

            chunks("vb", v_copy, last=first_softs, hold=True)
            for t in range(NH + 5):
                if 2 <= t < NH:
                    z_soft(t)
                if 3 <= t < NH + 3:
                    a = t - 3
                    pr = wk(8 + a % 2)[:, 0:ZW]
                    act.wait_ge(z_arg, a + 1)
                    act.activation(pr, pr, ACT.Exp).then_inc(z_prob, 1)
                gated_high("B", pb, t, 6)
            hi(2 * pb.n0 + 2)

            act.wait_ge(o_full, OBASE["B"] + NH)
            act.dma_start(nabias.rearrange("p h t s -> p (h t s)"), rpb).then_inc(rpb_in, 16)
            act.dma_start(gflat[:, 0:1024], dft[:, 0:1024]).then_inc(dft_in, 16)
            act.dma_start(gflat[:, 1024:1280], dft[:, 1024:1280]).then_inc(dft_in, 16)
            chunks("ob")
            layer_norm("1", "kx1", "mix0", "mix0")

            def scaled_tokens(dst):
                def f(c, b):
                    act.wait_ge(st_pow, POW["mix0"] + 1)
                    for t in range(2):
                        ins = act.activation(dst[:, t, CW * c:CW * c + CW], b[:, t, :], ACT.Copy, scale=rt[:, t:t + 1])
                    ins.then_inc(act_evac, 1)
                return f

            def memory_values(c, b):
                for t in range(2):
                    ins = act.activation(v[:, t, CW * c:CW * c + CW], b[:, t, :], ACT.Copy, scale=rt_m[:, t:t + 1])
                ins.then_inc(act_evac, 1)

            chunks("zf", saving("1", scaled_tokens(u_tok)))
            spread("mix0")
            chunks("qn")
            chunks("kn")
            chunks("vn", scaled_tokens(v), hold=True)
            exponentials("N", 0)
            pf = PH["fourier"]
            for g in range(5):
                if g < 4:
                    act.wait_ge(f_full, g + 1)
                    if g >= 2:
                        act.wait_ge(o_full, OBASE["F"] + g - 1)
                    act.activation(wk(8 + g % 2), bank[6 + g % 2][:, :], ACT.Copy).then_inc(f_copied, 1)
                if g >= 1:
                    a = g - 1
                    act.wait_ge(o_full, OBASE["F"] + a + 1)
                    act.activation(yh[:, a, :], bank[pf.pair + a % 2][:, 0:S], ACT.Copy).then_inc(y_hi, 1)

            def plain_high(name, heads, tiles, first):
                p = PH["att" + name]

                def f(t):
                    if t >= 4:
                        a = t - 4
                        act.wait_ge(o_full, OBASE[name] + a + 1)
                        act.activation(yh[:, first + tiles * a:first + tiles * a + tiles, :],
                                       b3(p.pair + a % 2)[:, 0:tiles, :], ACT.Copy).then_inc(y_hi, 1)
                return f

            soft_attention("N", 4, plain_high("N", 4, 1, 4), 4)
            act.dma_start(kt[:, :, :].rearrange("p k s -> p (k s)"), k_scratch[0]).then_inc(k_back, 16)
            residual("oab", "xa0", "xa0")

            def products(key, name, l=None, meanwhile=None):
                p = PH[name]
                taps, tiles = ("fconv" + l, 16) if l else ("conv_c", 8)

                def centre(c):
                    cv, cp = wk3(3 + c % 2), cpad[c % 2]
                    if l:
                        act.wait_ge(dve_evac, p.base + c + 1)
                    else:
                        act.wait_ge(gate_in, c + 1)
                        if c >= 2:
                            act.wait_ge(pf_ready, CBASE[key] + c - 1)
                    for j in range(2):
                        m = 2 * c + j
                        if l:
                            ins = act.activation(cv[:, j, :], cp[:, j, 1:S + 1], ACT.Identity, scale=vc(taps, tiles + m),
                                                 bias=vc("fbias" + l, m))
                        else:
                            ins = act.activation(cv[:, j, :], cp[:, j, 1:S + 1], ACT.Copy, scale=vc(taps, tiles + m))
                    ins.then_inc(centre_ready, 1)

                def gelu(c):
                    if not l:
                        return
                    act.wait_ge(cv_ready, CBASE[key] + c + 1)
                    if c >= 2:
                        act.wait_ge(pf_ready, CBASE[key] + c - 1)
                    act.activation(wk(5 + c % 2), wk(3 + c % 2), ACT.Gelu).then_inc(ge_ready, 1)

                def high(c):
                    act.wait_ge(pf_ready, CBASE[key] + c + 1)
                    act.activation(yh[:, 2 * c:2 * c + 2, :], wk3(7 + c % 2), ACT.Copy).then_inc(y_hi, 1)

                for c in range(p.n + 1):
                    n = p.n0 + c
                    hi(2 * n + 3)
                    if c == p.n and not l:
                        hi(2 * n + 4)
                    if c >= 1:
                        centre(c - 1)
                    if c < p.n:
                        hi(2 * n + 4)
                    if c >= 1:
                        gelu(c - 1)
                    if c >= 2:
                        high(c - 2)
                    if c == p.n:
                        hi(2 * n + (4 if l else 5))
                if meanwhile is not None:
                    meanwhile()
                high(p.n - 1)

            for l in "01":
                if l == "1":
                    fd = PH["fd0"]
                    act.wait_ge(w_used, 2 * (fd.n0 + fd.n))
                    act.wait_ge(m_saved, 32)
                    for part, y_ in enumerate((yh, yl)):
                        act.dma_start(y_[:, KT:, :].bitcast(F32).rearrange("p k s -> p (k s)"),
                                      m_scratch[part]).then_inc(m_back, 16)
                    chunks("cb", spreading("mix1"))
                    chunks("cc")

                    def first_values():
                        pv = PH["vx1"]
                        act.wait_ge(w_used, 2 * pv.n0 + 2)
                        memory_values(0, b3(pv.pair))

                    products("conv", "cu", meanwhile=first_values)
                    act.wait_ge(gate_in, 4)
                    act.dma_start(kt[:, :, :].rearrange("p k s -> p (k s)"), k_scratch[1]).then_inc(k_back, 16)
                    chunks("vx1", lambda c, b: memory_values(c, b) if c else None, split=3)
                    residual("oc", "xa1", "xa1")
                else:
                    chunks("vx0", memory_values)
                chunks("qx" + l, spreading("xa" + l), hold=True)
                exponentials("X" + l, 0)
                soft_attention("X" + l, 4, plain_high("X" + l, 4, 2, 0), 4)
                residual("ox" + l, "ffn" + l, "ffn" + l)
                chunks("fu" + l, spreading("ffn" + l))
                products("ffn" + l, "fg" + l, l)
                if l == "0":
                    residual("fd0", "mix1", "mix1", split=2)
                else:
                    residual("fd1", "fin", None, split=2)

        @block.vector
        def _(dve):
            chain = Chain(dve, chain_dve)

            def both(*instructions):
                for ins in instructions:
                    chain.n += 1
                    ins.then_inc(chain_dve, 1)
                dve.wait_ge(chain_dve, chain.n)

            def lo(h_):
                if h_ >= 2 * NCHUNK:
                    return
                n, j = divmod(h_, 2)
                dve.wait_ge(hi_ready, h_ + 1)
                part = slice(j * P, j * P + P)
                dve.tensor_tensor(wl[:, n % 2, :, part], raw[:, n % RAW_SLOTS, :, part],
                                  wh[:, n % 2, :, part].bitcast(F32), ALU.subtract).then_inc(lo_ready, 1)

            def chunks(name, evacuate=None, between=None, split=0, middle=None, hold=False):
                p = PH[name]
                for c in range(p.n):
                    n = p.n0 + c
                    for j in range(2):
                        if j == 1 and middle is not None:
                            middle(c)
                        if 2 * c + j >= split and not (hold and 2 * c + j == 2 * p.n - 1):
                            lo(2 * n + 3 + j)
                    if c % p.deep == p.deep - 1 and evacuate is not None:
                        dve.wait_ge(w_used, 2 * n + 2)
                        evacuate(c // p.deep, b3(p.pair + c // p.deep % 2))
                    if between is not None:
                        between(c)

            def rotate(r, width):
                if r == 0:
                    dve.wait_ge(const_in, 32)
                dve.wait_ge(act_evac, r + 1)
                if r >= 2:
                    dve.wait_ge(rope_done, r - 1)
                n = width // S
                for q in range(4):
                    to, frm = slice(32 * q, 32 * q + 32), slice(32 * (q ^ 1), 32 * (q ^ 1) + 32)
                    sines = sinT[frm, :].unsqueeze(1).broadcast_to([32, n, S])
                    ins = dve.tensor_tensor(wk(4 + r % 2)[to, 0:width].rearrange("p (a b) -> p a b", a=n),
                                            wk(r % 2)[frm, 0:width].rearrange("p (a b) -> p a b", a=n),
                                            sines, ALU.mult)
                ins.then_inc(rope_rot, 1)

            def x_low(c, use, gain):
                dve.wait_ge(x_hi, XBASE[use] + c + 1)
                if gain is None:
                    dve.tensor_tensor(xl[:, 2 * c:2 * c + 2, :], h[:, 2 * c:2 * c + 2, :],
                                      xh[:, 2 * c:2 * c + 2, :].bitcast(F32), ALU.subtract).then_inc(x_lo, 1)
                    return
                for j in range(2):
                    m = 2 * c + j
                    ins = dve.scalar_tensor_tensor(xl[:, m, :], h[:, m, :], vc(gain, m), xh[:, m, :].bitcast(F32),
                                                   ALU.mult, ALU.subtract)
                ins.then_inc(x_lo, 1)

            def diagonal(name, src):
                for t in range(2):
                    dve.tensor_scalar(diag[:, t, :], ident, src[:, t:t + 1], None, ALU.mult).then_inc(st_diag, 1)

            def inverse_rms(name, eps):
                dve.wait_ge(st_full, STAT[name] + 1)
                dve.tensor_scalar(stat[:, :], bank[4][:, 0:2], 1.0 / D, eps, ALU.mult, ALU.add).then_inc(st_read, 1)
                dve.wait_ge(st_pow, POW[name] + 1)
                diagonal(name, rt_m if name == "mem" else rt)

            def residual(name, use, gain, alpha=None, split=0):
                p = PH[name]
                for c in range(p.n):
                    n = p.n0 + c
                    if c % p.deep == 0 and c and use is not None:
                        x_low(c // p.deep - 1, use, gain)
                    for j in range(2):
                        if 2 * c + j >= split:
                            lo(2 * n + 3 + j)
                    if c % p.deep == p.deep - 1:
                        o = c // p.deep
                        dve.wait_ge(w_used, 2 * n + 2)
                        hc, b = h[:, 2 * o:2 * o + 2, :], b3(p.pair + o % 2)
                        if alpha is None:
                            dve.tensor_tensor(hc, b, hc, ALU.add).then_inc(dve_evac, 1)
                        else:
                            hf = hc.rearrange("p a b -> p (a b)")
                            dve.scalar_tensor_tensor(hf, hf, alpha, bank[p.pair + o % 2][:, :], ALU.mult,
                                                     ALU.add).then_inc(dve_evac, 1)
                if use is not None:
                    x_low(3, use, gain)

            def logits(name, t, bias, scale):
                u = UBASE[name] + t
                dve.wait_ge(s_full, u + 1)
                if t >= 2:
                    dve.wait_ge(e_done, 2 * u - 2)
                for q in range(2):
                    dve.tensor_tensor_reduce(wk3(t % 2)[:, q, :], b3(4 + t % 2)[:, q, :], bias[:, q, :],
                                             -scale, 3.0e38, ALU.add, ALU.min,
                                             nmax[:, u, q:q + 1]).then_inc(s_read, 1)

            def normalise(name, t):
                u = UBASE[name] + t
                dve.wait_ge(e_done, 2 * u + 2)
                chain(dve.reciprocal(erec[:, u, :], esum[:, u, :]))
                pr = wk3((2, 3, 6)[t % 3])
                for q in range(2):
                    dve.tensor_scalar(pr[:, q, :], pr[:, q, :], erec[:, u, q:q + 1], None, ALU.mult).then_inc(p_ready, 1)

            def soft_attention(name, heads, bias, scale, extra, lag):
                for t in range(2, heads + lag):
                    if t < heads:
                        logits(name, t, bias(t), scale)
                    if t < heads + 1:
                        normalise(name, t - 1)
                    extra(t)
                lo(2 * PH["att" + name].n0 + 2)

            def gated(key, p, lag):
                def f(t):
                    if t >= lag and (t - lag) % 2 == 0 and (t - lag) // 2 < 8:
                        g = (t - lag) // 2
                        dve.wait_ge(o_full, OBASE[key] + 2 * g + 2)
                        if g >= 2:
                            dve.wait_ge(g_lo, GBASE[key] + g - 1)
                        dve.tensor_tensor(wk(10 + g % 2)[:, 0:S], bank[p.pair + g % 2][:, 0:S], gt[:, g, :],
                                          ALU.mult).then_inc(dve_evac, 1)
                return f

            def plain_low(name, tiles, first):
                p = PH["att" + name]

                def f(t):
                    if t >= 4:
                        a = t - 4
                        m = slice(first + tiles * a, first + tiles * a + tiles)
                        dve.wait_ge(y_hi, YBASE[name] + a + 1)
                        dve.tensor_tensor(yl[:, m, :], b3(p.pair + a % 2)[:, 0:tiles, :], yh[:, m, :].bitcast(F32),
                                          ALU.subtract).then_inc(dve_evac, 1)
                return f

            lo(0)
            for c in range(4):
                x_low(c, "first", None)
            lo(1)
            lo(2)
            chunks("qi", lambda c, b: rotate(c, 2 * S))
            rotate(2, S)

            def qa(c, b):
                rotate(3 + c, 2 * S)
                if c == 2:
                    dve.wait_ge(wi_full, 1)
                    dve.tensor_scalar(wi[:, :, :].rearrange("p a b -> p (a b)"), bank[4][:, 0:2 * IH], IH ** -0.5, None,
                                      ALU.mult).then_inc(wi_ready, 1)

            chunks("qa", qa)
            dve.wait_ge(wi_ready, 1)
            for a in range(IH):
                dve.wait_ge(rel_ready, a + 1)
                for t in range(2):
                    if a >= 1:
                        dve.wait_ge(is_added, 2 * a - 1 + t)
                    dve.scalar_tensor_tensor(score[:, t, :], wk3(6 + a % 2)[:, t, :], wi[:, t, a:a + 1],
                                             (score if a else adm)[:, t, :], ALU.mult, ALU.add).then_inc(is_added, 1)
            dve.wait_ge(is_added, 2 * IH)
            chunks("ka", lambda c, b: rotate(7 + c, 2 * S))

            def pick(c):
                both(*[dve.max(top8[:, t, :], score[:, t, :]) for t in range(2)])
                both(*[dve.match_replace(score[:, t, :], top8[:, t, :], score[:, t, :], TAKEN) for t in range(2)])

            assert TOPK == 8 * 8
            def memory_low(c):
                dve.wait_ge(m_hi, c + 1)
                for m in (2 * c, 2 * c + 1):
                    ins = dve.scalar_tensor_tensor(yl[:, KT + m, :], m_raw[:, m, :], vc("mem", m),
                                                   yh[:, KT + m, :].bitcast(F32), ALU.mult, ALU.subtract)
                ins.then_inc(m_lo, 1)

            def va(c):
                pick(4 + c)
                if c == 0:
                    inverse_rms("mem", RMS_EPS)
                if c == 3:
                    chain(dve.tensor_scalar(selneg, score, 0.5 * TAKEN, NEG, ALU.is_gt, ALU.mult))
                    logits("A", 0, selneg, HD ** -0.5)

            chunks("ga", middle=pick, between=memory_low)
            chunks("va", middle=va, hold=True)
            logits("A", 1, selneg, HD ** -0.5)
            normalise("A", 0)
            soft_attention("A", NH, lambda a: selneg, HD ** -0.5, gated("A", PH["attA"], 5), 5)

            def layer_norm(l, filler, use, gain):
                i = int(l)
                p = PH[filler]
                for c in range(p.n):
                    n = p.n0 + c
                    if c == 2:
                        inverse_rms("var" + l, LN_EPS)
                    if c < 3:
                        lo(2 * n + 3)
                    if c == 0:
                        dve.wait_ge(st_full, STAT["mean" + l] + 1)
                        chain(dve.tensor_scalar(stat[:, :], bank[4][:, 0:2], 1.0 / D, None, ALU.mult))
                        diagonal("mean" + l, stat)
                    if c == 2:
                        dve.wait_ge(bc_full, STAT["var" + l] + 1)
                        for m in range(KT):
                            dve.scalar_tensor_tensor(h[:, m, :], h[:, m, :], vc("ln_g" + l, m), bank[5][:, 0:S], ALU.mult,
                                                     ALU.mult).then_inc(ln_g, 1)
                        for q in range(2):
                            x_low(q, use, gain)
                    lo(2 * n + 4)
                    if c == 0:
                        dve.wait_ge(bc_full, STAT["mean" + l] + 1)
                        for q in range(4):
                            hq = h[:, 2 * q:2 * q + 2, :]
                            dve.tensor_tensor(hq, hq, bank[5][:, 0:S].unsqueeze(1).broadcast_to([P, 2, S]),
                                              ALU.subtract).then_inc(ln_c, 1)
                        dve.wait_ge(ln_c, 4 * i + 4)
                    if c == 2:
                        lo(2 * n + 5)
                        for q in range(2, 4):
                            x_low(q, use, gain)
                    dve.wait_ge(w_used, 2 * n + 2)
                    dve.tensor_tensor(kt[:, 2 * c:2 * c + 2, :], b3(p.pair + c % 2),
                                      rb_m[:, :].unsqueeze(1).broadcast_to([P, 2, S]), ALU.mult).then_inc(dve_evac, 1)

            residual("oa", None, None, ALPHA)
            layer_norm("0", "kx0", "B", None)
            chunks("gb")
            chunks("qb")
            chunks("kb")

            ZW = S + P
            zgate = gated("B", PH["attB"], 5)

            def z_step(t):
                b = bank[4 + t % 2][:, 0:ZW]
                dve.wait_ge(z_ln, t + 1)
                if t >= 2:
                    dve.wait_ge(z_masked, t - 1)
                dve.scalar_tensor_tensor(wk(2 + t % 2)[:, 0:ZW], b, 0.0, wk(t % 2)[:, 0:ZW], ALU.max,
                                         ALU.add).then_inc(z_sp, 1)
                if t >= 2:
                    dve.wait_ge(z_arg, t - 1)
                dve.tensor_tensor(wk(6 + t % 2)[:, 0:ZW], b, c_("beforeneg"), ALU.add).then_inc(z_neg, 1)

            chunks("vb", middle=lambda c: z_step(0) if c == 3 else None, hold=True)
            for t in range(1, NH + 5):
                if 2 <= t < NH + 2:
                    a = t - 2
                    dve.wait_ge(c_full, a + 1)
                    if a >= 2:
                        dve.wait_ge(o_full, OBASE["B"] + a - 1)
                    dve.wait_ge(z_neg, a + 1)
                    dve.tensor_tensor(wk(8 + a % 2)[:, 0:ZW], wk(6 + a % 2)[:, 0:ZW], bank[6 + a % 2][:, 0:ZW],
                                      ALU.subtract).then_inc(z_arg, 1)
                if t < NH:
                    z_step(t)
                zgate(t)
            lo(2 * PH["attB"].n0 + 2)
            residual("ob", None, None, ALPHA)
            layer_norm("1", "kx1", "mix0", "mix0")

            def bias(c):
                dve.wait_ge(rpb_in, 16)
                for t in range(2):
                    dve.scalar_tensor_tensor(nabias[:, c, t, :], nabias[:, c, t, :], 1.0 / NA_SCALE, c_("colneg"),
                                             ALU.mult, ALU.add).then_inc(bias_ready, 1)

            def times_rb(dst, name=None):
                def f(c, b):
                    if c == 0 and name is not None:
                        dve.wait_ge(rb_ready, RBS[name] + 1)
                    dve.tensor_tensor(dst[:, 2 * c:2 * c + 2, :], b, rb[:, :].unsqueeze(1).broadcast_to([P, 2, S]),
                                      ALU.mult).then_inc(dve_evac, 1)
                return f

            lo(2 * PH["zf"].n0 + 3)
            inverse_rms("mix0", RMS_EPS)
            chunks("zf", between=bias, split=1)
            chunks("qn", times_rb(qz, "mix0"), between=lambda c: bias(2 + c))
            dve.wait_ge(k_saved, 32)
            chunks("kn", times_rb(kt))
            chunks("vn", hold=True)
            dve.wait_ge(bias_ready, 8)
            for a in range(2):
                logits("N", a, nabias[:, a, :, :], NA_SCALE)
            normalise("N", 0)
            pf = PH["fourier"]
            for g in range(4):
                dve.wait_ge(y_hi, YBASE["F"] + g + 1)
                dve.tensor_tensor(yl[:, g, :], bank[pf.pair + g % 2][:, 0:S], yh[:, g, :].bitcast(F32),
                                  ALU.subtract).then_inc(dve_evac, 1)
            soft_attention("N", 4, lambda a: nabias[:, a, :, :], NA_SCALE, plain_low("N", 1, 4), 4)
            residual("oab", "xa0", "xa0")

            def convolution(key, c, taps, tiles):
                cv, cp = wk3(3 + c % 2), cpad[c % 2]
                dve.wait_ge(centre_ready, CBASE[key] + c + 1)
                both(*[dve.scalar_tensor_tensor(cv[:, j, :], cp[:, j, 0:S], vc(taps, 2 * c + j), cv[:, j, :], ALU.mult,
                                                ALU.add) for j in range(2)])
                for j in range(2):
                    ins = dve.scalar_tensor_tensor(cv[:, j, :], cp[:, j, 2:S + 2], vc(taps, 2 * tiles + 2 * c + j),
                                                   cv[:, j, :], ALU.mult, ALU.add)
                ins.then_inc(cv_ready, 1)

            def convolved(name, key, evacuate, taps, tiles):
                p = PH[name]
                for c in range(p.n):
                    n = p.n0 + c
                    lo(2 * n + 3)
                    if c >= 1:
                        convolution(key, c - 1, taps, tiles)
                    lo(2 * n + 4)
                    dve.wait_ge(w_used, 2 * n + 2)
                    evacuate(c, b3(p.pair + c % 2))
                if key == "conv":
                    lo(2 * (p.n0 + p.n) + 3)
                    lo(2 * (p.n0 + p.n) + 4)
                    convolution(key, p.n - 1, taps, tiles)
                    lo(2 * (p.n0 + p.n) + 5)
                else:
                    convolution(key, p.n - 1, taps, tiles)
                    lo(2 * (p.n0 + p.n) + 3)
                    lo(2 * (p.n0 + p.n) + 4)

            for l in "01":
                if l == "1":
                    lo(2 * PH["cb"].n0 + 3)
                    inverse_rms("mix1", RMS_EPS)
                    chunks("cb", times_rb(qz, "mix1"), split=1)
                    chunks("cc", times_rb(kt))

                    def scaled(c, b):
                        if c >= 2:
                            dve.wait_ge(gate_in, c - 1)
                        dve.tensor_tensor(wk3(5 + c % 2), b, rb[:, :].unsqueeze(1).broadcast_to([P, 2, S]),
                                          ALU.mult).then_inc(dve_evac, 1)

                    convolved("cu", "conv", scaled, "conv_c", 8)
                    chunks("vx1", split=3)
                    residual("oc", "xa1", "xa1")
                else:
                    chunks("vx0")
                lo(2 * PH["qx" + l].n0 + 3)
                inverse_rms("xa" + l, RMS_EPS)
                dve.wait_ge(zero_ready, 1)

                def queries(c, b, l=l):
                    times_rb(qz, "xa" + l)(c, b)
                    if c == 2:
                        logits("X" + l, 0, adm, XA_SCALE)

                def second_logits(c, l=l):
                    if c == 3:
                        normalise("X" + l, 0)
                        logits("X" + l, 1, adm, XA_SCALE)

                chunks("qx" + l, queries, middle=second_logits, split=1, hold=True)
                soft_attention("X" + l, 4, lambda a: adm, XA_SCALE, plain_low("X" + l, 2, 0), 4)
                residual("ox" + l, "ffn" + l, "ffn" + l)
                lo(2 * PH["fu" + l].n0 + 3)
                inverse_rms("ffn" + l, RMS_EPS)
                chunks("fu" + l, times_rb(qz, "ffn" + l), split=1)
                dve.wait_ge(padded, 4 + 4 * int(l))

                def gate_chunk(c, b):
                    dve.tensor_tensor(cpad[c % 2][:, :, 1:S + 1], b, rb[:, :].unsqueeze(1).broadcast_to([P, 2, S]),
                                      ALU.mult).then_inc(dve_evac, 1)

                convolved("fg" + l, "ffn" + l, gate_chunk, "fconv" + l, 16)
                if l == "0":
                    residual("fd0", "mix1", "mix1", split=2)
                else:
                    residual("fd1", None, None, split=2)
            inverse_rms("fin", RMS_EPS)
            dve.wait_ge(bc_full, STAT["fin"] + 1)
            for m in range(KT):
                dve.scalar_tensor_tensor(gt[:, m, :], h[:, m, :], vc("fin", m), bank[5][:, 0:S], ALU.mult,
                                         ALU.mult).then_inc(fin_ready, 1)

        @block.gpsimd
        def _(pool):
            chain = Chain(pool, chain_pool)
            pool.memset(ones[:, :], 1.0).then_inc(filled, 1)
            pool.memset(half[:, :], -0.5).then_inc(filled, 1)
            pool.memset(qiz[:, :, :], 0.0).then_inc(filled, 1)
            pool.memset(qz[0:HD, 1:NH:2, :], 0.0).then_inc(filled, 1)
            pool.wait_ge(filled, 4)
            pool.memset(qz[HD:P, 0:NH:2, :], 0.0).then_inc(filled, 1)
            pool.wait_ge(filled, 5)

            def rope(r, width, targets):
                n = width // S
                t1 = wk(2 + r % 2)[:, 0:width].rearrange("p (a b) -> p a b", a=n)
                t2 = wk(4 + r % 2)[:, 0:width].rearrange("p (a b) -> p a b", a=n)
                pool.wait_ge(act_evac, r + 1)
                pool.tensor_tensor(t1, wk(r % 2)[:, 0:width].rearrange("p (a b) -> p a b", a=n),
                                   cosT.unsqueeze(1).broadcast_to([P, n, S]), ALU.mult).then_inc(rope_cos, 1)
                pool.wait_ge(rope_cos, r + 1)
                pool.wait_ge(rope_rot, r + 1)
                for dst, rows in targets:
                    if rows.start > 0:
                        chain(ins)
                    ins = pool.tensor_tensor(dst, t1[rows], t2[rows], ALU.add)
                ins.then_inc(rope_done, 1)
                pool.wait_ge(rope_done, r + 1)

            def heads(dst, c):
                return [(dst[0:HD, 4 * c:4 * c + 4:2, :], slice(0, HD)), (dst[HD:P, 4 * c + 1:4 * c + 4:2, :], slice(HD, P))]

            def sum_up(name, source):
                first = source(0)
                for c in range(1, 3 if name == "fin" else 4):
                    if c >= 2:
                        pool.wait_ge(acc_done, 3 * STAT[name] + c - 1)
                    a = first if c == 1 else acc[:, :, :]
                    pool.tensor_tensor(acc[:, :, :], a, source(c), ALU.add).then_inc(acc_done, 1)

            def squares(name):
                def source(c):
                    pool.wait_ge(sq_ready, SQ[name] + c + 1)
                    return wk3(10 + c % 2)
                return source

            def stream(name):
                def source(c):
                    pool.wait_ge(dve_evac, PH[name].base + c + 1)
                    return h[:, 2 * c:2 * c + 2, :]
                return source

            def power(name):
                pool.wait_ge(st_read, POW[name] + 1)
                dst = rt_m if name == "mem" else rt
                pool.tensor_tensor(dst[:, :], stat[:, :], half[:, :], ALU.pow).then_inc(st_pow, 1)

            def norm(name):
                sum_up(name, squares(name))
                power(name)

            def gated_low(key, g):
                pool.wait_ge(y_hi, YBASE[key] + g + 1)
                pool.tensor_tensor(yl[:, g, :], wk(10 + g % 2)[:, 0:S], yh[:, g, :].bitcast(F32),
                                   ALU.subtract).then_inc(g_lo, 1)

            def product(key, c, a, b):
                if c >= 2:
                    pool.wait_ge(g_lo, GBASE[key] + c - 1)
                pool.tensor_tensor(wk3(7 + c % 2), a, b, ALU.mult).then_inc(pf_ready, 1)

            def product_low(key, c):
                pool.wait_ge(y_hi, YBASE[key] + c + 1)
                pool.tensor_tensor(yl[:, 2 * c:2 * c + 2, :], wk3(7 + c % 2), yh[:, 2 * c:2 * c + 2, :].bitcast(F32),
                                   ALU.subtract).then_inc(g_lo, 1)

            def ffn_products(key):
                for c in range(8):
                    pool.wait_ge(ge_ready, GEBASE[key] + c + 1)
                    product(key, c, wk3(5 + c % 2), qz[:, 2 * c:2 * c + 2, :])
                    if c >= 1:
                        product_low(key, c - 1)
                product_low(key, 7)

            def pads(name):
                pool.wait_ge(o_full, OBASE[name] + 4)
                pool.wait_ge(e_done, 2 * UBASE[name] + 8)
                for b in cpad:
                    for col in (0, S + 1):
                        pool.memset(b[:, :, col:col + 1], 0.0).then_inc(padded, 1)

            pool.wait_ge(const_in, 32)
            for c in range(2):
                rope(c, 2 * S, heads(qiz, c))
            rope(2, S, [(ki.unsqueeze(1), slice(0, P))])
            for c in range(4):
                rope(3 + c, 2 * S, heads(qz, c))
            for c in range(4):
                rope(7 + c, 2 * S, [(kt[:, 2 * c:2 * c + 2, :], slice(0, P))])
            norm("mem")
            for g in range(8):
                gated_low("A", g)
            sum_up("mean0", stream("oa"))
            norm("var0")
            pool.memset(adm, 0.0).then_inc(zero_ready, 1)
            for t in range(NH + 6):
                if t < NH:
                    pool.wait_ge(z_sp, t + 1)
                    if t >= 2:
                        pool.wait_ge(c_full, t - 1)
                    ZW = S + P
                    pool.tensor_tensor(wk(4 + t % 2)[:, 0:ZW], wk(2 + t % 2)[:, 0:ZW], c_("before"),
                                       ALU.mult).then_inc(z_masked, 1)
                if t >= 6 and t % 2 == 0:
                    gated_low("B", (t - 6) // 2)
            sum_up("mean1", stream("ob"))
            norm("var1")
            norm("mix0")
            norm("xa0")
            pads("X0")
            norm("ffn0")
            ffn_products("ffn0")
            norm("mix1")
            for c in range(5):
                if c < 4:
                    pool.wait_ge(dve_evac, PH["cu"].base + c + 1)
                    if c >= 2:
                        pool.wait_ge(cv_ready, CBASE["conv"] + c - 1)
                    pool.tensor_tensor(cpad[c % 2][:, :, 1:S + 1], wk3(5 + c % 2), kt[:, 2 * c:2 * c + 2, :],
                                       ALU.mult).then_inc(gate_in, 1)
                if c >= 1:
                    a = c - 1
                    pool.wait_ge(cv_ready, CBASE["conv"] + a + 1)
                    product("conv", a, wk3(3 + a % 2), qz[:, 2 * a:2 * a + 2, :])
                if c >= 2:
                    product_low("conv", c - 2)
            product_low("conv", 3)
            norm("xa1")
            pads("X1")
            norm("ffn1")
            ffn_products("ffn1")
            norm("fin")


def tables():
    p = np.arange(P)
    cst = np.zeros((P, NCST), np.float32)

    def put(name, a):
        cst[:, CST[name][0]:CST[name][1]] = a.reshape(P, -1)

    put("ident", np.eye(P))
    inv = (1.0 / (np.float32(10000.0) ** (np.arange(0, HD, 2, dtype=np.float32) / np.float32(HD)))).astype(np.float32)
    ang = (np.arange(S, dtype=np.float32)[None, :] * inv[p % 32][:, None]).astype(np.float32)
    put("cos", np.cos(ang))
    put("sin", np.where((p // 32 % 2 == 0)[:, None], 1, -1) * np.sin(ang))
    s = np.arange(S)
    q = np.arange(2)[None, :] * P + p[:, None]
    put("adm", np.where(s[None, None, :] // CHUNK <= q[:, :, None] // CHUNK, 0.0, NEG))
    before = np.concatenate([p[:, None] < s[None, :], p[:, None] < p[None, :]], 1)
    put("before", before.astype(np.float32))
    put("beforeneg", np.where(before, 0.0, NEG))
    put("tri", (p[:, None] >= p[None, :]).astype(np.float32))
    start = np.clip(p % GW - 8, 0, GW - 16)[:, None]
    col = (s % GW)[None, :]
    put("colneg", np.where((col >= start) & (col < start + 16), 0.0, NEG))
    dft = np.zeros((P, 1280), np.float32)
    tok = (np.arange(2)[None, :, None] * P + p[:, None, None]) * s[None, None, :] % S
    a = 2 * np.pi * tok / S
    dft[:, 0:1024] = np.concatenate([np.cos(a), np.sin(a)], 2).reshape(P, -1)
    a = 2 * np.pi * (p[:, None] * p[None, :] % P) / P
    scale = 1.0 / math.sqrt(S * P)
    dft[:, 1024:1152] = np.cos(a) * scale
    dft[:, 1152:1280] = -np.sin(a) * scale
    return cst, dft


def neighbourhood_bias(rpb):
    s = np.arange(S)
    q = np.arange(2)[None, :] * P + np.arange(P)[:, None]
    dr = s[None, None, :] // GW - q[:, :, None] // GW + 7
    dc = np.clip(s[None, None, :] % GW - q[:, :, None] % GW + 15, 0, 30)
    return np.ascontiguousarray(rpb[:, dr, dc].transpose(1, 0, 2, 3)).reshape(P, -1)


def kernel(**inputs):
    import concourse.bacc as bacc
    from concourse.bass_utils import run_bass_kernel_spmd as run

    x = {k: np.asarray(a) for k, a in inputs.items()}

    def tiled(a):
        return np.ascontiguousarray(a.reshape(-1, P, a.shape[-1]).transpose(1, 0, 2))

    def cols(a, lo, hi):
        return [tiled(a[r:r + D, c:c + CW]) for c in range(lo, hi, CW) for r in range(0, a.shape[0], D)]

    wa, wb = x["w_in_a"][0], x["w_in_b"][0]
    IQ = 4 * D
    kv = x["xa_wkv_2"]
    chunks = cols(wa, IQ, IQ + 512) + cols(wa, 0, 2 * D) + cols(wa, 3 * D, 4 * D) + cols(wa, 2 * D, 3 * D)
    chunks += cols(x["w_out_a"][0], 0, D) + cols(kv[0], 0, D)
    chunks += cols(wb, 3 * D, 4 * D) + cols(wb, 0, 3 * D) + cols(x["w_out_b"][0], 0, D) + cols(kv[1], 0, D)
    chunks += cols(x["w_in_ab_2"][0], 0, 2048) + cols(x["w_out_ab_2"][0], 0, D)
    for l in range(2):
        if l == 1:
            chunks += cols(x["w_in_c_2"][0], 0, 3 * D)
        chunks += cols(kv[l], D, 2 * D)
        if l == 1:
            chunks += cols(x["w_out_c_2"][0], 0, D)
        chunks += cols(x["xa_wq_2"][l], 0, D) + cols(x["xa_wo_2"][l], 0, D)
        chunks += cols(x["ffn_w_up_2"][l], 0, 4 * D) + cols(x["ffn_w_down_2"][l], 0, D)
    w = np.stack(chunks)
    assert w.shape == (NCHUNK, P, KT, CW)
    wki = tiled(np.concatenate([wa[:, IQ + 520:IQ + 584]] * 2, 1))
    wwi = tiled(wa[:, IQ + 512:IQ + 520])

    vecs = np.zeros((P, NVEC), np.float32)

    def put(name, a):
        a = np.ascontiguousarray(a).reshape(-1, P).T
        vecs[:, VEC[name]:VEC[name] + a.shape[1]] = a

    for l in range(2):
        put(f"ln_g{l}", x["ln_g"][l])
        put(f"ln_b{l}", x["ln_b"][l])
        put(f"mix{l}", x["mix_norm_g_2"][l])
        put(f"xa{l}", x["xa_norm_g_2"][l])
        put(f"ffn{l}", x["ffn_norm_g_2"][l])
        put(f"fconv{l}", x["ffn_conv_w_2"][l])
        put(f"fbias{l}", x["ffn_conv_b_2"][l])
    put("mem", x["mem_norm_g_2"])
    put("fin", x["final_norm_g_2"])
    put("conv_c", x["conv_c_2"][0])
    cst, dft = tables()

    nc = bacc.Bacc("TRN2", target_bir_lowering=False, num_devices=1)
    arrays = {
        "w": w, "xt": tiled(x["x"][0].T), "memt": tiled(x["mem_2"][0].T).reshape(P, -1), "vecs": vecs, "cst": cst,
        "wki": wki, "wwi": wwi, "dft": dft, "rpb": neighbourhood_bias(x["rpb_2"][0]),
    }
    args = [nc.dram_tensor(k, a.shape, F32, kind="ExternalInput").ap() for k, a in arrays.items()]
    args.append(nc.dram_tensor("y", (P, KT, S), F32, kind="ExternalOutput").ap())
    build(nc, *args)
    r = run(nc, [arrays], core_ids=[0])
    y = r.results[0]["y"]
    return np.ascontiguousarray(y.transpose(2, 1, 0)).reshape(1, S, D)
```
